# Optimizing a Trainium2 kernel written in Bass

```python
import math
import jax
import jax.numpy as jnp
from jax import lax
import numpy as np

D_MODEL = 1024
BATCH = 1
SEQ = 256
DEPTH = 2

HEAD_DIM = 64
GRID_W = 64
Q_BLOCK = 128
EPS = 1e-6
NEG_INF = -1e30
ROPE_THETA = 10000.0

A_HEADS = 4
A_KV_HEADS = 2
A_HALF_WINDOW = 128
B_PATTERNS = ((128, 1), (512, 4), (2048, 16))
B_GROUPS = 3
B_HEADS = 4
C_HEADS = 4
C_Q_RANK = 256
C_KV_RANK = 128
C_NOPE = 64
C_ROPE = 32
C_QK_DIM = C_NOPE + C_ROPE
C_V = 64
D_HEADS = 4
D_KV_HEADS = 2

N_BRANCHES = 4
BRANCH_WIDTH = 4 * HEAD_DIM

REL_BUCKETS = 32
REL_MAX_DIST = 1024
REL_HEADS = A_HEADS + B_GROUPS * B_HEADS

PEER_HEADS = 8
PEER_N_KEYS = 128
PEER_N_EXPERTS = PEER_N_KEYS * PEER_N_KEYS
PEER_KEY_DIM = 128
PEER_TOPK = 16
PEER_TOKEN_BLOCK = 128

IN_SPLITS = (
    A_HEADS * HEAD_DIM, A_KV_HEADS * HEAD_DIM, A_KV_HEADS * HEAD_DIM,
    B_GROUPS * B_HEADS * HEAD_DIM, B_GROUPS * B_HEADS * HEAD_DIM, B_GROUPS * B_HEADS * HEAD_DIM,
    C_Q_RANK, C_KV_RANK, C_ROPE,
    D_HEADS * HEAD_DIM, D_KV_HEADS * HEAD_DIM, D_KV_HEADS * HEAD_DIM,
    N_BRANCHES * D_MODEL,
)
IN_WIDTH = sum(IN_SPLITS)

kernel_name = 'hybrid_gated_four_mixer_peer_encoder'

def rms_norm(x, gain):
    x32 = x.astype(jnp.float32)
    y = x32 * lax.rsqrt(jnp.mean(x32 * x32, axis=-1, keepdims=True) + EPS)
    return (y * gain.astype(jnp.float32)).astype(x.dtype)

def rope(x, pos):
    half = x.shape[-1] // 2
    freqs = ROPE_THETA ** (-jnp.arange(half, dtype=jnp.float32) / half)
    ang = pos.astype(jnp.float32)[:, None] * freqs[None, :]
    cos = jnp.cos(ang)[:, None, :]
    sin = jnp.sin(ang)[:, None, :]
    x32 = x.astype(jnp.float32)
    x1, x2 = x32[..., :half], x32[..., half:]
    return jnp.concatenate([x1 * cos - x2 * sin, x1 * sin + x2 * cos], axis=-1).astype(x.dtype)

def axial_rope(x, row, col):
    half = x.shape[-1] // 2
    return jnp.concatenate([rope(x[..., :half], row), rope(x[..., half:], col)], axis=-1)

def rel_bucket(rel):
    nb = REL_BUCKETS // 2
    max_exact = nb // 2
    ret = jnp.where(rel > 0, nb, 0)
    n = jnp.abs(rel)
    nf = jnp.maximum(n, 1).astype(jnp.float32)
    large = max_exact + (jnp.log(nf / max_exact) / math.log(REL_MAX_DIST / max_exact)
                         * (nb - max_exact)).astype(jnp.int32)
    large = jnp.minimum(large, nb - 1)
    return ret + jnp.where(n < max_exact, n, large)

def banded_attention(q, k, v, half_w, dilation, rel_table, sink):
    f32 = jnp.float32
    N, L, H, Dh = q.shape
    Hk = k.shape[2]
    G = H // Hk
    blk = min(Q_BLOCK, L)
    nb = -(-L // blk)
    Lp = nb * blk
    span = blk + 2 * half_w
    qp = jnp.pad(q.astype(f32), ((0, 0), (0, Lp - L), (0, 0), (0, 0)))
    kv_pad = ((0, 0), (half_w, Lp - L + half_w), (0, 0), (0, 0))
    kp = jnp.pad(k.astype(f32), kv_pad)
    vp = jnp.pad(v.astype(f32), kv_pad)
    kidx = jnp.arange(nb)[:, None] * blk + jnp.arange(span)[None, :]
    kb = kp[:, kidx]
    vb = vp[:, kidx]
    qb = qp.reshape(N, nb, blk, Hk, G, Dh)
    s = jnp.einsum('nbqkgd,nbskd->nbkgqs', qb, kb) * (Dh ** -0.5)
    rel = jnp.arange(span)[None, :] - half_w - jnp.arange(blk)[:, None]
    bias = rel_table.astype(f32)[rel_bucket(rel * dilation)]
    bias = bias.transpose(2, 0, 1).reshape(Hk, G, blk, span)
    kpos = kidx - half_w
    valid = (jnp.abs(rel) <= half_w)[None] & ((kpos >= 0) & (kpos < L))[:, None, :]
    s = jnp.where(valid[None, :, None, None], s + bias, NEG_INF)
    m = jnp.max(s, axis=-1, keepdims=True)
    if sink is not None:
        sk = sink.astype(f32).reshape(Hk, G, 1, 1)
        m = jnp.maximum(m, sk)
    p = jnp.exp(s - m)
    denom = jnp.sum(p, axis=-1, keepdims=True)
    if sink is not None:
        denom = denom + jnp.exp(sk - m)
    out = jnp.einsum('nbkgqs,nbskd->nbqkgd', p / denom, vb).reshape(N, Lp, H, Dh)[:, :L]
    lse = (m + jnp.log(denom))[..., 0].transpose(0, 1, 4, 2, 3).reshape(N, Lp, H)[:, :L]
    return out.astype(v.dtype), lse

def dense_attention(q, k, v):
    f32 = jnp.float32
    Bn, S, H, Dq = q.shape
    Hk, Dv = k.shape[2], v.shape[3]
    G = H // Hk
    nb = S // Q_BLOCK
    qb = q.astype(f32).reshape(Bn, nb, Q_BLOCK, Hk, G, Dq).swapaxes(0, 1)
    k32, v32 = k.astype(f32), v.astype(f32)
    scale = Dq ** -0.5

    def block(qblk):
        s = jnp.einsum('bqkgd,bskd->bkgqs', qblk, k32) * scale
        p = jax.nn.softmax(s, axis=-1)
        return jnp.einsum('bkgqs,bskd->bqkgd', p, v32)

    out = lax.map(block, qb)
    return out.swapaxes(0, 1).reshape(Bn, S, H, Dv).astype(v.dtype)

def to_strided(t, dil):
    Bn, S = t.shape[:2]
    return t.reshape(Bn, S // dil, dil, *t.shape[2:]).swapaxes(1, 2).reshape(Bn * dil, S // dil, *t.shape[2:])

def from_strided(t, dil, Bn):
    L = t.shape[1]
    return t.reshape(Bn, dil, L, *t.shape[2:]).swapaxes(1, 2).reshape(Bn, dil * L, *t.shape[2:])

def mixer_a(q, k, v, q_gain, k_gain, rel_table, sink):
    q = rms_norm(q, q_gain)
    k = rms_norm(k, k_gain)
    out, _ = banded_attention(q, k, v, A_HALF_WINDOW, 1, rel_table, sink)
    return out

def mixer_b(q, k, v, q_gain, k_gain, rel_table):
    Bn = q.shape[0]
    outs, lses = [], []
    for g, (window, dil) in enumerate(B_PATTERNS):
        half = window // (2 * dil)
        qg = rms_norm(q[:, :, g], q_gain[g])
        kg = rms_norm(k[:, :, g], k_gain[g])
        o, lse = banded_attention(to_strided(qg, dil), to_strided(kg, dil), to_strided(v[:, :, g], dil),
                                  half, dil, rel_table[:, g * B_HEADS:(g + 1) * B_HEADS], None)
        outs.append(from_strided(o, dil, Bn).astype(jnp.float32))
        lses.append(from_strided(lse, dil, Bn))
    w = jax.nn.softmax(jnp.stack(lses, axis=0), axis=0)
    return jnp.einsum('gbsh,gbshd->bshd', w, jnp.stack(outs, axis=0)).astype(v.dtype)

def mixer_c(cq, ckv, kpe, cq_lat_gain, ckv_lat_gain, w_uq, w_ukv, q_gain, k_gain, pos):
    Bn, S = cq.shape[:2]
    q = (rms_norm(cq, cq_lat_gain) @ w_uq).reshape(Bn, S, C_HEADS, C_QK_DIM)
    kv = (rms_norm(ckv, ckv_lat_gain) @ w_ukv).reshape(Bn, S, C_HEADS, C_NOPE + C_V)
    k_nope, v = kv[..., :C_NOPE], kv[..., C_NOPE:]
    q_nope = rms_norm(q[..., :C_NOPE], q_gain[:C_NOPE])
    q_pe = rope(rms_norm(q[..., C_NOPE:], q_gain[C_NOPE:]), pos)
    k_nope = rms_norm(k_nope, k_gain[:C_NOPE])
    k_pe = rope(rms_norm(kpe[:, :, None, :], k_gain[C_NOPE:]), pos)
    qf = jnp.concatenate([q_nope, q_pe], axis=-1)
    kf = jnp.concatenate([k_nope, jnp.broadcast_to(k_pe, (Bn, S, C_HEADS, C_ROPE))], axis=-1)
    return dense_attention(qf, kf, v)

def mixer_d(q, k, v, q_gain, k_gain, row, col):
    q = axial_rope(rms_norm(q, q_gain), row, col)
    k = axial_rope(rms_norm(k, k_gain), row, col)
    return dense_attention(q, k, v)

def peer_ffn(x, w_q, sub_keys, w_u, w_v):
    Bn, S, D = x.shape
    T = Bn * S
    xt = x.reshape(T, D)
    half = PEER_KEY_DIM // 2
    kk = PEER_TOPK * PEER_TOPK
    q = (xt @ w_q).reshape(T, PEER_HEADS, 2, half).astype(jnp.float32)
    scores = jnp.einsum('thcd,hcnd->thcn', q, sub_keys.astype(jnp.float32))
    s_half, i_half = lax.top_k(scores, PEER_TOPK)
    cand_s = (s_half[:, :, 0, :, None] + s_half[:, :, 1, None, :]).reshape(T, PEER_HEADS, kk)
    cand_i = (i_half[:, :, 0, :, None] * PEER_N_KEYS + i_half[:, :, 1, None, :]).reshape(T, PEER_HEADS, kk)
    top_s, top_pos = lax.top_k(cand_s, PEER_TOPK)
    idx = jnp.take_along_axis(cand_i, top_pos, axis=-1)
    gate = jax.nn.softmax(top_s, axis=-1)
    nb = T // PEER_TOKEN_BLOCK
    E = PEER_HEADS * PEER_TOPK

    def block(args):
        xb, ib, gb = args
        act = jax.nn.gelu(jnp.einsum('td,ted->te', xb, w_u[ib]).astype(jnp.float32), approximate=False)
        return jnp.einsum('te,ted->td', (act * gb).astype(xb.dtype), w_v[ib])

    out = lax.map(block, (xt.reshape(nb, PEER_TOKEN_BLOCK, D),
                          idx.reshape(nb, PEER_TOKEN_BLOCK, E),
                          gate.reshape(nb, PEER_TOKEN_BLOCK, E)))
    return out.reshape(Bn, S, D)

def setup_inputs(seed: int = 0) -> dict:
    key = jax.random.key(seed)
    ks = jax.random.split(key, 26)
    f32 = jnp.float32

    def nrm(k, shape, scale):
        return jax.random.normal(k, shape, f32) * scale

    def gain(k, shape):
        return 1.0 + 0.02 * jax.random.normal(k, shape, f32)

    L = DEPTH
    return {
        'x': nrm(ks[0], (BATCH, SEQ, D_MODEL), 1.0),
        'rel_bias': nrm(ks[1], (REL_BUCKETS, REL_HEADS), 0.5),
        'norm1_gain': gain(ks[2], (L, D_MODEL)),
        'w_in': nrm(ks[3], (L, D_MODEL, IN_WIDTH), D_MODEL ** -0.5),
        'gate_bias': nrm(ks[4], (L, N_BRANCHES * D_MODEL), 0.01),
        'a_q_gain': gain(ks[5], (L, HEAD_DIM)),
        'a_k_gain': gain(ks[6], (L, HEAD_DIM)),
        'a_sink': nrm(ks[7], (L, A_HEADS), 0.5),
        'b_q_gain': gain(ks[8], (L, B_GROUPS, HEAD_DIM)),
        'b_k_gain': gain(ks[9], (L, B_GROUPS, HEAD_DIM)),
        'c_q_lat_gain': gain(ks[10], (L, C_Q_RANK)),
        'c_kv_lat_gain': gain(ks[11], (L, C_KV_RANK)),
        'c_w_uq': nrm(ks[12], (L, C_Q_RANK, C_HEADS * C_QK_DIM), C_Q_RANK ** -0.5),
        'c_w_ukv': nrm(ks[13], (L, C_KV_RANK, C_HEADS * (C_NOPE + C_V)), C_KV_RANK ** -0.5),
        'c_q_gain': gain(ks[14], (L, C_QK_DIM)),
        'c_k_gain': gain(ks[15], (L, C_QK_DIM)),
        'd_q_gain': gain(ks[16], (L, HEAD_DIM)),
        'd_k_gain': gain(ks[17], (L, HEAD_DIM)),
        'w_branch': nrm(ks[18], (L, N_BRANCHES, BRANCH_WIDTH, D_MODEL), BRANCH_WIDTH ** -0.5),
        'w_out': nrm(ks[19], (L, D_MODEL, D_MODEL), D_MODEL ** -0.5),
        'norm2_gain': gain(ks[20], (L, D_MODEL)),
        'peer_w_q': nrm(ks[21], (L, D_MODEL, PEER_HEADS * PEER_KEY_DIM), D_MODEL ** -0.5),
        'peer_sub_keys': nrm(ks[22], (L, PEER_HEADS, 2, PEER_N_KEYS, PEER_KEY_DIM // 2), (PEER_KEY_DIM // 2) ** -0.5),
        'peer_w_u': nrm(ks[23], (L, PEER_N_EXPERTS, D_MODEL), D_MODEL ** -0.5),
        'peer_w_v': nrm(ks[24], (L, PEER_N_EXPERTS, D_MODEL), PEER_HEADS ** -0.5),
    }

def reference(x, rel_bias, norm1_gain, w_in, gate_bias, a_q_gain, a_k_gain, a_sink, b_q_gain, b_k_gain,
              c_q_lat_gain, c_kv_lat_gain, c_w_uq, c_w_ukv, c_q_gain, c_k_gain, d_q_gain, d_k_gain,
              w_branch, w_out, norm2_gain, peer_w_q, peer_sub_keys, peer_w_u, peer_w_v):
    Bn, S, D = x.shape
    rows = S // GRID_W
    pos = jnp.arange(S, dtype=jnp.int32)
    row = jnp.broadcast_to(jnp.arange(rows, dtype=jnp.int32)[:, None], (rows, GRID_W)).reshape(S)
    col = jnp.broadcast_to(jnp.arange(GRID_W, dtype=jnp.int32)[None, :], (rows, GRID_W)).reshape(S)
    offsets = [int(o) for o in np.cumsum(IN_SPLITS)[:-1]]

    def heads(t, n):
        return t.reshape(Bn, S, n, HEAD_DIM)

    def groups(t):
        return t.reshape(Bn, S, B_GROUPS, B_HEADS, HEAD_DIM)

    h = x
    for l in range(DEPTH):
        hn = rms_norm(h, norm1_gain[l])
        proj = hn @ w_in[l]
        (aq, ak, av, bq, bk, bv, cq, ckv, ckr, dq, dk, dv, gpre) = jnp.split(proj, offsets, axis=-1)
        ya = mixer_a(heads(aq, A_HEADS), heads(ak, A_KV_HEADS), heads(av, A_KV_HEADS),
                     a_q_gain[l], a_k_gain[l], rel_bias[:, :A_HEADS], a_sink[l])
        yb = mixer_b(groups(bq), groups(bk), groups(bv), b_q_gain[l], b_k_gain[l], rel_bias[:, A_HEADS:])
        yc = mixer_c(cq, ckv, ckr, c_q_lat_gain[l], c_kv_lat_gain[l], c_w_uq[l], c_w_ukv[l],
                     c_q_gain[l], c_k_gain[l], pos)
        yd = mixer_d(heads(dq, D_HEADS), heads(dk, D_KV_HEADS), heads(dv, D_KV_HEADS),
                     d_q_gain[l], d_k_gain[l], row, col)
        ys = jnp.stack([ya.reshape(Bn, S, BRANCH_WIDTH), yb.reshape(Bn, S, BRANCH_WIDTH),
                        yc.reshape(Bn, S, BRANCH_WIDTH), yd.reshape(Bn, S, BRANCH_WIDTH)], axis=2)
        branches = jnp.einsum('bsnc,ncd->bsnd', ys, w_branch[l])
        gates = jax.nn.sigmoid(gpre.reshape(Bn, S, N_BRANCHES, D) + gate_bias[l].reshape(N_BRANCHES, D))
        merged = jnp.einsum('bsnd,bsnd->bsd', gates, branches)
        h = h + merged @ w_out[l]
        h = h + peer_ffn(rms_norm(h, norm2_gain[l]), peer_w_q[l], peer_sub_keys[l], peer_w_u[l], peer_w_v[l])
    return h


_drawn_inputs = setup_inputs


def setup_inputs(seed=0):
    import zlib

    import numpy as np

    out = dict(_drawn_inputs(seed))
    spreads = {}
    factors = {'gate_bias': 5.153,
     'a_q_gain': 3.344,
     'a_k_gain': 3.583,
     'a_sink': 8.0,
     'b_q_gain': 3.377,
     'b_k_gain': 3.712,
     'c_q_lat_gain': 3.593,
     'c_kv_lat_gain': 3.051,
     'c_q_gain': 3.756,
     'c_k_gain': 4.063,
     'd_q_gain': 3.569,
     'd_k_gain': 4.019}
    for name, (base, spread) in spreads.items():
        noise = np.random.default_rng([zlib.crc32(name.encode()), seed]).standard_normal(out[name].shape)
        drawn = base * np.exp(spread * noise) if base else spread * noise
        out[name] = jnp.asarray(drawn.astype(out[name].dtype))
    for name, factor in factors.items():
        out[name] = (out[name] * factor).astype(out[name].dtype)
    return out
```

```python
import math
from contextlib import ExitStack

import numpy as np

import concourse.bass as bass
from concourse import mybir

F32 = mybir.dt.float32
F32R = mybir.dt.float32r
U32 = mybir.dt.uint32
I32 = mybir.dt.int32
ALU = mybir.AluOpType
ACT = mybir.ActivationFunctionType
AX_X = mybir.AxisListType.X
AX_XY = mybir.AxisListType.XY

P = 128
LAYERS = 2
SEQ = 256
TT = SEQ // P
DM = 1024
DC = DM // P
EPS = 1e-6
NEG = -1e30
DH = 64

AQ, AK, AV = 0, 256, 384
BQ, BK, BV = 512, 1280, 2048
CQ, CKV, CKR = 2816, 3072, 3200
DQ, DK, DV = 3232, 3488, 3616
MIX = 3744
C_HEADS, C_NOPE, C_ROPE, C_QK = 4, 64, 32, 96
HEAD_ORDER = (0, 2, 1, 3)

RING = 4
N_PROJ = 16
PROJ_W = MIX // N_PROJ
N_GATE = 16
T_PROJ = 0
T_GATE_A = T_PROJ + N_PROJ
T_CW = T_GATE_A + 2
T_GATE_B = T_CW + 2
T_BRANCH = T_GATE_B + N_GATE - 2
T_OUT = T_BRANCH + 4
T_WQ = T_OUT + 4
T_KEYS = T_WQ + 4
N_PRE = T_KEYS + 2
N_EXP = 128
N_TILES = N_PRE + N_EXP
assert N_PRE % RING == 0 and N_EXP % RING == 0

BL_H1, BL_A, BL_B, BL_LAT, BL_D, BL_C, BL_H2 = 0, 8, 11, 23, 26, 29, 37
N_BLOCK = 45
QK_A, QK_B, QK_D, QK_C = 0, 3, 15, 18

UNITS = [("a", h) for h in range(4)] + [("b", h) for h in range(4)] \
    + [("d", h) for h in range(4)] + [("c", h) for h in range(4)]
N_UNIT = 16
PT_JOBS = [3 if m == "b" else 1 for m, _ in UNITS]
PT_BEFORE = [sum(PT_JOBS[:u]) for u in range(N_UNIT + 1)]
N_PT = PT_BEFORE[N_UNIT]
BRANCH_OF = {"a": 0, "b": 1, "c": 2, "d": 3}
GATE_BATCH = {4: (8, 12), 9: (12, 16)}

J_PROJ, J_GATE_A, J_C, J_GATE_B, J_MERGE, J_OUT, J_WQ = 0, 16, 18, 22, 36, 52, 56
N_JOB = 60
N_JOB_ACT = 40
N_JOB_VEC = 20

ST_H1, ST_A, ST_B, ST_LAT, ST_D, ST_C, ST_H2 = 0, 2, 14, 62, 68, 80, 104
N_STAT = 106
N_RMS = 7
N_SQ = 10

GC_N1, GC_N2, GC_GB, GC_AQ, GC_AK, GC_BQ, GC_BK, GC_CQL, GC_CKL = 0, 8, 16, 48, 49, 50, 53, 56, 58
N_GC = 59
GR_CQ, GR_CK, GR_DQ, GR_DK, GR_SINK = 0, 96, 192, 256, 320
N_GR = 324

HEADS, TOPK, KEYS = 8, 16, 128
CAND_ROWS = [(0, 1, 16), (1, 1, 8), (2, 1, 5), (3, 1, 4), (4, 1, 3), (5, 3, 2), (8, 8, 1)]
N_CAND = sum(n * w for _, n, w in CAND_ROWS)
DEAD = -3.0e38
GROUP = 4
N_GROUP = SEQ // GROUP

VEC_ORDER = 102
N_NORMED = 5


def trunk(nc, x, relb, w_proj, w_gate, w_cq, w_ckv, w_branch, w_out, w_q, keys, w_u, w_v,
          gcols, grows, ident_d, iota_d, rope_d, onehot_d, mask_d, out):
    ctx = ExitStack()
    with ctx:
        base = (nc.sbuf_base + 31) // 32 * 32
        top = nc.sbuf_usable_end // 32 * 32
        taken = {}

        def place(name, shape, dt, at):
            size = 4 * int(np.prod(shape[1:]))
            assert at + size <= top, (name, at, size, top)
            taken[name] = (at, size)
            return nc.alloc_sbuf_tensor_at(name, shape, dt, offset=at)

        class Region:
            def __init__(self, at):
                self.at = at

            def put(self, name, shape, dt=F32):
                t = place(name, shape, dt, self.at)
                self.at += (4 * int(np.prod(shape[1:])) + 31) // 32 * 32
                return t

        lasting = Region(base)
        ident = lasting.put("ident", [P, P])
        iota = lasting.put("iota", [P, P])
        rope_t = lasting.put("rope_t", [P, TT, 3, 2, 16])
        gcol = lasting.put("gcol", [P, N_GC])
        grow = lasting.put("grow", [P, N_GR])
        half_neg = lasting.put("half_neg", [P, 64])
        gate_t = lasting.put("gate_t", [P, SEQ])
        i1_t = lasting.put("i1_t", [P, SEQ])
        i2_t = lasting.put("i2_t", [P, SEQ])
        stream_at = lasting.at
        tile = lasting.put("stream_tile", [P, RING, 2048])
        stream_lo = place("stream_lo", [P, RING, 2048], F32R, stream_at)
        hi_at = lasting.at
        u_hi = lasting.put("u_hi", [P, 2, DC, P], F32R)
        v_hi = lasting.put("v_hi", [P, 2, DM], F32R)
        x_hi = lasting.put("x_hi", [P, DC, SEQ], F32R)
        x_lo = lasting.put("x_lo", [P, DC, SEQ], F32R)
        gates = place("gates", [P, 32, SEQ], F32, hi_at)
        hot1 = place("hot1", [P, 2, GROUP, P], F32, hi_at)
        hot2 = place("hot2", [P, 2, GROUP, P], F32, hi_at + 4096)
        h_at = lasting.at
        h = lasting.put("h", [P, TT, DM])
        act_out = place("act_out", [P, 2, SEQ], F32, h_at)
        gated = place("gated", [P, 2, SEQ], F32, h_at + 2048)
        g_hi = place("g_hi", [P, 2, SEQ], F32R, h_at + 4096)
        g_lo = place("g_lo", [P, 2, SEQ], F32R, h_at + 6144)
        union = lasting.at

        mix = Region(union)
        proj = mix.put("proj", [P, TT, MIX])
        bias_t = mix.put("bias_t", [P, 2, 3, 384])
        qk_at = mix.at
        qk_t = mix.put("qk_t", [P, 26, SEQ])
        s_at = mix.at
        prob = mix.put("prob", [P, 2, TT, 772])
        pt_at = mix.at
        prob_t = mix.put("prob_t", [P, 2, 6, SEQ])
        y_at = mix.at
        y_t = mix.put("y_t", [P, 8, SEQ])
        x_t = mix.put("x_t", [P, DC, SEQ])
        m_at = mix.at
        merged = mix.put("merged", [P, DC, SEQ])
        c_out = mix.put("c_out", [P, TT, 896])
        cat_at = mix.at
        cat = mix.put("cat", [P, TT, 8, C_QK])
        stat = mix.put("stat", [P, N_STAT])
        rstd = mix.put("rstd", [P, N_STAT])
        unit_m = mix.put("unit_m", [P, 2, TT])
        unit_n = mix.put("unit_n", [P, 2, TT])
        unit_d = mix.put("unit_d", [P, 2, TT])
        unit_r = mix.put("unit_r", [P, 2, TT])
        r_sb = mix.put("r_sb", [16, 128])
        hn = place("hn", [P, TT, DM], F32, qk_at)
        junk = place("junk", [P, TT, DM], F32, s_at)
        sq_b = place("sq_b", [P, TT, 1536], F32, s_at)
        sq_c = place("sq_c", [P, TT, 640], F32, s_at)
        rot = place("rot", [P, TT, 4, 192], F32, s_at + 5120)
        sq_a = place("sq_a", [P, TT, 384], F32, pt_at)
        sq_d = place("sq_d", [P, TT, 384], F32, pt_at + 3072)
        lat_t = place("lat_t", [P, 3, SEQ], F32, pt_at + 6144)
        sq_l = place("sq_l", [P, TT, 416], F32, cat_at)
        prod = place("prod", [P, 2, 512], F32, s_at)
        one_hot_b = place("one_hot_b", [33, 512], F32, s_at)
        relb_sb = place("relb_sb", [33, 16], F32, s_at + 2048)
        mask_sb = place("mask_sb", [16, 512], F32, s_at + 4096)
        rel_sb = place("rel_sb", [16, 512], F32, s_at + 6144)

        q_t = place("q_t", [P, HEADS, SEQ], F32, y_at)
        left = place("left", [P, 2 * HEADS, KEYS], F32, m_at)
        peer = Region(union)
        top_v = peer.put("top_v", [P, 2 * HEADS, TOPK])
        top_i = peer.put("top_i", [P, 2 * HEADS, TOPK], U32)
        top_f = peer.put("top_f", [P, 2 * HEADS, TOPK])
        cand = peer.put("cand", [P, HEADS, N_CAND])
        cand_i = peer.put("cand_i", [P, HEADS, N_CAND])
        cand_left = peer.put("cand_left", [P, HEADS, N_CAND])
        best = peer.put("best", [P, HEADS, TOPK])
        best_p = peer.put("best_p", [P, HEADS, TOPK], U32)
        best_f = peer.put("best_f", [P, HEADS, TOPK])
        shifted = peer.put("shifted", [P, HEADS, TOPK])
        expd = peer.put("expd", [P, HEADS, TOPK])
        esum = peer.put("esum", [P, HEADS])
        erec = peer.put("erec", [P, HEADS])
        idx_f = peer.put("idx_f", [P, HEADS, TOPK])
        idx_i = peer.put("idx_i", [P, HEADS, TOPK], I32)
        idx_1 = peer.put("idx_1", [P, HEADS, TOPK], I32)
        idx_2 = peer.put("idx_2", [P, HEADS, TOPK], I32)
        sel = peer.put("sel", [P, 3, TT, P])
        match = peer.put("match", [P, HEADS, TOPK, N_CAND])
        assert peer.at <= y_at

        gate_all = place("gate_all", [P, N_EXP, SEQ], F32, union)

        psum = [ctx.enter_context(nc.psum_tensor(f"bank{b}", [P, 512], F32)) for b in range(8)]
        rel_dram = nc.dram_tensor("rel_by_distance", (16, P, 512), F32).ap()

        def sem(name):
            return ctx.enter_context(nc.semaphore(name))

        consts_loaded = sem("consts_loaded")
        x_loaded = sem("x_loaded")
        rel_loaded = sem("rel_loaded")
        half_set = sem("half_set")
        vec_passed = sem("vec_passed")
        pool_passed = sem("pool_passed")
        rel_product = sem("rel_product")
        rel_ready = sem("rel_ready")
        rel_stored = sem("rel_stored")
        h_ready = sem("h_ready")
        gains_loaded = sem("gains_loaded")
        bias_loaded = [sem(f"bias_loaded{i}") for i in range(2)]
        loaded = [sem(f"loaded{i}") for i in range(RING)]
        v_loaded = [sem(f"v_loaded{i}") for i in range(RING)]
        tile_used = sem("tile_used")
        v_used = sem("v_used")
        squared = sem("squared")
        mean_ready = sem("mean_ready")
        rstd_ready = sem("rstd_ready")
        hn_ready = sem("hn_ready")
        turned = sem("turned")
        block_ready = sem("block_ready")
        job_ready = sem("job_ready")
        job_out = sem("job_out")
        job_sum = sem("job_sum")
        normed = sem("normed")
        scored = sem("scored")
        score_read = sem("score_read")
        max_ready = sem("max_ready")
        exped = sem("exped")
        prob_ready = sem("prob_ready")
        pt_ready = sem("pt_ready")
        pt_out = sem("pt_out")
        mixed = sem("mixed")
        mixed_out = sem("mixed_out")
        merged_ready = sem("merged_ready")
        h2_ready = sem("h2_ready")
        x_split = sem("x_split")
        peer_scored = sem("peer_scored")
        gate_exp = sem("gate_exp")
        gate_shift = sem("gate_shift")
        chosen = sem("chosen")
        chosen_turned = sem("chosen_turned")
        chosen_out = sem("chosen_out")
        hot_ready = sem("hot_ready")
        gates_filled = sem("gates_filled")
        gates_out = sem("gates_out")
        u_hi_ready = sem("u_hi_ready")
        v_hi_ready = sem("v_hi_ready")
        u_lo_ready = sem("u_lo_ready")
        v_lo_ready = sem("v_lo_ready")
        act_ready = sem("act_ready")
        gated_ready = sem("gated_ready")
        experts_done = sem("experts_done")
        vec_order = sem("vec_order")
        stored = sem("stored")

        block = ctx.enter_context(nc.Block())

        @block.sync
        def _(sp):
            sp.dma_start(h[:], x.rearrange("(t p) d -> p t d", p=P)).then_inc(x_loaded, 16)
            pre = [(w_proj, j, DC * PROJ_W) for j in range(N_PROJ)]
            pre += [(w_gate, j, 2048) for j in range(2)]
            pre += [(w_cq, 0, 768), (w_ckv, 0, 512)]
            pre += [(w_gate, j, 2048) for j in range(2, N_GATE)]
            pre += [(w_branch, j, 2048) for j in range(4)]
            pre += [(w_out, j, 2048) for j in range(4)]
            pre += [(w_q, j, 2048) for j in range(4)]
            pre += [(keys, j, 512) for j in range(2)]
            assert len(pre) == N_PRE
            with sp.Fori(0, LAYERS) as layer:
                for j, (src, n, width) in enumerate(pre):
                    if j == 0:
                        sp.wait_ge(v_used, layer * N_EXP + RING)
                    sp.wait_ge(tile_used, layer * N_TILES + (j + 1))
                    sp.dma_start(tile[:, j % RING, 0:width], src[layer, n]).then_inc(loaded[j % RING], 16)
                with sp.Fori(0, N_EXP // RING) as lap:
                    for s in range(RING):
                        sp.wait_ge(tile_used, layer * N_TILES + lap * RING + (N_PRE + s + 1))
                        sp.dma_start(tile[:, s, 0:1024], w_u[layer, lap * RING + s]).then_inc(loaded[s], 16)
                        sp.wait_ge(v_used, layer * N_EXP + lap * RING + (s + 1))
                        sp.dma_start(tile[:, s, 1024:2048], w_v[layer, lap * RING + s]).then_inc(v_loaded[s], 16)
            sp.wait_ge(h_ready, LAYERS + 1)
            sp.dma_start(out.rearrange("(t p) d -> p t d", p=P), h[:]).then_inc(stored, 16)
            sp.wait_ge(stored, 16)

        @block.gpsimd
        def _(pool):
            pool.dma_start(one_hot_b[:], onehot_d).then_inc(rel_loaded, 16)
            pool.dma_start(relb_sb[:], relb).then_inc(rel_loaded, 16)
            pool.dma_start(mask_sb[:], mask_d).then_inc(rel_loaded, 16)
            pool.dma_start(ident[:], ident_d).then_inc(consts_loaded, 16)
            pool.dma_start(iota[:], iota_d).then_inc(consts_loaded, 16)
            pool.dma_start(rope_t[:], rope_d).then_inc(consts_loaded, 16)
            nc.gpsimd.memset(half_neg[:], -0.5).then_inc(half_set, 1)
            pool.wait_ge(rel_ready, 1)
            pool.dma_start(rel_dram, rel_sb[:].unsqueeze(1).broadcast_to([16, P, 512])).then_inc(rel_stored, 16)
            pool.wait_ge(half_set, 1)

            def bias_load(layer, u):
                mixer, head = UNITS[u]
                if u >= 2:
                    pool.wait_ge(score_read, layer * N_UNIT + (u - 1))
                    pool.sem_inc(pool_passed, 1)
                if mixer == "a":
                    src = bass.AP(tensor=rel_dram.tensor, offset=head * P * 512 + 127, ap=[[511, P], [1, 384]])
                    dst = bias_t[:, u % 2, 0, :]
                else:
                    src = bass.AP(tensor=rel_dram.tensor, offset=(4 + head) * P * 512 + 127,
                                  ap=[[511, P], [4 * P * 512, 3], [1, 384]])
                    dst = bias_t[:, u % 2]
                pool.dma_start(dst, src).then_inc(bias_loaded[u % 2], 16)

            def rsqrt(layer, k, at, n):
                pool.wait_ge(mean_ready, layer * N_RMS + (k + 1))
                if n <= 64:
                    nc.gpsimd.tensor_tensor(rstd[:, at:at + n], stat[:, at:at + n], half_neg[:, 0:n],
                                            ALU.pow).then_inc(rstd_ready, 1)

            with pool.Fori(0, LAYERS) as layer:
                pool.wait_ge(h_ready, layer + 1)
                pool.sem_inc(pool_passed, 1)
                pool.dma_start(gcol[:], gcols[layer]).then_inc(gains_loaded, 16)
                pool.dma_start(grow[:], grows[layer].partition_broadcast(P)).then_inc(gains_loaded, 16)
                rsqrt(layer, 0, ST_H1, 2)
                rsqrt(layer, 1, ST_A, 12)
                rsqrt(layer, 2, ST_B, 48)
                rsqrt(layer, 3, ST_LAT, 6)
                pool.wait_ge(rel_stored, 16)
                bias_load(layer, 0)
                bias_load(layer, 1)
                rsqrt(layer, 4, ST_D, 12)
                rsqrt(layer, 5, ST_C, 24)
                for u in range(2, 8):
                    bias_load(layer, u)
                rsqrt(layer, 6, ST_H2, 2)

        @block.scalar
        def _(act):
            act.sem_inc(gates_out, 2)
            act.wait_ge(consts_loaded, 48)
            act.wait_ge(x_loaded, 16)

            def rms_rows(layer, at, n_before, hn_before, block0, gain0, src_ready):
                src_ready()
                for t in range(TT):
                    nc.scalar.activation(junk[:, t], h[:, t], ACT.Square,
                                         accum_out=stat[:, at + t:at + t + 1]).then_inc(squared, 1)
                act.wait_ge(rstd_ready, layer * N_RMS + (n_before + 1))
                for t in range(TT):
                    nc.scalar.activation(hn[:, t], h[:, t], ACT.Copy,
                                         scale=rstd[:, at + t:at + t + 1]).then_inc(hn_ready, 1)
                for c in range(DC):
                    turn_out(layer, block0 + c, x_t[:, c, :], gcol[:, gain0 + c:gain0 + c + 1])

            def turn_out(layer, k, dst, gain=None, rows=P):
                act.wait_ge(turned, layer * N_BLOCK + (k + 1))
                scale = 1.0 if gain is None else gain
                nc.scalar.activation(dst, psum[5 + k % 2][0:rows, 0:SEQ], ACT.Copy,
                                     scale=scale).then_inc(block_ready, 1)

            def job_wait(layer, j):
                act.wait_ge(job_ready, layer * N_JOB + (j + 1))

            def gate_out(layer, j, tile_no):
                job_wait(layer, j)
                for i in range(2):
                    c = 2 * tile_no + i
                    ins = nc.scalar.activation(gates[:, c, :], psum[j % 2][:, i * SEQ:(i + 1) * SEQ],
                                               ACT.Sigmoid, bias=gcol[:, GC_GB + c:GC_GB + c + 1])
                ins.then_inc(job_out, 1)

            def exp_rows(layer, u):
                mixer, _ = UNITS[u]
                act.wait_ge(max_ready, layer * N_UNIT + (u + 1))
                if mixer in "cd":
                    act.wait_ge(pt_ready, layer * N_PT + PT_BEFORE[u - 1])
                for t in range(TT):
                    if mixer == "a":
                        dst, src, scale = prob[:, u % 2, t, 0:257], prob[:, u % 2, t, 0:257], 1.0
                    elif mixer == "b":
                        dst, src, scale = prob[:, u % 2, t, 0:768], prob[:, u % 2, t, 0:768], 1.0
                    else:
                        scale = DH ** -0.5 if mixer == "d" else C_QK ** -0.5
                        dst = prob[:, u % 2, t, 0:SEQ]
                        src = psum[2 + u % 3][:, t * SEQ:(t + 1) * SEQ]
                    nc.scalar.activation(dst, src, ACT.Exp, bias=unit_m[:, u % 2, t:t + 1], scale=scale,
                                         accum_out=unit_d[:, u % 2, t:t + 1]).then_inc(exped, 1)
                if mixer in "cd":
                    act.wait_ge(exped, layer * (2 * N_UNIT) + (2 * u + 2))
                    act.sem_inc(score_read, 1)

            def turned_probs_out(layer, u):
                if u >= 2:
                    act.wait_ge(mixed, layer * N_UNIT + (u - 1))
                for i in range(PT_JOBS[u]):
                    k = PT_BEFORE[u] + i
                    act.wait_ge(pt_ready, layer * N_PT + (k + 1))
                    nc.scalar.activation(prob_t[:, u % 2, 2 * i:2 * i + 2, :],
                                         psum[5 + k % 2][:].rearrange("p (c q) -> p c q", c=2),
                                         ACT.Copy).then_inc(pt_out, 1)
                if u % 2:
                    mixer, head = UNITS[u]
                    act.wait_ge(mixed, layer * N_UNIT + (u + 1))
                    nc.scalar.activation(y_t[:, 2 * BRANCH_OF[mixer] + head // 2, :], psum[7][:, 0:SEQ],
                                         ACT.Copy).then_inc(mixed_out, 1)

            def hi_u(m_slot, wait):
                wait()
                nc.scalar.activation(u_hi[:, m_slot % 2], tile[:, m_slot, 0:1024]
                                     .rearrange("p (c e) -> p c e", c=DC), ACT.Copy).then_inc(u_hi_ready, 1)

            def hi_v(m_slot):
                nc.scalar.activation(v_hi[:, m_slot % 2], tile[:, m_slot, 1024:2048],
                                     ACT.Copy).then_inc(v_hi_ready, 1)

            with act.Fori(0, LAYERS) as layer:
                def layer_start():
                    act.wait_ge(h_ready, layer + 1)
                    act.wait_ge(gains_loaded, layer * 32 + 32)

                rms_rows(layer, ST_H1, 0, 0, BL_H1, GC_N1, layer_start)
                for j in range(N_PROJ):
                    job_wait(layer, j)
                    nc.scalar.activation(proj[:, :, j * PROJ_W:(j + 1) * PROJ_W],
                                         psum[j % 2][:, 0:2 * PROJ_W].rearrange("p (t c) -> p t c", t=TT),
                                         ACT.Copy).then_inc(job_out, 1)
                    if j == 1:
                        act.wait_ge(job_out, layer * N_JOB_ACT + 2)
                        nc.scalar.activation(sq_a[:], proj[:, :, AQ:AV], ACT.Square).then_inc(squared, 1)
                    if j == 8:
                        act.wait_ge(job_out, layer * N_JOB_ACT + 9)
                        nc.scalar.activation(sq_b[:], proj[:, :, BQ:BV], ACT.Square).then_inc(squared, 1)
                    if j == 13:
                        act.wait_ge(job_out, layer * N_JOB_ACT + 14)
                        nc.scalar.activation(sq_l[:], proj[:, :, CQ:DQ], ACT.Square).then_inc(squared, 1)
                act.wait_ge(job_out, layer * N_JOB_ACT + N_PROJ)
                nc.scalar.activation(sq_d[:], proj[:, :, DQ:DV], ACT.Square).then_inc(squared, 1)

                for i in range(3):
                    gain = GC_AK if i == 2 else GC_AQ
                    turn_out(layer, BL_A + i, qk_t[:, QK_A + i, :], gcol[:, gain:gain + 1])
                for i in range(12):
                    gain = (GC_BQ if i < 6 else GC_BK) + i % 6 // 2
                    turn_out(layer, BL_B + i, qk_t[:, QK_B + i, :], gcol[:, gain:gain + 1])
                for i in range(3):
                    turn_out(layer, BL_LAT + i, lat_t[:, i, :], gcol[:, GC_CQL + i:GC_CQL + i + 1])
                for i in range(2):
                    gate_out(layer, J_GATE_A + i, i)
                for i in range(4):
                    j = J_C + i
                    job_wait(layer, j)
                    dst = c_out[:, i % 2, 0:384] if i < 2 else c_out[:, i % 2, 384:896]
                    nc.scalar.activation(dst, psum[j % 2][:, 0:384 if i < 2 else 512],
                                         ACT.Copy).then_inc(job_out, 1)
                act.wait_ge(job_out, layer * N_JOB_ACT + (J_C + 4))
                nc.scalar.activation(sq_c[:, :, 0:384], c_out[:, :, 0:384], ACT.Square).then_inc(squared, 1)
                for t in range(TT):
                    ins = nc.scalar.activation(
                        sq_c[:, t, 384:640].rearrange("p (h c) -> p h c", h=4),
                        c_out[:, t, 384:896].rearrange("p (h c) -> p h c", h=4)[:, :, 0:C_NOPE], ACT.Square)
                ins.then_inc(squared, 1)
                for i in range(2, 8):
                    gate_out(layer, J_GATE_B + i - 2, i)
                for i in range(3):
                    turn_out(layer, BL_D + i, qk_t[:, QK_D + i, :])
                for i in range(8):
                    turn_out(layer, BL_C + i, qk_t[0:C_QK, QK_C + i, :], rows=C_QK)
                for u in range(N_UNIT + 1):
                    for i in range(*GATE_BATCH.get(u, (0, 0))):
                        gate_out(layer, J_GATE_B + i - 2, i)
                    if u < N_UNIT:
                        exp_rows(layer, u)
                    if u:
                        turned_probs_out(layer, u - 1)

                def h2_there():
                    act.wait_ge(h2_ready, layer + 1)

                rms_rows(layer, ST_H2, 6, 2, BL_H2, GC_N2, h2_there)
                for i in range(4):
                    j = J_WQ + i
                    job_wait(layer, j)
                    nc.scalar.activation(q_t[:, 2 * i:2 * i + 2, :],
                                         psum[j % 2][:].rearrange("p (h t) -> p h t", h=2),
                                         ACT.Copy).then_inc(job_out, 1)
                for t in range(TT):
                    act.wait_ge(gate_shift, layer * TT + (t + 1))
                    nc.scalar.activation(expd[:], shifted[:], ACT.Exp).then_inc(gate_exp, 1)
                act.wait_ge(chosen_turned, layer + 1)
                for i, dst in enumerate((gate_t, i1_t, i2_t)):
                    ins = nc.scalar.activation(dst[:], psum[4 + i][:, 0:SEQ], ACT.Copy)
                ins.then_inc(chosen_out, 1)
                with act.Fori(0, N_GROUP // 2) as pair:
                    for b in range(2):
                        act.wait_ge(gates_filled, layer * N_GROUP + pair * 2 + (b + 3))
                        nc.scalar.activation(
                            gate_all[:, :, bass.ds(pair * (2 * GROUP) + b * GROUP, GROUP)],
                            psum[6 + b][:].rearrange("p (t e) -> p e t", t=GROUP),
                            ACT.Copy).then_inc(gates_out, 1)

                def u_there(lap, s, more):
                    def wait():
                        act.wait_ge(loaded[s], layer * (16 * N_TILES // RING) + lap * 16
                                    + 16 * (N_PRE // RING + 1 + more))
                    return wait

                def v_there(lap, s, more):
                    act.wait_ge(v_loaded[s], layer * (16 * N_EXP // RING) + lap * 16 + 16 * (1 + more))

                hi_u(0, u_there(0, 0, 0))
                hi_u(1, u_there(0, 1, 0))
                v_there(0, 0, 0)
                hi_v(0)

                def expert_step(lap, s, last):
                    n = layer * N_TILES + lap * RING + (N_PRE + RING + s)
                    act.wait_ge(tile_used, n + 1)
                    nc.scalar.activation(act_out[:, s % 2], psum[4 + s % 2][:, 0:SEQ],
                                         ACT.Gelu).then_inc(act_ready, 1)
                    if not (last and s >= 2):
                        hi_u((s + 2) % RING, u_there(lap, (s + 2) % RING, (s + 2) // RING))
                    if not (last and s >= 3):
                        v_there(lap, (s + 1) % RING, (s + 1) // RING)
                        act.wait_ge(v_used, layer * N_EXP + lap * RING + (s + RING))
                        hi_v((s + 1) % RING)

                with act.Fori(0, N_EXP // RING - 1) as lap:
                    for s in range(RING):
                        expert_step(lap, s, False)
                for s in range(RING):
                    expert_step(N_EXP // RING - 1, s, True)

        @block.vector
        def _(vec):
            count = [0]

            def done(ins):
                count[0] += 1
                ins.then_inc(vec_order, 1)

            def settle(layer):
                vec.wait_ge(vec_order, layer * VEC_ORDER + count[0])

            def settle_apart(layer):
                settle(layer)
                vec.sem_inc(vec_passed, 1)

            vec.wait_ge(rel_product, 1)
            vec.wait_ge(rel_loaded, 48)
            nc.vector.tensor_tensor(rel_sb[:], psum[0][0:16, :], mask_sb[:], ALU.add).then_inc(rel_ready, 1)
            vec.wait_ge(consts_loaded, 48)
            vec.wait_ge(x_loaded, 16)
            vec.sem_inc(h_ready, 1)

            def mean(at, n, width):
                return nc.vector.tensor_scalar(stat[:, at:at + n], stat[:, at:at + n], 1.0 / width, EPS,
                                               ALU.mult, ALU.add)

            def stats(at, heads):
                return stat[:, at:at + TT * heads].rearrange("p (t h) -> p t h", t=TT)

            def scales(at, heads, width):
                r = rstd[:, at:at + TT * heads].rearrange("p (t h) -> p t h", t=TT)
                return r.unsqueeze(3).broadcast_to([P, TT, heads, width])

            def rope(layer, src, dst, heads, axes, t, at=0):
                n = heads * len(axes) * 16
                parts = [rot[:, t, i, at:at + n].rearrange("p (h a c) -> p h a c", h=heads, a=len(axes))
                         for i in range(4)]
                tab = rope_t[:, t, axes[0]:axes[-1] + 1]
                cos, sin = (tab[:, :, i, :].unsqueeze(1).broadcast_to([P, heads, len(axes), 16])
                            for i in range(2))
                lo, hi = src[:, :, :, 0:16], src[:, :, :, 16:32]
                nc.vector.tensor_tensor(parts[0], lo, cos, ALU.mult)
                nc.vector.tensor_tensor(parts[1], hi, sin, ALU.mult)
                nc.vector.tensor_tensor(parts[2], lo, sin, ALU.mult)
                done(nc.vector.tensor_tensor(parts[3], hi, cos, ALU.mult))
                settle(layer)
                nc.vector.tensor_tensor(dst[:, :, :, 0:16], parts[0], parts[1], ALU.subtract)
                return nc.vector.tensor_tensor(dst[:, :, :, 16:32], parts[2], parts[3], ALU.add)

            def unit_scores(layer, u):
                mixer, head = UNITS[u]
                vec.wait_ge(scored, layer * N_UNIT + (u + 1))
                if mixer in "cd":
                    src = psum[2 + u % 3][:].rearrange("p (t k) -> p t k", t=TT)
                    done(nc.vector.tensor_reduce(unit_n[:, u % 2], src, AX_X, ALU.max))
                    settle(layer)
                    scale = DH ** -0.5 if mixer == "d" else C_QK ** -0.5
                    nc.vector.tensor_scalar(unit_m[:, u % 2], unit_n[:, u % 2], -scale, None,
                                            ALU.mult).then_inc(max_ready, 1)
                    return
                vec.wait_ge(bias_loaded[u % 2], layer * 64 + 16 * (u // 2 + 1))
                if u >= 2:
                    vec.wait_ge(pt_ready, layer * N_PT + PT_BEFORE[u - 1])
                groups = 1 if mixer == "a" else 3
                for g in range(groups):
                    bank = 2 + u % 3 if mixer == "a" else 2 + g
                    for t in range(TT):
                        ins = nc.vector.scalar_tensor_tensor(
                            out=prob[:, u % 2, t, g * SEQ:(g + 1) * SEQ], in0=psum[bank][:, t * SEQ:(t + 1) * SEQ],
                            scalar=DH ** -0.5, in1=bias_t[:, u % 2, g, P - P * t:P - P * t + SEQ],
                            op0=ALU.mult, op1=ALU.add)
                width = groups * SEQ
                ins.then_inc(score_read, 1)
                if mixer == "a":
                    done(nc.vector.tensor_copy(
                        prob[:, u % 2, :, SEQ:SEQ + 1],
                        grow[:, GR_SINK + head:GR_SINK + head + 1].unsqueeze(1).broadcast_to([P, TT, 1])))
                    width += 1
                    settle(layer)
                vec.wait_ge(score_read, layer * N_UNIT + (u + 1))
                nc.vector.tensor_reduce(unit_m[:, u % 2], prob[:, u % 2, :, 0:width], AX_X, ALU.max,
                                        negate=True).then_inc(max_ready, 1)

            def unit_norm(layer, u):
                width = 768 if UNITS[u][0] == "b" else SEQ
                vec.wait_ge(exped, layer * (2 * N_UNIT) + (2 * u + 2))
                done(nc.vector.reciprocal(unit_r[:, u % 2], unit_d[:, u % 2]))
                settle(layer)
                for t in range(TT):
                    ins = nc.vector.tensor_scalar(prob[:, u % 2, t, 0:width], prob[:, u % 2, t, 0:width],
                                                  unit_r[:, u % 2, t:t + 1], None, ALU.mult)
                ins.then_inc(prob_ready, 1)

            def top16(layer, n, src, work, values, places):
                for i in range(n):
                    ins = nc.vector.max(values[:, i, 0:8], src(i))
                done(ins)
                settle_apart(layer)
                for i in range(n):
                    nc.vector.max_index(places[:, i, 0:8], values[:, i, 0:8], src(i))
                for i in range(n):
                    ins = nc.vector.match_replace(work[:, i, :], values[:, i, 0:8], src(i), DEAD)
                done(ins)
                settle_apart(layer)
                for i in range(n):
                    ins = nc.vector.max(values[:, i, 8:16], work[:, i, :])
                done(ins)
                settle_apart(layer)
                for i in range(n):
                    ins = nc.vector.max_index(places[:, i, 8:16], values[:, i, 8:16], work[:, i, :])
                return ins

            def spread(dst, first, second, op):
                at = 0
                for a, rows, width in CAND_ROWS:
                    o = dst[:, :, at:at + rows * width].rearrange("p h (a b) -> p h a b", a=rows)
                    shape = [P, HEADS, rows, width]
                    ins = nc.vector.tensor_tensor(o, first[:, :, a:a + rows].unsqueeze(3).broadcast_to(shape),
                                                  second[:, :, 0:width].unsqueeze(2).broadcast_to(shape), op)
                    at += rows * width
                return ins

            def choose(layer, t):
                banks = (4, 0)[t]

                def scores(i):
                    head, half = i // 2, i % 2
                    b = psum[banks + 2 * half + head // 4]
                    at = head % 4 * KEYS
                    return b[:, at:at + KEYS]

                done(top16(layer, 2 * HEADS, scores, left, top_v, top_i))
                settle(layer)
                done(nc.vector.tensor_copy(top_f[:], top_i[:]))
                halves_v = top_v[:].rearrange("p (h c) k -> p h c k", c=2)
                halves_f = top_f[:].rearrange("p (h c) k -> p h c k", c=2)
                done(spread(cand, halves_v[:, :, 0], halves_v[:, :, 1], ALU.add))
                settle(layer)
                done(nc.vector.tensor_scalar(halves_f[:, :, 0], halves_f[:, :, 0], float(KEYS), None, ALU.mult))
                settle(layer)
                done(spread(cand_i, halves_f[:, :, 0], halves_f[:, :, 1], ALU.add))
                settle_apart(layer)
                done(top16(layer, HEADS, lambda i: cand[:, i, :], cand_left, best, best_p))
                settle(layer)
                nc.vector.tensor_tensor(shifted[:], best[:], best[:, :, 0:1].broadcast_to([P, HEADS, TOPK]),
                                        ALU.subtract).then_inc(gate_shift, 1)
                done(nc.vector.tensor_copy(best_f[:], best_p[:]))
                settle(layer)
                shape = [P, HEADS, TOPK, N_CAND]
                for i in range(HEADS):
                    sub = shape[0:1] + shape[2:]
                    ins = nc.vector.tensor_tensor(match[:, i], iota[:, 0:N_CAND].unsqueeze(1).broadcast_to(sub),
                                                  best_f[:, i].unsqueeze(2).broadcast_to(sub), ALU.is_equal)
                done(ins)
                settle(layer)
                done(nc.vector.tensor_tensor(match[:], match[:], cand_i[:].unsqueeze(2).broadcast_to(shape),
                                             ALU.mult))
                settle(layer)
                done(nc.vector.tensor_reduce(idx_f[:], match[:], AX_X, ALU.add))
                settle(layer)
                done(nc.vector.tensor_copy(idx_i[:], idx_f[:]))
                settle(layer)
                nc.vector.tensor_scalar(idx_1[:], idx_i[:], 7, None, ALU.arith_shift_right)
                done(nc.vector.tensor_scalar(idx_2[:], idx_i[:], KEYS - 1, None, ALU.bitwise_and))
                settle(layer)

                def flat(a):
                    return a[:].rearrange("p h k -> p (h k)")

                nc.vector.tensor_copy(sel[:, 1, t], flat(idx_1))
                nc.vector.tensor_copy(sel[:, 2, t], flat(idx_2))
                vec.wait_ge(gate_exp, layer * TT + (t + 1))
                done(nc.vector.tensor_reduce(esum[:], expd[:], AX_X, ALU.add))
                settle(layer)
                done(nc.vector.reciprocal(erec[:], esum[:]))
                settle(layer)
                nc.vector.tensor_tensor(sel[:, 0, t].rearrange("p (h k) -> p h k", h=HEADS), expd[:],
                                        erec[:].unsqueeze(2).broadcast_to([P, HEADS, TOPK]),
                                        ALU.mult).then_inc(chosen, 1)

            with vec.Fori(0, LAYERS) as layer:
                count[0] = 0

                def squares(k):
                    vec.wait_ge(squared, layer * N_SQ + k)

                def rsqrts(k):
                    vec.wait_ge(rstd_ready, layer * N_RMS + k)

                squares(2)
                mean(ST_H1, 2, DM).then_inc(mean_ready, 1)

                squares(3)
                done(nc.vector.tensor_reduce(stats(ST_A, 6), sq_a[:].rearrange("p t (h c) -> p t h c", h=6),
                                             AX_X, ALU.add))
                settle(layer)
                mean(ST_A, 12, DH).then_inc(mean_ready, 1)
                rsqrts(2)
                v = proj[:, :, AQ:AV].rearrange("p t (h c) -> p t h c", h=6)
                nc.vector.tensor_tensor(v, v, scales(ST_A, 6, DH), ALU.mult).then_inc(normed, 1)

                squares(4)
                done(nc.vector.tensor_reduce(stats(ST_B, 24), sq_b[:].rearrange("p t (h c) -> p t h c", h=24),
                                             AX_X, ALU.add))
                settle(layer)
                mean(ST_B, 48, DH).then_inc(mean_ready, 1)
                rsqrts(3)
                v = proj[:, :, BQ:BV].rearrange("p t (h c) -> p t h c", h=24)
                nc.vector.tensor_tensor(v, v, scales(ST_B, 24, DH), ALU.mult).then_inc(normed, 1)

                squares(5)
                for i, (lo, hi) in enumerate(((0, 256), (256, 384), (384, 416))):
                    ins = nc.vector.tensor_reduce(stat[:, ST_LAT + 2 * i:ST_LAT + 2 * i + 2].unsqueeze(2),
                                                  sq_l[:, :, lo:hi], AX_X, ALU.add)
                done(ins)
                settle(layer)
                mean(ST_LAT, 2, 256)
                mean(ST_LAT + 2, 2, 128)
                mean(ST_LAT + 4, 2, C_ROPE).then_inc(mean_ready, 1)
                rsqrts(4)
                for i, (lo, hi) in enumerate(((CQ, CKV), (CKV, CKR), (CKR, DQ))):
                    r = rstd[:, ST_LAT + 2 * i:ST_LAT + 2 * i + 2].unsqueeze(2).broadcast_to([P, TT, hi - lo])
                    ins = nc.vector.tensor_tensor(proj[:, :, lo:hi], proj[:, :, lo:hi], r, ALU.mult)
                ins.then_inc(normed, 1)

                squares(6)
                done(nc.vector.tensor_reduce(stats(ST_D, 6), sq_d[:].rearrange("p t (h c) -> p t h c", h=6),
                                             AX_X, ALU.add))
                settle(layer)
                mean(ST_D, 12, DH).then_inc(mean_ready, 1)
                rsqrts(5)
                v = proj[:, :, DQ:DV].rearrange("p t (h c) -> p t h c", h=6)
                done(nc.vector.tensor_tensor(v, v, scales(ST_D, 6, DH), ALU.mult))
                settle(layer)
                vec.wait_ge(gains_loaded, layer * 32 + 32)
                for lo, hi, g in ((0, 4, GR_DQ), (4, 6, GR_DK)):
                    shape = [P, TT, hi - lo, DH]
                    gain = grow[:, g:g + DH].unsqueeze(1).unsqueeze(1).broadcast_to(shape)
                    ins = nc.vector.tensor_tensor(v[:, :, lo:hi], v[:, :, lo:hi], gain, ALU.mult)
                done(ins)
                settle(layer)
                for t in range(TT):
                    s = proj[:, t, DQ:DV].rearrange("p (h a c) -> p h a c", h=6, a=2)
                    ins = rope(layer, s, s, 6, (1, 2), t)
                    done(ins)
                settle(layer)
                vec.sem_inc(normed, 1)

                squares(8)
                q4 = sq_c[:, :, 0:384].rearrange("p t (h c) -> p t h c", h=4)
                nc.vector.tensor_reduce(stats(ST_C, 4), q4[:, :, :, 0:C_NOPE], AX_X, ALU.add)
                nc.vector.tensor_reduce(stats(ST_C + 8, 4), q4[:, :, :, C_NOPE:C_QK], AX_X, ALU.add)
                done(nc.vector.tensor_reduce(stats(ST_C + 16, 4), sq_c[:, :, 384:640]
                                             .rearrange("p t (h c) -> p t h c", h=4), AX_X, ALU.add))
                settle(layer)
                mean(ST_C, 8, C_NOPE)
                mean(ST_C + 8, 8, C_ROPE)
                mean(ST_C + 16, 8, C_NOPE).then_inc(mean_ready, 1)
                rsqrts(6)
                qv = c_out[:, :, 0:384].rearrange("p t (h c) -> p t h c", h=4)
                kv = c_out[:, :, 384:896].rearrange("p t (h c) -> p t h c", h=4)
                qo, ko = cat[:, :, 0:4], cat[:, :, 4:8]
                nc.vector.tensor_tensor(qo[:, :, :, 0:C_NOPE], qv[:, :, :, 0:C_NOPE], scales(ST_C, 4, C_NOPE),
                                        ALU.mult)
                nc.vector.tensor_tensor(qo[:, :, :, C_NOPE:C_QK], qv[:, :, :, C_NOPE:C_QK],
                                        scales(ST_C + 8, 4, C_ROPE), ALU.mult)
                done(nc.vector.tensor_tensor(ko[:, :, :, 0:C_NOPE], kv[:, :, :, 0:C_NOPE],
                                             scales(ST_C + 16, 4, C_NOPE), ALU.mult))
                settle(layer)
                gq = grow[:, GR_CQ:GR_CQ + C_QK].unsqueeze(1).unsqueeze(1).broadcast_to([P, TT, 4, C_QK])
                nc.vector.tensor_tensor(qo, qo, gq, ALU.mult)
                gk = grow[:, GR_CK:GR_CK + C_NOPE].unsqueeze(1).unsqueeze(1).broadcast_to([P, TT, 4, C_NOPE])
                nc.vector.tensor_tensor(ko[:, :, :, 0:C_NOPE], ko[:, :, :, 0:C_NOPE], gk, ALU.mult)
                gp = grow[:, GR_CK + C_NOPE:GR_CK + C_QK].unsqueeze(1).broadcast_to([P, TT, C_ROPE])
                done(nc.vector.tensor_tensor(proj[:, :, CKR:DQ], proj[:, :, CKR:DQ], gp, ALU.mult))
                settle(layer)
                for t in range(TT):
                    s = cat[:, t, 0:4, C_NOPE:C_QK].unsqueeze(2)
                    done(rope(layer, s, s, 4, (0,), t))
                    s = proj[:, t, CKR:DQ].unsqueeze(1).unsqueeze(1)
                    done(rope(layer, s, s, 1, (0,), t, 128))
                settle(layer)
                for t in range(TT):
                    ins = nc.vector.tensor_copy(cat[:, t, 4:8, C_NOPE:C_QK],
                                                proj[:, t, CKR:DQ].unsqueeze(1).broadcast_to([P, 4, C_ROPE]))
                ins.then_inc(normed, 1)

                for u in range(N_UNIT + 1):
                    if u < N_UNIT:
                        unit_scores(layer, u)
                    if u:
                        unit_norm(layer, u - 1)

                for j in range(16):
                    n, pair = j // 4, j % 4
                    vec.wait_ge(job_ready, layer * N_JOB + (J_MERGE + j + 1))
                    if j == 0:
                        vec.wait_ge(job_out, layer * N_JOB_ACT + J_MERGE)
                        vec.wait_ge(mixed, layer * N_UNIT + N_UNIT)
                    dst = merged[:, 2 * pair:2 * pair + 2, :]
                    gate = gates[:, 8 * n + 2 * pair:8 * n + 2 * pair + 2, :]
                    src = psum[(J_MERGE + j) % 2][:].rearrange("p (c t) -> p c t", c=2)
                    if n == 0:
                        nc.vector.tensor_tensor(dst, src, gate, ALU.mult).then_inc(job_sum, 1)
                        continue
                    part = prod[:, j % 2].rearrange("p (c t) -> p c t", c=2)
                    nc.vector.tensor_tensor(part, src, gate, ALU.mult).then_inc(job_sum, 1)
                    vec.wait_ge(job_sum, layer * N_JOB_VEC + (j + 1))
                    ins = nc.vector.tensor_tensor(dst, dst, part, ALU.add)
                    done(ins)
                    if pair == 3:
                        settle(layer)
                vec.sem_inc(merged_ready, 1)

                for j in range(4):
                    vec.wait_ge(job_ready, layer * N_JOB + (J_OUT + j + 1))
                    dst = h[:, :, j * 256:(j + 1) * 256]
                    nc.vector.tensor_tensor(dst, psum[(J_OUT + j) % 2][:].rearrange("p (t c) -> p t c", t=TT),
                                            dst, ALU.add).then_inc(job_sum, 1)
                vec.wait_ge(job_sum, layer * N_JOB_VEC + N_JOB_VEC)
                vec.sem_inc(h2_ready, 1)

                squares(10)
                mean(ST_H2, 2, DM).then_inc(mean_ready, 1)
                vec.wait_ge(block_ready, layer * N_BLOCK + N_BLOCK)
                done(nc.vector.tensor_copy(x_hi[:], x_t[:]))
                settle(layer)
                nc.vector.tensor_tensor(x_lo[:], x_t[:], x_hi[:], ALU.subtract).then_inc(x_split, 1)

                vec.wait_ge(peer_scored, layer + 1)
                vec.sem_inc(vec_passed, 1)
                for t in range(TT):
                    choose(layer, t)
                assert count[0] == VEC_ORDER, count[0]

                vec.wait_ge(chosen_out, layer + 1)
                vec.sem_inc(vec_passed, 1)
                with vec.Fori(0, N_GROUP // 2) as pair:
                    for b in range(2):
                        vec.wait_ge(gates_filled, layer * N_GROUP + pair * 2 + (b + 1))
                        for i in range(GROUP):
                            t = pair * (2 * GROUP) + (b * GROUP + i)
                            nc.vector.tensor_scalar(hot1[:, b, i], iota[:], i1_t[:, bass.ds(t, 1)],
                                                    gate_t[:, bass.ds(t, 1)], ALU.is_equal, ALU.mult)
                            ins = nc.vector.tensor_scalar(hot2[:, b, i], iota[:], i2_t[:, bass.ds(t, 1)],
                                                          None, ALU.is_equal)
                        ins.then_inc(hot_ready, 1)

                def lo_u(lap, s, more):
                    vec.wait_ge(u_hi_ready, layer * N_EXP + lap * RING + (more * RING + s + 1))
                    src = tile[:, s, 0:1024]
                    nc.vector.tensor_tensor(stream_lo[:, s, 0:1024], src,
                                            u_hi[:, s % 2].rearrange("p c e -> p (c e)"),
                                            ALU.subtract).then_inc(u_lo_ready, 1)

                def lo_v(lap, s, more):
                    vec.wait_ge(v_hi_ready, layer * N_EXP + lap * RING + (more * RING + s + 1))
                    nc.vector.tensor_tensor(stream_lo[:, s, 1024:2048], tile[:, s, 1024:2048], v_hi[:, s % 2],
                                            ALU.subtract).then_inc(v_lo_ready, 1)

                def expert_step(lap, s, last):
                    n = layer * N_EXP + lap * RING
                    vec.wait_ge(act_ready, n + (s + 1))
                    i1 = lap * RING + s
                    g = gate_all[:, bass.ds(i1, 1), :] if not last else gate_all[:, i1:i1 + 1, :]
                    nc.vector.tensor_tensor(gated[:, s % 2].unsqueeze(1), act_out[:, s % 2].unsqueeze(1), g,
                                            ALU.mult).then_inc(gated_ready, 1)
                    vec.wait_ge(gated_ready, 3 * n + (3 * s + 1))
                    nc.vector.tensor_copy(g_hi[:, s % 2], gated[:, s % 2]).then_inc(gated_ready, 1)
                    vec.wait_ge(gated_ready, 3 * n + (3 * s + 2))
                    nc.vector.tensor_tensor(g_lo[:, s % 2], gated[:, s % 2], g_hi[:, s % 2],
                                            ALU.subtract).then_inc(gated_ready, 1)
                    if not (last and s >= 2):
                        lo_u(lap, (s + 2) % RING, (s + 2) // RING)
                    if not (last and s >= 3):
                        lo_v(lap, (s + 1) % RING, (s + 1) // RING)

                lo_u(0, 0, 0)
                lo_u(0, 1, 0)
                lo_v(0, 0, 0)
                with vec.Fori(0, N_EXP // RING - 1) as lap:
                    for s in range(RING):
                        expert_step(lap, s, False)
                for s in range(RING):
                    expert_step(N_EXP // RING - 1, s, True)

                vec.wait_ge(experts_done, layer + 1)
                for b in range(4):
                    ins = nc.vector.tensor_copy(h[:, b // 2, b % 2 * 512:(b % 2 + 1) * 512], psum[b][:])
                ins.then_inc(h_ready, 1)

        @block.tensor
        def _(pe):
            pe.sem_inc(tile_used, RING)
            pe.sem_inc(v_used, RING)
            pe.sem_inc(gates_filled, 2)
            pe.wait_ge(rel_loaded, 48)
            nc.tensor.matmul(psum[0][0:16, :], relb_sb[0:32, :], one_hot_b[0:32, :], start=True,
                             stop=True).then_inc(rel_product, 1)
            pe.wait_ge(consts_loaded, 48)

            def turn(layer, k, srcs, rows=P):
                if k % 8 or k == BL_A:
                    pass
                if k not in (BL_H1, BL_H1 + 1):
                    pe.wait_ge(block_ready, layer * N_BLOCK + (k - 1))
                for t, src in enumerate(srcs):
                    ins = nc.tensor.transpose(psum[5 + k % 2][0:rows, t * P:(t + 1) * P], src, ident[:])
                ins.then_inc(turned, 1)

            def tile_there(layer, j):
                pe.wait_ge(loaded[j % RING], layer * (16 * N_TILES // RING) + 16 * (j // RING + 1))

            def bank_free(layer, j):
                if j < 2:
                    return
                k = j - 2
                if k < J_MERGE:
                    pe.wait_ge(job_out, layer * N_JOB_ACT + (k + 1))
                elif k < J_WQ:
                    pe.wait_ge(job_sum, layer * N_JOB_VEC + (k - J_MERGE + 1))
                else:
                    pe.wait_ge(job_out, layer * N_JOB_ACT + (J_MERGE + k - J_WQ + 1))

            def rows_job(layer, j, stile, width, x_rows, w, chunks, halves=TT):
                tile_there(layer, stile)
                bank_free(layer, j)
                for t in range(TT):
                    for c in range(chunks):
                        ins = nc.tensor.matmul(psum[j % 2][:, t * width:(t + 1) * width], x_rows(c, t), w(c),
                                               start=(c == 0), stop=(c == chunks - 1))
                return ins

            def cols_job(layer, j, stile, w, x_cols, chunks):
                tile_there(layer, stile)
                bank_free(layer, j)
                for i in range(2):
                    for c in range(chunks):
                        ins = nc.tensor.matmul(psum[j % 2][:, i * SEQ:(i + 1) * SEQ], w(c, i), x_cols(c),
                                               start=(c == 0), stop=(c == chunks - 1))
                return ins

            def used_and_ready(layer, j, ins):
                ins.then_inc(job_ready, 1)
                pe.wait_ge(job_ready, layer * N_JOB + (j + 1))
                pe.sem_inc(tile_used, 1)

            def x_rows(c, t):
                return x_t[:, c, t * P:(t + 1) * P]

            def wide(stile, width=256):
                return lambda c: tile[:, stile % RING, c * width:(c + 1) * width]

            def gate_job(layer, j, n):
                stile = T_GATE_A + n if n < 2 else T_GATE_B + n - 2
                w = tile[:, stile % RING, :].rearrange("p (c i m) -> p c i m", c=DC, i=2)
                ins = cols_job(layer, j, stile, lambda c, i: w[:, c, i], lambda c: x_t[:, c, :], DC)
                used_and_ready(layer, j, ins)

            def scores(layer, u):
                mixer, head = UNITS[u]
                if mixer == "a" and u >= 3:
                    pe.wait_ge(score_read, layer * N_UNIT + (u - 2))
                elif mixer == "b" or u in (8, 9, 10):
                    pe.wait_ge(score_read, layer * N_UNIT + min(u, 8))
                elif u > 10:
                    pe.wait_ge(score_read, layer * N_UNIT + (u - 2))
                for g in range(3 if mixer == "b" else 1):
                    if mixer in "ad":
                        first = QK_A if mixer == "a" else QK_D
                        q, k, rows = first + head % 2, first + 2, slice(64 * (head // 2), 64 * (head // 2) + 64)
                    elif mixer == "b":
                        q, k, rows = QK_B + 2 * g + head // 2, QK_B + 6 + 2 * g + head // 2, \
                            slice(64 * (head % 2), 64 * (head % 2) + 64)
                    else:
                        q, k, rows = QK_C + head, QK_C + 4 + head, slice(0, C_QK)
                    bank = 2 + g if mixer == "b" else 2 + u % 3
                    for t in range(TT):
                        ins = nc.tensor.matmul(psum[bank][:, t * SEQ:(t + 1) * SEQ],
                                               qk_t[rows, q, t * P:(t + 1) * P], qk_t[rows, k, :],
                                               start=True, stop=True)
                ins.then_inc(scored, 1)

            def values(u, chunk):
                mixer, head = UNITS[u]
                g, t = chunk // 2, chunk % 2
                if mixer == "a":
                    return proj[:, t, AV + head // 2 * DH:AV + (head // 2 + 1) * DH]
                if mixer == "b":
                    at = BV + (g * 4 + head) * DH
                    return proj[:, t, at:at + DH]
                if mixer == "d":
                    return proj[:, t, DV + head // 2 * DH:DV + (head // 2 + 1) * DH]
                at = 384 + head * 128 + C_NOPE
                return c_out[:, t, at:at + DH]

            def mix_values(layer, u):
                pe.wait_ge(prob_ready, layer * N_UNIT + (u + 1))
                for i in range(PT_JOBS[u]):
                    k = PT_BEFORE[u] + i
                    if k >= 2:
                        pe.wait_ge(pt_out, layer * N_PT + (k - 1))
                    for c in range(2):
                        for t in range(TT):
                            at = (2 * i + c) * P
                            ins = nc.tensor.transpose(psum[5 + k % 2][:, c * SEQ + t * P:c * SEQ + (t + 1) * P],
                                                      prob[:, u % 2, t, at:at + P], ident[:])
                    ins.then_inc(pt_ready, 1)
                if u % 2 == 0 and u:
                    pe.wait_ge(mixed_out, layer * (N_UNIT // 2) + u // 2)
                pe.wait_ge(pt_out, layer * N_PT + PT_BEFORE[u + 1])
                n = 2 * PT_JOBS[u]
                rows = slice(64 * (u % 2), 64 * (u % 2) + 64)
                for c in range(n):
                    ins = nc.tensor.matmul(psum[7][rows, 0:SEQ], values(u, c), prob_t[:, u % 2, c, :],
                                           start=(c == 0), stop=(c == n - 1))
                ins.then_inc(mixed, 1)

            def split_product(dst, hi_hi, hi_lo, lo_hi, start, stop):
                nc.tensor.matmul(dst, *hi_hi, start=start, stop=False, skip_group_check=True)
                nc.tensor.matmul(dst, *hi_lo, start=False, stop=False, skip_group_check=True)
                return nc.tensor.matmul(dst, *lo_hi, start=False, stop=stop, skip_group_check=True)

            def expert_up(layer, lap, s):
                pe.wait_ge(u_lo_ready, layer * N_EXP + lap * RING + (s + 1))
                hi = u_hi[:, s % 2]
                lo = stream_lo[:, s, 0:1024].rearrange("p (c e) -> p c e", c=DC)
                for c in range(DC):
                    ins = split_product(psum[4 + s % 2][:, 0:SEQ], (hi[:, c], x_hi[:, c]), (hi[:, c], x_lo[:, c]),
                                        (lo[:, c], x_hi[:, c]), c == 0, c == DC - 1)
                ins.then_inc(tile_used, 1)

            def expert_down(layer, lap, s, stop=False):
                pe.wait_ge(v_lo_ready, layer * N_EXP + lap * RING + (s + 1))
                pe.wait_ge(gated_ready, layer * (3 * N_EXP) + lap * (3 * RING) + (3 * s + 3))
                for t in range(TT):
                    a_hi, a_lo = (a[:, s % 2, t * P:(t + 1) * P] for a in (g_hi, g_lo))
                    for half in range(2):
                        v = slice(1024 + half * 512, 1024 + (half + 1) * 512)
                        vh, vl = v_hi[:, s % 2, half * 512:(half + 1) * 512], stream_lo[:, s, v]
                        ins = split_product(psum[2 * t + half][:], (a_hi, vh), (a_hi, vl), (a_lo, vh),
                                            False, stop)
                ins.then_inc(v_used, 1)

            with pe.Fori(0, LAYERS) as layer:
                pe.wait_ge(hn_ready, layer * 4 + 2)
                for c in range(DC):
                    turn(layer, BL_H1 + c, [hn[:, t, c * P:(c + 1) * P] for t in range(TT)])
                pe.wait_ge(block_ready, layer * N_BLOCK + 8)
                for j in range(N_PROJ):
                    ins = rows_job(layer, j, T_PROJ + j, PROJ_W, x_rows, wide(T_PROJ + j, PROJ_W), DC)
                    used_and_ready(layer, j, ins)

                def proj_blocks(first, cols, n, ready):
                    pe.wait_ge(normed, layer * N_NORMED + ready)
                    for i in range(n):
                        turn(layer, first + i,
                             [proj[:, t, cols + i * P:cols + (i + 1) * P] for t in range(TT)])

                proj_blocks(BL_A, AQ, 3, 1)
                proj_blocks(BL_B, BQ, 12, 2)
                proj_blocks(BL_LAT, CQ, 3, 3)
                for n in range(2):
                    gate_job(layer, J_GATE_A + n, n)
                pe.wait_ge(block_ready, layer * N_BLOCK + BL_D)
                for i in range(4):
                    j, stile = J_C + i, T_CW + i // 2
                    t = i % 2
                    tile_there(layer, stile)
                    bank_free(layer, j)
                    if i < 2:
                        for c in range(2):
                            ins = nc.tensor.matmul(psum[j % 2][:, 0:384], lat_t[:, c, t * P:(t + 1) * P],
                                                   tile[:, stile % RING, c * 384:(c + 1) * 384],
                                                   start=(c == 0), stop=(c == 1))
                    else:
                        ins = nc.tensor.matmul(psum[j % 2][:], lat_t[:, 2, t * P:(t + 1) * P],
                                               tile[:, stile % RING, 0:512], start=True, stop=True)
                    if t == 1:
                        used_and_ready(layer, j, ins)
                    else:
                        ins.then_inc(job_ready, 1)
                for n in range(2, 8):
                    gate_job(layer, J_GATE_B + n - 2, n)
                proj_blocks(BL_D, DQ, 3, 4)
                pe.wait_ge(normed, layer * N_NORMED + 5)
                for i in range(8):
                    turn(layer, BL_C + i, [cat[:, t, i, :] for t in range(TT)], rows=C_QK)
                pe.wait_ge(block_ready, layer * N_BLOCK + BL_H2)
                for u in range(N_UNIT + 1):
                    for n in range(*GATE_BATCH.get(u, (0, 0))):
                        gate_job(layer, J_GATE_B + n - 2, n)
                    if u < N_UNIT:
                        scores(layer, u)
                    if u:
                        mix_values(layer, u - 1)

                pe.wait_ge(mixed_out, layer * (N_UNIT // 2) + N_UNIT // 2)
                for n in range(4):
                    stile = T_BRANCH + n
                    w = tile[:, stile % RING, :].rearrange("p (c m) -> p c m", c=2)
                    for pair in range(4):
                        j = J_MERGE + 4 * n + pair
                        ins = cols_job(layer, j, stile, lambda c, i: w[:, c, (2 * pair + i) * P:(2 * pair + i + 1) * P],
                                       lambda c: y_t[:, 2 * n + c, :], 2)
                        if pair == 3:
                            used_and_ready(layer, j, ins)
                        else:
                            ins.then_inc(job_ready, 1)
                pe.wait_ge(merged_ready, layer + 1)
                for j in range(4):
                    ins = rows_job(layer, J_OUT + j, T_OUT + j, 256, lambda c, t: merged[:, c, t * P:(t + 1) * P],
                                   wide(T_OUT + j), DC)
                    used_and_ready(layer, J_OUT + j, ins)

                pe.wait_ge(hn_ready, layer * 4 + 4)
                for c in range(DC):
                    turn(layer, BL_H2 + c, [hn[:, t, c * P:(c + 1) * P] for t in range(TT)])
                pe.wait_ge(block_ready, layer * N_BLOCK + N_BLOCK)
                for n in range(4):
                    j = J_WQ + n
                    w = tile[:, (T_WQ + n) % RING, :].rearrange("p (c i m) -> p c i m", c=DC, i=2)
                    ins = cols_job(layer, j, T_WQ + n, lambda c, i: w[:, c, i], lambda c: x_t[:, c, :], DC)
                    used_and_ready(layer, j, ins)
                pe.wait_ge(job_out, layer * N_JOB_ACT + N_JOB_ACT)
                for n in range(2):
                    stile = T_KEYS + n
                    tile_there(layer, stile)
                    w = tile[:, stile % RING, 0:512].rearrange("p (h k) -> p h k", h=4)
                    for t in range(TT):
                        for i in range(4):
                            head = 4 * n + i
                            for half in range(2):
                                rows = slice(64 * half, 64 * half + 64)
                                bank = (4, 0)[t] + 2 * half + head // 4
                                ins = nc.tensor.matmul(psum[bank][:, i * KEYS:(i + 1) * KEYS],
                                                       q_t[rows, head, t * P:(t + 1) * P], w[rows, i, :],
                                                       start=True, stop=True)
                    ins.then_inc(tile_used, 1)
                pe.wait_ge(tile_used, layer * N_TILES + (N_PRE + RING))
                pe.sem_inc(peer_scored, 1)

                pe.wait_ge(chosen, layer * TT + TT)
                for i in range(3):
                    for t in range(TT):
                        ins = nc.tensor.transpose(psum[4 + i][:, t * P:(t + 1) * P], sel[:, i, t], ident[:])
                ins.then_inc(chosen_turned, 1)

                with pe.Fori(0, N_GROUP // 2) as pair:
                    for b in range(2):
                        pe.wait_ge(hot_ready, layer * N_GROUP + pair * 2 + (b + 1))
                        pe.wait_ge(gates_out, layer * N_GROUP + pair * 2 + (b + 1))
                        for i in range(GROUP):
                            ins = nc.tensor.matmul(psum[6 + b][:, i * P:(i + 1) * P], hot2[:, b, i], hot1[:, b, i],
                                                   start=True, stop=True)
                        ins.then_inc(gates_filled, 1)

                for t in range(TT):
                    for half in range(2):
                        nc.tensor.matmul(psum[2 * t + half][:], ident[:], h[:, t, half * 512:(half + 1) * 512],
                                         start=True, stop=False, skip_group_check=True)
                expert_up(layer, 0, 0)
                with pe.Fori(0, N_EXP // RING - 1) as lap:
                    for s in range(RING):
                        expert_up(layer, lap + (s + 1) // RING, (s + 1) % RING)
                        expert_down(layer, lap, s)
                for s in range(RING):
                    if s < RING - 1:
                        expert_up(layer, N_EXP // RING - 1, s + 1)
                    expert_down(layer, N_EXP // RING - 1, s, s == RING - 1)
                pe.wait_ge(v_used, layer * N_EXP + (N_EXP + RING))
                pe.sem_inc(experts_done, 1)


def distance_buckets():
    rel = np.arange(-255, 257)
    n = np.abs(rel)
    nf = np.maximum(n, 1).astype(np.float32)
    large = 8 + (np.log(nf / np.float32(8)) / np.float32(math.log(1024 / 8)) * np.float32(8)).astype(np.int32)
    return np.where(rel > 0, 16, 0) + np.where(n < 8, n, np.minimum(large, 15)), rel


def shape_constants():
    bucket, rel = distance_buckets()
    onehot = np.zeros((33, 512), np.float32)
    onehot[bucket, np.arange(512)] = 1.0
    mask = np.zeros((16, 512), np.float32)
    mask[0:4, np.abs(rel) > 128] = NEG
    for g, dil in enumerate((1, 4, 16)):
        mask[4 + 4 * g:8 + 4 * g, (rel % dil != 0) | (np.abs(rel) > 64 * dil)] = NEG
    pos = np.arange(SEQ)
    freqs = (np.float32(10000.0) ** (-np.arange(16, dtype=np.float32) / np.float32(16))).astype(np.float32)
    rope = np.zeros((P, TT, 3, 2, 16), np.float32)
    for i, at in enumerate((pos, pos // 64, pos % 64)):
        ang = at.astype(np.float32)[:, None] * freqs[None, :]
        rope[:, :, i, 0] = np.cos(ang).reshape(TT, P, 16).transpose(1, 0, 2)
        rope[:, :, i, 1] = np.sin(ang).reshape(TT, P, 16).transpose(1, 0, 2)
    iota = np.broadcast_to(np.arange(P, dtype=np.float32), (P, P))
    return {"ident": np.eye(P, dtype=np.float32), "iota": np.ascontiguousarray(iota), "rope": rope,
            "onehot": onehot, "mask": mask}


def tiles_of(w, n):
    layers, rows, cols = w.shape
    t = w.reshape(layers, rows // P, P, n, cols // n).transpose(0, 3, 2, 1, 4)
    return np.ascontiguousarray(t).reshape(layers, n, P, -1)


def laid_out(i):
    w_in = i["w_in"]
    order = [h * DH + c for h in HEAD_ORDER for c in range(DH)]
    cols = np.arange(MIX)
    cols[AQ:AQ + 256] = AQ + np.array(order)
    cols[DQ:DQ + 256] = DQ + np.array(order)
    per = lambda a: a.reshape(LAYERS, -1, P).transpose(0, 2, 1)
    twice = lambda a: np.concatenate([a, a], axis=1)[:, :, None]
    gcols = np.concatenate(
        [per(i["norm1_gain"]), per(i["norm2_gain"]), per(i["gate_bias"]), twice(i["a_q_gain"]),
         twice(i["a_k_gain"])] + [twice(i["b_q_gain"][:, g]) for g in range(3)]
        + [twice(i["b_k_gain"][:, g]) for g in range(3)] + [per(i["c_q_lat_gain"]), per(i["c_kv_lat_gain"])],
        axis=2)
    grows = np.concatenate([i["c_q_gain"], i["c_k_gain"], i["d_q_gain"], i["d_k_gain"], i["a_sink"]], axis=1)
    relb = np.zeros((33, 16), np.float32)
    relb[0:32] = i["rel_bias"]
    keys = i["peer_sub_keys"].transpose(0, 2, 4, 1, 3).reshape(LAYERS, P, 2, 4 * KEYS).transpose(0, 2, 1, 3)
    w_u = i["peer_w_u"].reshape(LAYERS, N_EXP, P, DC, P).transpose(0, 1, 4, 3, 2)
    branch = i["w_branch"].reshape(LAYERS, 4, 2, P, DM).transpose(0, 1, 3, 2, 4)
    return {
        "x": i["x"].reshape(SEQ, DM), "relb": relb,
        "w_proj": tiles_of(w_in[:, :, cols], N_PROJ), "w_gate": tiles_of(w_in[:, :, MIX:], N_GATE),
        "w_cq": tiles_of(i["c_w_uq"], 1), "w_ckv": tiles_of(i["c_w_ukv"], 1),
        "w_branch": branch.reshape(LAYERS, 4, P, 2048), "w_out": tiles_of(i["w_out"], 4),
        "w_q": tiles_of(i["peer_w_q"], 4), "keys": keys,
        "w_u": w_u.reshape(LAYERS, N_EXP, P, 1024), "w_v": i["peer_w_v"].reshape(LAYERS, N_EXP, P, DM),
        "gcols": gcols, "grows": grows[:, None, :],
    } | shape_constants()


ORDER = ["x", "relb", "w_proj", "w_gate", "w_cq", "w_ckv", "w_branch", "w_out", "w_q", "keys", "w_u", "w_v",
         "gcols", "grows", "ident", "iota", "rope", "onehot", "mask"]


def kernel(**inputs):
    import concourse.bacc as bacc
    from concourse.bass_utils import run_bass_kernel_spmd

    placed = laid_out({k: np.asarray(v) for k, v in inputs.items()})
    arrays = {f"in_{n}": np.ascontiguousarray(placed[n]) for n in ORDER}
    nc = bacc.Bacc("TRN2", target_bir_lowering=False, num_devices=1)
    args = [nc.dram_tensor(f"in_{n}", arrays[f"in_{n}"].shape, F32, kind="ExternalInput").ap() for n in ORDER]
    out = nc.dram_tensor("out_0", (SEQ, DM), F32, kind="ExternalOutput").ap()
    trunk(nc, *args, out)
    r = run_bass_kernel_spmd(nc, [arrays], core_ids=[0])
    return r.results[0]["out_0"].reshape(1, SEQ, DM)
```

```python
import math
from contextlib import ExitStack

import numpy as np

import concourse.bass as bass
from concourse import mybir

F32 = mybir.dt.float32
F32R = mybir.dt.float32r
U32 = mybir.dt.uint32
I32 = mybir.dt.int32
ALU = mybir.AluOpType
ACT = mybir.ActivationFunctionType
AX_X = mybir.AxisListType.X
AX_XY = mybir.AxisListType.XY

P = 128
LAYERS = 2
SEQ = 256
TT = SEQ // P
DM = 1024
DC = DM // P
EPS = 1e-6
NEG = -1e30
DH = 64

AQ, AK, AV = 0, 256, 384
BQ, BK, BV = 512, 1280, 2048
CQ, CKV, CKR = 2816, 3072, 3200
DQ, DK, DV = 3232, 3488, 3616
MIX = 3744
C_HEADS, C_NOPE, C_ROPE, C_QK = 4, 64, 32, 96
HEAD_ORDER = (0, 2, 1, 3)

RING = 4
N_PROJ = 16
PROJ_W = MIX // N_PROJ
N_GATE = 16
T_PROJ = 0
T_GATE_A = T_PROJ + N_PROJ
T_CW = T_GATE_A + 2
T_GATE_B = T_CW + 2
T_BRANCH = T_GATE_B + N_GATE - 2
T_OUT = T_BRANCH + 4
T_WQ = T_OUT + 4
T_KEYS = T_WQ + 4
N_PRE = T_KEYS + 2
N_EXP = 128
N_KEYS = 2
N_USED = N_KEYS + N_EXP
assert N_PRE % RING == 0 and N_EXP % RING == 0

BL_H1, BL_A, BL_B, BL_LAT, BL_D, BL_C, BL_H2 = 0, 8, 11, 23, 26, 29, 37
N_BLOCK = 45
QK_A, QK_B, QK_D, QK_C = 0, 3, 15, 18

UNITS = [("a", h) for h in range(4)] + [("b", h) for h in range(4)] \
    + [("d", h) for h in range(4)] + [("c", h) for h in range(4)]
N_UNIT = 16
PT_JOBS = [3 if m == "b" else 1 for m, _ in UNITS]
PT_BEFORE = [sum(PT_JOBS[:u]) for u in range(N_UNIT + 1)]
N_PT = PT_BEFORE[N_UNIT]
BRANCH_OF = {"a": 0, "b": 1, "c": 2, "d": 3}
STEP_C = 1
STEP_TURN_D = 3
STEP_NORM_C = 8
STEP_ROPE_C = 9
STEP_TURN_C = 11

J_PROJ, J_GATE_A, J_C, J_GATE_B, J_MERGE, J_OUT, J_WQ = 0, 16, 18, 22, 36, 52, 56
N_JOB = 60
LAST_JOB = [J_PROJ + j for j in range(N_PROJ)] + [J_GATE_A, J_GATE_A + 1, J_C + 1, J_C + 3] \
    + [J_GATE_B + j for j in range(N_GATE - 2)] + [J_MERGE + 4 * n + 3 for n in range(4)] \
    + [J_OUT + j for j in range(4)] + [J_WQ + n for n in range(4)]
N_JOB_ACT = 40
N_JOB_VEC = 20

ST_H1, ST_A, ST_B, ST_LAT, ST_D, ST_C, ST_H2 = 0, 2, 14, 62, 68, 80, 104
N_STAT = 106
N_RMS = 7
N_SQ = 10

GC_N1, GC_N2, GC_GB, GC_AQ, GC_AK, GC_BQ, GC_BK, GC_CQL, GC_CKL = 0, 8, 16, 48, 49, 50, 53, 56, 58
N_GC = 59
GR_CQ, GR_CK, GR_DQ, GR_DK, GR_SINK = 0, 96, 192, 256, 320
N_GR = 324

HEADS, TOPK, KEYS = 8, 16, 128
CAND_ROWS = [(0, 1, 16), (1, 1, 8), (2, 1, 5), (3, 1, 4), (4, 1, 3), (5, 3, 2), (8, 8, 1)]
N_CAND = sum(n * w for _, n, w in CAND_ROWS)
DEAD = -3.0e38
GROUP = 4
N_GROUP = SEQ // GROUP
N_FREE = 40
N_PAIR = N_GROUP // 2
EXP_LAP = 2
AHEAD = N_FREE + N_PAIR
N_BOTH = N_EXP - AHEAD
ONES_LAP = 2
DEEP = 2 * RING
assert N_FREE % DEEP == 0 and N_PAIR % DEEP == 0 and N_BOTH % RING == 0
U_LOADS = N_PRE // RING + AHEAD // DEEP + N_BOTH // RING
V_LOADS = AHEAD // DEEP + N_EXP // RING

VEC_ORDER = 116
N_NORMED = 5


def trunk(nc, x, relb, w_proj, w_gate, w_cq, w_ckv, w_branch, w_out, w_q, keys, w_u, w_v,
          gcols, grows, ident_d, iota_d, rope_d, onehot_d, mask_d, out):
    ctx = ExitStack()
    with ctx:
        base = (nc.sbuf_base + 31) // 32 * 32
        top = nc.sbuf_usable_end // 32 * 32
        taken = {}

        def place(name, shape, dt, at):
            size = 4 * int(np.prod(shape[1:]))
            assert at + size <= top, (name, at, size, top)
            taken[name] = (at, size)
            return nc.alloc_sbuf_tensor_at(name, shape, dt, offset=at)

        class Region:
            def __init__(self, at):
                self.at = at

            def put(self, name, shape, dt=F32):
                t = place(name, shape, dt, self.at)
                self.at += (4 * int(np.prod(shape[1:])) + 31) // 32 * 32
                return t

        lasting = Region(base)
        ident = lasting.put("ident", [P, P])
        iota = lasting.put("iota", [P, P])
        rope_t = lasting.put("rope_t", [P, TT, 3, 2, 16])
        gcol = lasting.put("gcol", [P, N_GC])
        grow_at = lasting.at
        grow = lasting.put("grow", [P, N_GR])
        act_out = [lasting.put("act_out0", [P, SEQ]), place("act_out1", [P, SEQ], F32, grow_at)]
        half_neg = lasting.put("half_neg", [P, 64])
        gate_t = lasting.put("gate_t", [P, SEQ])
        i12_t = lasting.put("i12_t", [P, 2, SEQ])
        stream_at = lasting.at
        tile = lasting.put("stream_tile", [P, RING, 2048])
        stream_lo = place("stream_lo", [P, RING, 2048], F32R, stream_at)
        hi_at = lasting.at
        u_hi = lasting.put("u_hi", [P, RING, DC, P], F32R)
        v_hi = place("v_hi", [P, 2, DM], F32R, hi_at + 8192)
        x_hi = lasting.put("x_hi", [P, DC, SEQ], F32R)
        x_lo = lasting.put("x_lo", [P, DC, SEQ], F32R)
        gates_low = place("gates_low", [P, 16, SEQ], F32, hi_at)
        hots = place("hots", [P, 2, 2, GROUP, P], F32, hi_at + 8192)
        h_at = lasting.at
        h = lasting.put("h", [P, TT, DM])
        g_hi = place("g_hi", [P, 2, SEQ], F32R, h_at)
        g_lo = place("g_lo", [P, 2, SEQ], F32R, h_at + 2048)
        union = lasting.at

        mix = Region(union)
        proj_at = mix.at
        proj = mix.put("proj", [P, TT, MIX])
        gates_high = [place(f"gates_high{t}", [P, 8, SEQ], F32, proj_at + 4 * (t * MIX + BQ)) for t in range(TT)]
        bias_t = mix.put("bias_t", [P, 2, 3, 384])
        qk_at = mix.at
        qk_t = mix.put("qk_t", [P, 26, SEQ])
        s_at = mix.at
        prob = mix.put("prob", [P, 2, TT, 772])
        pt_at = mix.at
        prob_t = mix.put("prob_t", [P, 2, 6, SEQ])
        y_at = mix.at
        y_t = mix.put("y_t", [P, 8, SEQ])
        x_at = mix.at
        x_t = mix.put("x_t", [P, DC, SEQ])
        m_at = mix.at
        merged = mix.put("merged", [P, DC, SEQ])
        c_out = mix.put("c_out", [P, TT, 896])
        cat_at = mix.at
        cat = mix.put("cat", [P, TT, 8, C_QK])
        stat_at = mix.at
        stat = mix.put("stat", [P, N_STAT])
        rstd = mix.put("rstd", [P, N_STAT])
        unit_m = mix.put("unit_m", [P, 2, TT])
        unit_n = mix.put("unit_n", [P, 2, TT])
        unit_d = mix.put("unit_d", [P, 2, TT])
        unit_r = mix.put("unit_r", [P, 2, TT])
        r_sb = mix.put("r_sb", [16, 128])
        w_hi = [place(f"w_hi{i}", [P, DC * PROJ_W], F32R, at)
                for i, at in enumerate((hi_at, hi_at + 8192, m_at))]
        gw_hi = [place(f"gw_hi{i}", [P, 2048], F32R, at) for i, at in enumerate((x_at, m_at))]
        hn = place("hn", [P, TT, DM], F32, qk_at)
        junk = place("junk", [P, TT, DM], F32, s_at)
        sq_b = place("sq_b", [P, TT, 1536], F32, s_at)
        sq_c = place("sq_c", [P, TT, 640], F32, proj_at + 4 * BQ)
        rot = place("rot", [P, 4, 192], F32, proj_at + 4 * (MIX + BQ))
        sq_a = place("sq_a", [P, TT, 384], F32, pt_at + 8192)
        sq_d = place("sq_d", [P, TT, 384], F32, pt_at + 2048)
        lat_t = place("lat_t", [P, 3, SEQ], F32, pt_at + 8192)
        sq_l = place("sq_l", [P, TT, 416], F32, cat_at)
        prod = place("prod", [P, 2, 512], F32, s_at)
        one_hot_b = place("one_hot_b", [33, 512], F32, y_at)
        relb_sb = place("relb_sb", [33, 16], F32, y_at + 2048)
        mask_sb = place("mask_sb", [16, 512], F32, y_at + 4096)
        rel_sb = place("rel_sb", [16, 512], F32, y_at + 6144)

        q_t = place("q_t", [P, HEADS, SEQ], F32, y_at)
        peer = Region(union + AHEAD * SEQ * 4)
        score_sb = peer.put("score_sb", [P, 4, 512])
        left = peer.put("left", [P, 2 * HEADS, KEYS])
        top_v = peer.put("top_v", [P, 2 * HEADS, TOPK])
        top_i = peer.put("top_i", [P, 2 * HEADS, TOPK], U32)
        top_f = peer.put("top_f", [P, 2 * HEADS, TOPK])
        cand = peer.put("cand", [P, HEADS, N_CAND])
        cand_i = peer.put("cand_i", [P, HEADS, N_CAND])
        cand_left = peer.put("cand_left", [P, HEADS, N_CAND])
        best = peer.put("best", [P, HEADS, TOPK])
        best_p = peer.put("best_p", [P, HEADS, TOPK], U32)
        best_f = peer.put("best_f", [P, HEADS, TOPK])
        shifted = peer.put("shifted", [P, HEADS, TOPK])
        expd = peer.put("expd", [P, HEADS, TOPK])
        esum = peer.put("esum", [P, HEADS])
        erec = peer.put("erec", [P, HEADS])
        idx_f = peer.put("idx_f", [P, HEADS, TOPK])
        idx_i = peer.put("idx_i", [P, HEADS, TOPK], I32)
        idx_1 = peer.put("idx_1", [P, HEADS, TOPK], I32)
        idx_2 = peer.put("idx_2", [P, HEADS, TOPK], I32)
        sel = peer.put("sel", [P, 3, TT, P])
        match = peer.put("match", [P, HEADS // 2, TOPK, N_CAND])
        assert peer.at <= stat_at

        gate_all = place("gate_all", [P, N_EXP, SEQ], F32, union)

        psum = [ctx.enter_context(nc.psum_tensor(f"bank{b}", [P, 512], F32)) for b in range(8)]
        rel_dram = nc.dram_tensor("rel_by_distance", (16, P, 512), F32).ap()

        def half_tile(buf, s):
            return buf[:, s % RING, s // RING * 1024:(s // RING + 1) * 1024]

        def half_there(eng, layer, lap, s):
            if s < RING:
                eng.wait_ge(loaded[s], layer * (16 * U_LOADS) + lap * 16 + 16 * (N_PRE // RING + 1))
            else:
                eng.wait_ge(v_loaded[s - RING], layer * (16 * V_LOADS) + lap * 16 + 16)

        def gate_chunks(c, n):
            if c < 16:
                return gates_low[:, c:c + n, :]
            return gates_high[(c - 16) // 8][:, c % 8:c % 8 + n, :]

        def gate_tile(n):
            return T_GATE_A + n if n < 2 else T_GATE_B + n - 2

        def sem(name):
            return ctx.enter_context(nc.semaphore(name))

        consts_loaded = sem("consts_loaded")
        x_loaded = sem("x_loaded")
        rel_loaded = sem("rel_loaded")
        half_set = sem("half_set")
        act_passed = sem("act_passed")
        vec_passed = sem("vec_passed")
        pool_passed = sem("pool_passed")
        pe_passed = sem("pe_passed")
        rel_product = sem("rel_product")
        rel_ready = sem("rel_ready")
        rel_stored = sem("rel_stored")
        h_ready = sem("h_ready")
        gains_loaded = sem("gains_loaded")
        bias_loaded = [sem(f"bias_loaded{i}") for i in range(2)]
        loaded = [sem(f"loaded{i}") for i in range(RING)]
        v_loaded = [sem(f"v_loaded{i}") for i in range(RING)]
        half_loaded = loaded + v_loaded
        tile_used = sem("tile_used")
        v_used = sem("v_used")
        squared = sem("squared")
        mean_ready = sem("mean_ready")
        rstd_ready = sem("rstd_ready")
        hn_ready = sem("hn_ready")
        turned = sem("turned")
        block_ready = sem("block_ready")
        job_ready = sem("job_ready")
        job_out = sem("job_out")
        job_sum = sem("job_sum")
        normed = sem("normed")
        scored = sem("scored")
        score_read = sem("score_read")
        max_ready = sem("max_ready")
        exped = sem("exped")
        prob_ready = sem("prob_ready")
        pt_ready = sem("pt_ready")
        pt_out = sem("pt_out")
        mixed = sem("mixed")
        mixed_out = sem("mixed_out")
        gate_ready = sem("gate_ready")
        merged_ready = sem("merged_ready")
        h2_ready = sem("h2_ready")
        w_hi_ready = sem("w_hi_ready")
        w_lo_ready = sem("w_lo_ready")
        gw_hi_ready = sem("gw_hi_ready")
        gw_lo_ready = sem("gw_lo_ready")
        chunk_split = sem("chunk_split")
        x_split = sem("x_split")
        peer_scored = sem("peer_scored")
        gate_exp = sem("gate_exp")
        gate_shift = sem("gate_shift")
        chosen = sem("chosen")
        chosen_turned = sem("chosen_turned")
        chosen_out = sem("chosen_out")
        hot_ready = sem("hot_ready")
        hot_gated = sem("hot_gated")
        score_out = sem("score_out")
        ones_ready = sem("ones_ready")
        gates_filled = sem("gates_filled")
        gates_mult = sem("gates_mult")
        gates_out = sem("gates_out")
        u_hi_ready = sem("u_hi_ready")
        v_hi_ready = sem("v_hi_ready")
        u_lo_ready = sem("u_lo_ready")
        v_lo_ready = sem("v_lo_ready")
        act_ready = sem("act_ready")
        act_gated = sem("act_gated")
        residual_in = sem("residual_in")
        gated_ready = sem("gated_ready")
        experts_done = sem("experts_done")
        vec_order = sem("vec_order")
        stored = sem("stored")

        block = ctx.enter_context(nc.Block())

        @block.sync
        def _(sp):
            sp.dma_start(h[:], x.rearrange("(t p) d -> p t d", p=P)).then_inc(x_loaded, 16)
            pre = [(w_proj, j, DC * PROJ_W) for j in range(N_PROJ)]
            pre += [(w_gate, j, 2048) for j in range(2)]
            pre += [(w_cq, 0, 768), (w_ckv, 0, 512)]
            pre += [(w_gate, j, 2048) for j in range(2, N_GATE)]
            pre += [(w_branch, j, 2048) for j in range(4)]
            pre += [(w_out, j, 2048) for j in range(4)]
            pre += [(w_q, j, 2048) for j in range(4)]
            pre += [(keys, j, 512) for j in range(2)]
            assert len(pre) == N_PRE
            with sp.Fori(0, LAYERS) as layer:
                def pre_used(j):
                    if j < T_KEYS:
                        sp.wait_ge(job_ready, layer * N_JOB + (LAST_JOB[j] + 1))
                    else:
                        sp.wait_ge(tile_used, layer * N_USED + (RING + j - T_KEYS + 1))

                for j, (src, n, width) in enumerate(pre):
                    if j == 0:
                        sp.wait_ge(tile_used, layer * N_USED + RING)
                        sp.wait_ge(v_used, layer * N_EXP + RING)
                    if j >= RING:
                        pre_used(j - RING)
                    sp.dma_start(tile[:, j % RING, 0:width], src[layer, n]).then_inc(loaded[j % RING], 16)

                def load_ahead(lap, s):
                    sp.dma_start(half_tile(tile, s), w_u[layer, lap * DEEP + s]).then_inc(half_loaded[s], 16)

                def load_u(lap, s, used):
                    sp.wait_ge(tile_used, used)
                    sp.dma_start(tile[:, s, 0:1024], w_u[layer, lap * RING + s]).then_inc(loaded[s], 16)

                def load_v(lap, s):
                    sp.dma_start(tile[:, s, 1024:2048], w_v[layer, lap * RING + s]).then_inc(v_loaded[s], 16)

                experts_used = layer * N_USED + (N_KEYS + RING)
                for s in range(DEEP):
                    if s < RING:
                        pre_used(N_PRE - RING + s)
                    load_ahead(0, s)
                with sp.Fori(1, AHEAD // DEEP) as lap:
                    for s in range(DEEP):
                        sp.wait_ge(tile_used, experts_used + (lap - 1) * DEEP + (s + 1))
                        load_ahead(lap, s)
                for s in range(RING):
                    load_u(AHEAD // RING, s, experts_used + (AHEAD - DEEP + s + 1))
                for s in range(RING):
                    sp.wait_ge(tile_used, experts_used + (AHEAD - RING + s + 1))
                    load_v(0, s)
                with sp.Fori(1, N_BOTH // RING) as lap:
                    for s in range(RING):
                        load_u(lap + AHEAD // RING, s, experts_used + AHEAD + (lap - 1) * RING + (s + 1))
                        sp.wait_ge(v_used, layer * N_EXP + lap * RING + (s + 1))
                        load_v(lap, s)
                with sp.Fori(N_BOTH // RING, N_EXP // RING) as lap:
                    for s in range(RING):
                        sp.wait_ge(v_used, layer * N_EXP + lap * RING + (s + 1))
                        load_v(lap, s)
            sp.wait_ge(h_ready, LAYERS + 1)
            sp.dma_start(out.rearrange("(t p) d -> p t d", p=P), h[:]).then_inc(stored, 16)
            sp.wait_ge(stored, 16)

        @block.gpsimd
        def _(pool):
            nc.gpsimd.memset(half_neg[:], -0.5).then_inc(half_set, 1)
            pool.wait_ge(rel_ready, 1)
            pool.dma_start(rel_dram, rel_sb[:].unsqueeze(1).broadcast_to([16, P, 512])).then_inc(rel_stored, 16)
            pool.wait_ge(half_set, 1)

            def bias_load(layer, u):
                mixer, head = UNITS[u]
                if u >= 2:
                    pool.wait_ge(score_read, layer * N_UNIT + (u - 1))
                    pool.sem_inc(pool_passed, 1)
                if mixer == "a":
                    src = bass.AP(tensor=rel_dram.tensor, offset=head * P * 512 + 127, ap=[[511, P], [1, 384]])
                    dst = bias_t[:, u % 2, 0, :]
                else:
                    src = bass.AP(tensor=rel_dram.tensor, offset=(4 + head) * P * 512 + 127,
                                  ap=[[511, P], [4 * P * 512, 3], [1, 384]])
                    dst = bias_t[:, u % 2]
                pool.dma_start(dst, src).then_inc(bias_loaded[u % 2], 16)

            def rsqrt(layer, k, at, n):
                pool.wait_ge(mean_ready, layer * N_RMS + (k + 1))
                if n <= 64:
                    nc.gpsimd.tensor_tensor(rstd[:, at:at + n], stat[:, at:at + n], half_neg[:, 0:n],
                                            ALU.pow).then_inc(rstd_ready, 1)

            with pool.Fori(0, LAYERS) as layer:
                rsqrt(layer, 0, ST_H1, 2)
                pool.wait_ge(rel_stored, 16)
                bias_load(layer, 0)
                bias_load(layer, 1)
                for j in range(N_PROJ):
                    pool.wait_ge(w_hi_ready, layer * N_PROJ + (j + 1))
                    nc.gpsimd.tensor_tensor(stream_lo[:, j % RING, 0:DC * PROJ_W], tile[:, j % RING, 0:DC * PROJ_W],
                                            w_hi[j % 3][:], ALU.subtract).then_inc(w_lo_ready, 1)
                    if j == 5:
                        rsqrt(layer, 1, ST_A, 12)
                    if j == 13:
                        rsqrt(layer, 2, ST_B, 48)
                rsqrt(layer, 3, ST_LAT, 6)
                for u in range(N_UNIT):
                    if 2 <= u < 8:
                        bias_load(layer, u)
                    pool.wait_ge(gw_hi_ready, layer * N_GATE + (u + 1))
                    slot = gate_tile(u) % RING
                    nc.gpsimd.tensor_tensor(stream_lo[:, slot, :], tile[:, slot, :], gw_hi[u % 2][:],
                                            ALU.subtract).then_inc(gw_lo_ready, 1)
                    if u == 0:
                        rsqrt(layer, 4, ST_D, 12)
                    if u == 4:
                        rsqrt(layer, 5, ST_C, 24)
                rsqrt(layer, 6, ST_H2, 2)

                def lo_u(first, s, hi):
                    pool.wait_ge(u_hi_ready, layer * N_EXP + first + (s + 1))
                    nc.gpsimd.tensor_tensor(half_tile(stream_lo, s), half_tile(tile, s),
                                            hi.rearrange("p c e -> p (c e)"),
                                            ALU.subtract).then_inc(u_lo_ready, 1)

                with pool.Fori(0, ONES_LAP) as lap:
                    for s in range(DEEP):
                        lo_u(lap * DEEP, s, u_hi[:, s % RING])
                nc.gpsimd.memset(gate_all[:, N_FREE:AHEAD, :], 1.0).then_inc(ones_ready, 1)
                with pool.Fori(ONES_LAP, N_FREE // DEEP) as lap:
                    for s in range(DEEP):
                        lo_u(lap * DEEP, s, u_hi[:, s % RING])
                with pool.Fori(N_FREE // DEEP, AHEAD // DEEP) as lap:
                    for s in range(DEEP):
                        lo_u(lap * DEEP, s, u_hi[:, s % 2])
                with pool.Fori(AHEAD // RING, N_EXP // RING) as lap:
                    for s in range(RING):
                        lo_u(lap * RING, s, u_hi[:, s % 2])

        @block.scalar
        def _(act):
            act.sem_inc(gates_out, 4)
            act.sem_inc(act_ready, RING)
            act.dma_start(relb_sb[:], relb).then_inc(rel_loaded, 16)
            act.dma_start(one_hot_b[:], onehot_d).then_inc(rel_loaded, 16)
            act.dma_start(mask_sb[:], mask_d).then_inc(rel_loaded, 16)
            act.dma_start(ident[:], ident_d).then_inc(consts_loaded, 16)
            act.dma_start(iota[:], iota_d).then_inc(consts_loaded, 16)
            act.dma_start(rope_t[:], rope_d).then_inc(consts_loaded, 16)
            act.wait_ge(x_loaded, 16)

            def rms_rows(layer, at, n_before, hn_before, block0, gain0, src_ready, meanwhile=None):
                src_ready()
                for t in range(TT):
                    nc.scalar.activation(junk[:, t], h[:, t], ACT.Square,
                                         accum_out=stat[:, at + t:at + t + 1]).then_inc(squared, 1)
                if meanwhile:
                    meanwhile()
                act.wait_ge(rstd_ready, layer * N_RMS + (n_before + 1))
                for t in range(TT):
                    nc.scalar.activation(hn[:, t], h[:, t], ACT.Copy,
                                         scale=rstd[:, at + t:at + t + 1]).then_inc(hn_ready, 1)
                act.wait_ge(gains_loaded, layer * 32 + 32)
                for c in range(DC):
                    turn_out(layer, block0 + c, x_t[:, c, :], gcol[:, gain0 + c:gain0 + c + 1])

            def turn_out(layer, k, dst, gain=None, rows=P):
                act.wait_ge(turned, layer * N_BLOCK + (k + 1))
                scale = 1.0 if gain is None else gain
                nc.scalar.activation(dst, psum[5 + k % 2][0:rows, 0:SEQ], ACT.Copy,
                                     scale=scale).then_inc(block_ready, 1)

            def job_wait(layer, j):
                act.wait_ge(job_ready, layer * N_JOB + (j + 1))

            def gate_out(layer, j, tile_no):
                job_wait(layer, j)
                for i in range(2):
                    c = 2 * tile_no + i
                    ins = nc.scalar.activation(gate_chunks(c, 1).rearrange("p a t -> p (a t)"),
                                               psum[j % 2][:, i * SEQ:(i + 1) * SEQ],
                                               ACT.Identity, bias=gcol[:, GC_GB + c:GC_GB + c + 1])
                ins.then_inc(job_out, 1)

            def exp_rows(layer, u):
                mixer, _ = UNITS[u]
                act.wait_ge(max_ready, layer * N_UNIT + (u + 1))
                if mixer in "cd":
                    act.wait_ge(pt_ready, layer * N_PT + PT_BEFORE[u - 1])
                for t in range(TT):
                    if mixer == "a":
                        dst, src, scale = prob[:, u % 2, t, 0:257], prob[:, u % 2, t, 0:257], 1.0
                    elif mixer == "b":
                        dst, src, scale = prob[:, u % 2, t, 0:768], prob[:, u % 2, t, 0:768], 1.0
                    else:
                        scale = DH ** -0.5 if mixer == "d" else C_QK ** -0.5
                        dst = prob[:, u % 2, t, 0:SEQ]
                        src = psum[2 + u % 3][:, t * SEQ:(t + 1) * SEQ]
                    nc.scalar.activation(dst, src, ACT.Exp, bias=unit_m[:, u % 2, t:t + 1], scale=scale,
                                         accum_out=unit_d[:, u % 2, t:t + 1]).then_inc(exped, 1)
                if mixer in "cd":
                    act.wait_ge(exped, layer * (2 * N_UNIT) + (2 * u + 2))
                    act.sem_inc(score_read, 1)

            def turned_probs_out(layer, u):
                if u >= 2:
                    act.wait_ge(mixed, layer * N_UNIT + (u - 1))
                for i in range(PT_JOBS[u]):
                    k = PT_BEFORE[u] + i
                    act.wait_ge(pt_ready, layer * N_PT + (k + 1))
                    nc.scalar.activation(prob_t[:, u % 2, 2 * i:2 * i + 2, :],
                                         psum[5 + k % 2][:].rearrange("p (c q) -> p c q", c=2),
                                         ACT.Copy).then_inc(pt_out, 1)

            def mixed_pair_out(layer, u):
                if u % 2:
                    mixer, head = UNITS[u]
                    act.wait_ge(mixed, layer * N_UNIT + (u + 1))
                    nc.scalar.activation(y_t[:, 2 * BRANCH_OF[mixer] + head // 2, :], psum[7][:, 0:SEQ],
                                         ACT.Copy).then_inc(mixed_out, 1)

            with act.Fori(0, LAYERS) as layer:
                act.wait_ge(act_gated, layer * (N_EXP - N_FREE) + 2)
                act.sem_inc(act_passed, 1)
                act.dma_start(gcol[:], gcols[layer]).then_inc(gains_loaded, 16)
                act.dma_start(grow[:], grows[layer].partition_broadcast(P)).then_inc(gains_loaded, 16)

                def layer_start():
                    act.wait_ge(h_ready, layer + 1)

                def w_hi_part(j):
                    act.wait_ge(loaded[j % RING], layer * (16 * U_LOADS) + 16 * (j // RING + 1))
                    nc.scalar.activation(w_hi[j % 3][:], tile[:, j % RING, 0:DC * PROJ_W],
                                         ACT.Copy).then_inc(w_hi_ready, 1)

                def gw_hi_part(n):
                    j = gate_tile(n)
                    act.wait_ge(loaded[j % RING], layer * (16 * U_LOADS) + 16 * (j // RING + 1))
                    nc.scalar.activation(gw_hi[n % 2][:], tile[:, j % RING, :], ACT.Copy).then_inc(gw_hi_ready, 1)

                rms_rows(layer, ST_H1, 0, 0, BL_H1, GC_N1, layer_start, lambda: w_hi_part(0))
                w_hi_part(1)
                w_hi_part(2)
                for j in range(N_PROJ):
                    job_wait(layer, j)
                    nc.scalar.activation(proj[:, :, j * PROJ_W:(j + 1) * PROJ_W],
                                         psum[j % 2][:, 0:2 * PROJ_W].rearrange("p (t c) -> p t c", t=TT),
                                         ACT.Copy).then_inc(job_out, 1)
                    if j + 3 < N_PROJ:
                        w_hi_part(j + 3)
                    elif j < N_PROJ - 1:
                        gw_hi_part(j + 3 - N_PROJ)
                    if j == 1:
                        act.wait_ge(job_out, layer * N_JOB_ACT + 2)
                        nc.scalar.activation(sq_a[:], proj[:, :, AQ:AV], ACT.Square).then_inc(squared, 1)
                    if j == 8:
                        act.wait_ge(job_out, layer * N_JOB_ACT + 9)
                        nc.scalar.activation(sq_b[:], proj[:, :, BQ:BV], ACT.Square).then_inc(squared, 1)
                    if j == 13:
                        act.wait_ge(job_out, layer * N_JOB_ACT + 14)
                        nc.scalar.activation(sq_l[:], proj[:, :, CQ:DQ], ACT.Square).then_inc(squared, 1)
                act.wait_ge(job_out, layer * N_JOB_ACT + N_PROJ)
                nc.scalar.activation(sq_d[:], proj[:, :, DQ:DV], ACT.Square).then_inc(squared, 1)

                for i in range(3):
                    gain = GC_AK if i == 2 else GC_AQ
                    turn_out(layer, BL_A + i, qk_t[:, QK_A + i, :], gcol[:, gain:gain + 1])
                for i in range(12):
                    gain = (GC_BQ if i < 6 else GC_BK) + i % 6 // 2
                    turn_out(layer, BL_B + i, qk_t[:, QK_B + i, :], gcol[:, gain:gain + 1])
                for i in range(3):
                    turn_out(layer, BL_LAT + i, lat_t[:, i, :], gcol[:, GC_CQL + i:GC_CQL + i + 1])

                def second_c_out():
                    for i in range(4):
                        j = J_C + i
                        job_wait(layer, j)
                        dst = c_out[:, i % 2, 0:384] if i < 2 else c_out[:, i % 2, 384:896]
                        nc.scalar.activation(dst, psum[j % 2][:, 0:384 if i < 2 else 512],
                                             ACT.Copy).then_inc(job_out, 1)
                    act.wait_ge(job_out, layer * N_JOB_ACT + (J_C + 4))
                    nc.scalar.activation(sq_c[:, :, 0:384], c_out[:, :, 0:384], ACT.Square).then_inc(squared, 1)
                    for t in range(TT):
                        ins = nc.scalar.activation(
                            sq_c[:, t, 384:640].rearrange("p (h c) -> p h c", h=4),
                            c_out[:, t, 384:896].rearrange("p (h c) -> p h c", h=4)[:, :, 0:C_NOPE], ACT.Square)
                    ins.then_inc(squared, 1)

                for u in range(N_UNIT + 1):
                    if u == STEP_TURN_D:
                        for i in range(3):
                            turn_out(layer, BL_D + i, qk_t[:, QK_D + i, :])
                    if u == STEP_TURN_C:
                        for i in range(8):
                            turn_out(layer, BL_C + i, qk_t[0:C_QK, QK_C + i, :], rows=C_QK)
                    if u:
                        turned_probs_out(layer, u - 1)
                    if u < N_UNIT:
                        exp_rows(layer, u)
                        gate_out(layer, J_GATE_A + u if u < 2 else J_GATE_B + u - 2, u)
                    if u == STEP_C:
                        second_c_out()
                    if u:
                        mixed_pair_out(layer, u - 1)
                    if u + 2 < N_UNIT:
                        gw_hi_part(u + 2)

                act.wait_ge(job_out, layer * N_JOB_ACT + J_MERGE)
                for i in range(N_GATE):
                    pair = gate_chunks(2 * i, 2)
                    nc.scalar.activation(pair, pair, ACT.Sigmoid).then_inc(gate_ready, 1)

                def h2_there():
                    act.wait_ge(h2_ready, layer + 1)

                rms_rows(layer, ST_H2, 6, 2, BL_H2, GC_N2, h2_there)
                for i in range(4):
                    j = J_WQ + i
                    job_wait(layer, j)
                    nc.scalar.activation(q_t[:, 2 * i:2 * i + 2, :],
                                         psum[j % 2][:].rearrange("p (h t) -> p h t", h=2),
                                         ACT.Copy).then_inc(job_out, 1)

                def hi_part(dst, src, ready):
                    nc.scalar.activation(dst, src.rearrange("p (c e) -> p c e", c=DC), ACT.Copy).then_inc(ready, 1)

                def hi_ahead(lap, s, dst):
                    half_there(act, layer, lap, s)
                    hi_part(dst, half_tile(tile, s), u_hi_ready)

                def hi_u(lap, s, dst):
                    act.wait_ge(loaded[s], layer * (16 * U_LOADS) + (lap - AHEAD // RING) * 16
                                + 16 * (N_PRE // RING + AHEAD // DEEP + 1))
                    hi_part(dst, tile[:, s, 0:1024], u_hi_ready)

                def hi_v(lap, s):
                    act.wait_ge(v_loaded[s], layer * (16 * V_LOADS) + lap * 16 + 16 * (AHEAD // DEEP + 1))
                    act.wait_ge(v_used, layer * N_EXP + lap * RING + (s - 1 + RING))
                    nc.scalar.activation(v_hi[:, s % 2], tile[:, s, 1024:2048], ACT.Copy).then_inc(v_hi_ready, 1)

                def product_done(first, s):
                    act.wait_ge(tile_used, layer * N_USED + first + (N_KEYS + RING + s + 1))

                def gelu(s, dst):
                    nc.scalar.activation(dst, psum[4 + s % RING][:, 0:SEQ], ACT.Gelu).then_inc(act_ready, 1)

                def next_v(lap, s):
                    hi_v(lap + (s + 1) // RING, (s + 1) % RING)

                for s in range(2):
                    hi_ahead(0, s, u_hi[:, s])
                act.wait_ge(peer_scored, layer + 1)
                for b in range(4):
                    nc.scalar.activation(score_sb[:, b], psum[4 + b][:], ACT.Copy).then_inc(score_out, 1)
                for s in range(2, RING):
                    hi_ahead(0, s, u_hi[:, s])

                def gelu_out(first, s):
                    act.wait_ge(act_gated, layer * (N_EXP - N_FREE) + first - N_FREE + (s + 1))
                    gelu(s, act_out[s % 2][:])

                def free_laps(first, last):
                    with act.Fori(first, last) as lap:
                        for s in range(DEEP):
                            product_done(lap * DEEP, s)
                            hi_ahead(lap + (s + RING) // DEEP, (s + RING) % DEEP, u_hi[:, s % RING])
                            gelu(s, gate_all[:, bass.ds(lap * DEEP + s, 1), :].rearrange("p a t -> p (a t)"))

                def choice_exp(t):
                    act.wait_ge(gate_shift, layer * TT + (t + 1))
                    nc.scalar.activation(expd[:], shifted[:], ACT.Exp).then_inc(gate_exp, 1)

                free_laps(0, EXP_LAP)
                choice_exp(0)
                last = N_FREE // DEEP - 1
                free_laps(EXP_LAP, last)
                for s in range(DEEP):
                    product_done(last * DEEP, s)
                    if s < RING + 2:
                        hi_ahead(last + (s + RING) // DEEP, (s + RING) % DEEP, u_hi[:, s % RING])
                    gelu(s, gate_all[:, last * DEEP + s])
                choice_exp(1)
                act.wait_ge(chosen_turned, layer + 1)
                for i, dst in enumerate((gate_t[:], i12_t[:, 0], i12_t[:, 1])):
                    ins = nc.scalar.activation(dst, psum[i][:, 0:SEQ], ACT.Copy)
                ins.then_inc(chosen_out, 1)

                def gate_hots(lap, k):
                    act.wait_ge(hot_ready, layer * N_GROUP + lap * (2 * DEEP) + (k + 1))
                    for i in range(GROUP):
                        t = lap * (2 * DEEP * GROUP) + (k * GROUP + i)
                        row = hots[:, k % 2, 0, i]
                        ins = nc.scalar.activation(row, row, ACT.Copy, scale=gate_t[:, bass.ds(t, 1)])
                    ins.then_inc(hot_gated, 1)

                def gates_rest(lap, k):
                    act.wait_ge(gates_mult, layer * N_GROUP + lap * (2 * DEEP) + (k + 1))
                    nc.scalar.activation(
                        gate_all[:, AHEAD:N_EXP, bass.ds(lap * (2 * DEEP * GROUP) + k * GROUP, GROUP)],
                        psum[k % 4][:].rearrange("p (t e) -> p e t", t=GROUP)[:, AHEAD:N_EXP],
                        ACT.Copy).then_inc(gates_out, 1)

                for k in range(2):
                    gate_hots(0, k)
                def pair_step(lap, s, last=False):
                    for b in range(2):
                        gates_rest(lap, 2 * s + b)
                        if not (last and s == DEEP - 1):
                            gate_hots(lap + (s + 1) // DEEP, (2 * s + 2 + b) % (2 * DEEP))
                    tiles = lap + N_FREE // DEEP
                    product_done(tiles * DEEP, s)
                    if last and s >= DEEP - 2:
                        hi_u(AHEAD // RING, s + 2 - DEEP, u_hi[:, s % 2])
                    else:
                        hi_ahead(tiles + (s + 2) // DEEP, (s + 2) % DEEP, u_hi[:, s % 2])
                    gelu_out(tiles * DEEP, s)

                with act.Fori(0, N_PAIR // DEEP - 1) as lap:
                    for s in range(DEEP):
                        pair_step(lap, s)
                for s in range(DEEP):
                    pair_step(N_PAIR // DEEP - 1, s, True)
                act.wait_ge(gates_filled, layer * N_GROUP + (N_GROUP + 2))
                hi_v(0, 0)

                def both_step(lap, s, last=False):
                    tiles = lap + AHEAD // RING
                    product_done(tiles * RING, s)
                    if not (last and s >= 2):
                        hi_u(tiles + (s + 2) // RING, (s + 2) % RING, u_hi[:, s % 2])
                    gelu_out(tiles * RING, s)
                    next_v(lap, s)

                with act.Fori(0, N_BOTH // RING - 1) as lap:
                    for s in range(RING):
                        both_step(lap, s)
                for s in range(RING):
                    both_step(N_BOTH // RING - 1, s, True)
                with act.Fori(N_BOTH // RING, N_EXP // RING - 1) as lap:
                    for s in range(RING):
                        next_v(lap, s)
                for s in range(RING - 1):
                    next_v(N_EXP // RING - 1, s)

        @block.vector
        def _(vec):
            count = [0]

            def done(ins):
                count[0] += 1
                ins.then_inc(vec_order, 1)

            def settle(layer):
                vec.wait_ge(vec_order, layer * VEC_ORDER + count[0])

            def settle_apart(layer):
                settle(layer)
                vec.sem_inc(vec_passed, 1)

            vec.wait_ge(rel_product, 1)
            vec.wait_ge(rel_loaded, 48)
            nc.vector.tensor_tensor(rel_sb[:], psum[0][0:16, :], mask_sb[:], ALU.add).then_inc(rel_ready, 1)
            vec.wait_ge(consts_loaded, 48)
            vec.wait_ge(x_loaded, 16)
            vec.sem_inc(h_ready, 1)
            vec.sem_inc(act_gated, 2)

            def mean(at, n, width):
                return nc.vector.tensor_scalar(stat[:, at:at + n], stat[:, at:at + n], 1.0 / width, EPS,
                                               ALU.mult, ALU.add)

            def stats(at, heads):
                return stat[:, at:at + TT * heads].rearrange("p (t h) -> p t h", t=TT)

            def scales(at, heads, width):
                r = rstd[:, at:at + TT * heads].rearrange("p (t h) -> p t h", t=TT)
                return r.unsqueeze(3).broadcast_to([P, TT, heads, width])

            def rope(layer, src, dst, heads, axes, t, at=0):
                n = heads * len(axes) * 16
                parts = [rot[:, i, at:at + n].rearrange("p (h a c) -> p h a c", h=heads, a=len(axes))
                         for i in range(4)]
                tab = rope_t[:, t, axes[0]:axes[-1] + 1]
                cos, sin = (tab[:, :, i, :].unsqueeze(1).broadcast_to([P, heads, len(axes), 16])
                            for i in range(2))
                lo, hi = src[:, :, :, 0:16], src[:, :, :, 16:32]
                nc.vector.tensor_tensor(parts[0], lo, cos, ALU.mult)
                nc.vector.tensor_tensor(parts[1], hi, sin, ALU.mult)
                nc.vector.tensor_tensor(parts[2], lo, sin, ALU.mult)
                done(nc.vector.tensor_tensor(parts[3], hi, cos, ALU.mult))
                settle(layer)
                nc.vector.tensor_tensor(dst[:, :, :, 0:16], parts[0], parts[1], ALU.subtract)
                return nc.vector.tensor_tensor(dst[:, :, :, 16:32], parts[2], parts[3], ALU.add)

            def unit_scores(layer, u):
                mixer, head = UNITS[u]
                vec.wait_ge(scored, layer * N_UNIT + (u + 1))
                if mixer in "cd":
                    src = psum[2 + u % 3][:].rearrange("p (t k) -> p t k", t=TT)
                    done(nc.vector.tensor_reduce(unit_n[:, u % 2], src, AX_X, ALU.max))
                    settle(layer)
                    scale = DH ** -0.5 if mixer == "d" else C_QK ** -0.5
                    nc.vector.tensor_scalar(unit_m[:, u % 2], unit_n[:, u % 2], -scale, None,
                                            ALU.mult).then_inc(max_ready, 1)
                    return
                vec.wait_ge(bias_loaded[u % 2], layer * 64 + 16 * (u // 2 + 1))
                if u >= 2:
                    vec.wait_ge(pt_ready, layer * N_PT + PT_BEFORE[u - 1])
                groups = 1 if mixer == "a" else 3
                for g in range(groups):
                    bank = 2 + u % 3 if mixer == "a" else 2 + g
                    for t in range(TT):
                        ins = nc.vector.scalar_tensor_tensor(
                            out=prob[:, u % 2, t, g * SEQ:(g + 1) * SEQ], in0=psum[bank][:, t * SEQ:(t + 1) * SEQ],
                            scalar=DH ** -0.5, in1=bias_t[:, u % 2, g, P - P * t:P - P * t + SEQ],
                            op0=ALU.mult, op1=ALU.add)
                width = groups * SEQ
                ins.then_inc(score_read, 1)
                if mixer == "a":
                    done(nc.vector.tensor_copy(
                        prob[:, u % 2, :, SEQ:SEQ + 1],
                        grow[:, GR_SINK + head:GR_SINK + head + 1].unsqueeze(1).broadcast_to([P, TT, 1])))
                    width += 1
                    settle(layer)
                vec.wait_ge(score_read, layer * N_UNIT + (u + 1))
                nc.vector.tensor_reduce(unit_m[:, u % 2], prob[:, u % 2, :, 0:width], AX_X, ALU.max,
                                        negate=True).then_inc(max_ready, 1)

            def unit_norm(layer, u):
                width = 768 if UNITS[u][0] == "b" else SEQ
                vec.wait_ge(exped, layer * (2 * N_UNIT) + (2 * u + 2))
                done(nc.vector.reciprocal(unit_r[:, u % 2], unit_d[:, u % 2]))
                settle(layer)
                for t in range(TT):
                    ins = nc.vector.tensor_scalar(prob[:, u % 2, t, 0:width], prob[:, u % 2, t, 0:width],
                                                  unit_r[:, u % 2, t:t + 1], None, ALU.mult)
                ins.then_inc(prob_ready, 1)

            def top16(layer, n, src, work, values, places):
                for i in range(n):
                    ins = nc.vector.max(values[:, i, 0:8], src(i))
                done(ins)
                settle_apart(layer)
                for i in range(n):
                    nc.vector.max_index(places[:, i, 0:8], values[:, i, 0:8], src(i))
                for i in range(n):
                    ins = nc.vector.match_replace(work[:, i, :], values[:, i, 0:8], src(i), DEAD)
                done(ins)
                settle_apart(layer)
                for i in range(n):
                    ins = nc.vector.max(values[:, i, 8:16], work[:, i, :])
                done(ins)
                settle_apart(layer)
                for i in range(n):
                    ins = nc.vector.max_index(places[:, i, 8:16], values[:, i, 8:16], work[:, i, :])
                return ins

            def spread(dst, first, second, op):
                at = 0
                for a, rows, width in CAND_ROWS:
                    o = dst[:, :, at:at + rows * width].rearrange("p h (a b) -> p h a b", a=rows)
                    shape = [P, HEADS, rows, width]
                    ins = nc.vector.tensor_tensor(o, first[:, :, a:a + rows].unsqueeze(3).broadcast_to(shape),
                                                  second[:, :, 0:width].unsqueeze(2).broadcast_to(shape), op)
                    at += rows * width
                return ins

            def choose(layer, n, t):
                def scores(i):
                    head, half = i // 2, i % 2
                    b = score_sb[:, 2 * half + head // 4] if t == 0 else psum[2 * half + head // 4]
                    at = head % 4 * KEYS
                    return b[:, at:at + KEYS]

                done(top16(layer, 2 * HEADS, scores, left, top_v, top_i))
                settle(layer)
                done(nc.vector.tensor_copy(top_f[:], top_i[:]))
                halves_v = top_v[:].rearrange("p (h c) k -> p h c k", c=2)
                halves_f = top_f[:].rearrange("p (h c) k -> p h c k", c=2)
                done(spread(cand, halves_v[:, :, 0], halves_v[:, :, 1], ALU.add))
                settle(layer)
                done(nc.vector.tensor_scalar(halves_f[:, :, 0], halves_f[:, :, 0], float(KEYS), None, ALU.mult))
                settle(layer)
                done(spread(cand_i, halves_f[:, :, 0], halves_f[:, :, 1], ALU.add))
                settle_apart(layer)
                done(top16(layer, HEADS, lambda i: cand[:, i, :], cand_left, best, best_p))
                settle(layer)
                nc.vector.tensor_tensor(shifted[:], best[:], best[:, :, 0:1].broadcast_to([P, HEADS, TOPK]),
                                        ALU.subtract).then_inc(gate_shift, 1)
                done(nc.vector.tensor_copy(best_f[:], best_p[:]))
                settle(layer)
                few = HEADS // 2
                for first in (0, few):
                    for i in range(few):
                        shape = [P, TOPK, N_CAND]
                        ins = nc.vector.tensor_tensor(match[:, i],
                                                      iota[:, 0:N_CAND].unsqueeze(1).broadcast_to(shape),
                                                      best_f[:, first + i].unsqueeze(2).broadcast_to(shape),
                                                      ALU.is_equal)
                    done(ins)
                    settle(layer)
                    of = cand_i[:, first:first + few].unsqueeze(2).broadcast_to([P, few, TOPK, N_CAND])
                    done(nc.vector.tensor_tensor(match[:], match[:], of, ALU.mult))
                    settle(layer)
                    done(nc.vector.tensor_reduce(idx_f[:, first:first + few], match[:], AX_X, ALU.add))
                    settle(layer)
                done(nc.vector.tensor_copy(idx_i[:], idx_f[:]))
                settle(layer)
                nc.vector.tensor_scalar(idx_1[:], idx_i[:], 7, None, ALU.arith_shift_right)
                done(nc.vector.tensor_scalar(idx_2[:], idx_i[:], KEYS - 1, None, ALU.bitwise_and))
                settle(layer)

                def flat(a):
                    return a[:].rearrange("p h k -> p (h k)")

                nc.vector.tensor_copy(sel[:, 1, t], flat(idx_1))
                nc.vector.tensor_copy(sel[:, 2, t], flat(idx_2))
                vec.wait_ge(gate_exp, layer * TT + (n + 1))
                done(nc.vector.tensor_reduce(esum[:], expd[:], AX_X, ALU.add))
                settle(layer)
                done(nc.vector.reciprocal(erec[:], esum[:]))
                settle(layer)
                nc.vector.tensor_tensor(sel[:, 0, t].rearrange("p (h k) -> p h k", h=HEADS), expd[:],
                                        erec[:].unsqueeze(2).broadcast_to([P, HEADS, TOPK]),
                                        ALU.mult).then_inc(chosen, 1)

            with vec.Fori(0, LAYERS) as layer:
                count[0] = 0

                def squares(k):
                    vec.wait_ge(squared, layer * N_SQ + k)

                def rsqrts(k):
                    vec.wait_ge(rstd_ready, layer * N_RMS + k)

                squares(2)
                mean(ST_H1, 2, DM).then_inc(mean_ready, 1)

                for c in range(DC):
                    vec.wait_ge(block_ready, layer * N_BLOCK + (c + 1))
                    done(nc.vector.tensor_copy(x_hi[:, c, :], x_t[:, c, :]))
                    settle(layer)
                    nc.vector.tensor_tensor(x_lo[:, c, :], x_t[:, c, :], x_hi[:, c, :],
                                            ALU.subtract).then_inc(chunk_split, 1)

                squares(3)
                done(nc.vector.tensor_reduce(stats(ST_A, 6), sq_a[:].rearrange("p t (h c) -> p t h c", h=6),
                                             AX_X, ALU.add))
                settle(layer)
                mean(ST_A, 12, DH).then_inc(mean_ready, 1)
                rsqrts(2)
                v = proj[:, :, AQ:AV].rearrange("p t (h c) -> p t h c", h=6)
                nc.vector.tensor_tensor(v, v, scales(ST_A, 6, DH), ALU.mult).then_inc(normed, 1)

                squares(4)
                done(nc.vector.tensor_reduce(stats(ST_B, 24), sq_b[:].rearrange("p t (h c) -> p t h c", h=24),
                                             AX_X, ALU.add))
                settle(layer)
                mean(ST_B, 48, DH).then_inc(mean_ready, 1)
                rsqrts(3)
                v = proj[:, :, BQ:BV].rearrange("p t (h c) -> p t h c", h=24)
                nc.vector.tensor_tensor(v, v, scales(ST_B, 24, DH), ALU.mult).then_inc(normed, 1)

                squares(5)
                for i, (lo, hi) in enumerate(((0, 256), (256, 384), (384, 416))):
                    ins = nc.vector.tensor_reduce(stat[:, ST_LAT + 2 * i:ST_LAT + 2 * i + 2].unsqueeze(2),
                                                  sq_l[:, :, lo:hi], AX_X, ALU.add)
                done(ins)
                settle(layer)
                mean(ST_LAT, 2, 256)
                mean(ST_LAT + 2, 2, 128)
                mean(ST_LAT + 4, 2, C_ROPE).then_inc(mean_ready, 1)
                rsqrts(4)
                for i, (lo, hi) in enumerate(((CQ, CKV), (CKV, CKR), (CKR, DQ))):
                    r = rstd[:, ST_LAT + 2 * i:ST_LAT + 2 * i + 2].unsqueeze(2).broadcast_to([P, TT, hi - lo])
                    ins = nc.vector.tensor_tensor(proj[:, :, lo:hi], proj[:, :, lo:hi], r, ALU.mult)
                ins.then_inc(normed, 1)

                def prepare_d():
                    squares(6)
                    done(nc.vector.tensor_reduce(stats(ST_D, 6), sq_d[:].rearrange("p t (h c) -> p t h c", h=6),
                                                 AX_X, ALU.add))
                    settle(layer)
                    mean(ST_D, 12, DH).then_inc(mean_ready, 1)
                    rsqrts(5)
                    v = proj[:, :, DQ:DV].rearrange("p t (h c) -> p t h c", h=6)
                    done(nc.vector.tensor_tensor(v, v, scales(ST_D, 6, DH), ALU.mult))
                    settle(layer)
                    vec.wait_ge(gains_loaded, layer * 32 + 32)
                    for lo, hi, g in ((0, 4, GR_DQ), (4, 6, GR_DK)):
                        shape = [P, TT, hi - lo, DH]
                        gain = grow[:, g:g + DH].unsqueeze(1).unsqueeze(1).broadcast_to(shape)
                        ins = nc.vector.tensor_tensor(v[:, :, lo:hi], v[:, :, lo:hi], gain, ALU.mult)
                    done(ins)
                    settle(layer)
                    for t in range(TT):
                        s = proj[:, t, DQ:DV].rearrange("p (h a c) -> p h a c", h=6, a=2)
                        done(rope(layer, s, s, 6, (1, 2), t))
                        settle(layer)
                    vec.sem_inc(normed, 1)

                def mean_c():
                    squares(8)
                    q4 = sq_c[:, :, 0:384].rearrange("p t (h c) -> p t h c", h=4)
                    nc.vector.tensor_reduce(stats(ST_C, 4), q4[:, :, :, 0:C_NOPE], AX_X, ALU.add)
                    nc.vector.tensor_reduce(stats(ST_C + 8, 4), q4[:, :, :, C_NOPE:C_QK], AX_X, ALU.add)
                    done(nc.vector.tensor_reduce(stats(ST_C + 16, 4), sq_c[:, :, 384:640]
                                                 .rearrange("p t (h c) -> p t h c", h=4), AX_X, ALU.add))
                    settle(layer)
                    mean(ST_C, 8, C_NOPE)
                    mean(ST_C + 8, 8, C_ROPE)
                    mean(ST_C + 16, 8, C_NOPE).then_inc(mean_ready, 1)

                def norm_c():
                    rsqrts(6)
                    qv = c_out[:, :, 0:384].rearrange("p t (h c) -> p t h c", h=4)
                    kv = c_out[:, :, 384:896].rearrange("p t (h c) -> p t h c", h=4)
                    qo, ko = cat[:, :, 0:4], cat[:, :, 4:8]
                    nc.vector.tensor_tensor(qo[:, :, :, 0:C_NOPE], qv[:, :, :, 0:C_NOPE], scales(ST_C, 4, C_NOPE),
                                            ALU.mult)
                    nc.vector.tensor_tensor(qo[:, :, :, C_NOPE:C_QK], qv[:, :, :, C_NOPE:C_QK],
                                            scales(ST_C + 8, 4, C_ROPE), ALU.mult)
                    done(nc.vector.tensor_tensor(ko[:, :, :, 0:C_NOPE], kv[:, :, :, 0:C_NOPE],
                                                 scales(ST_C + 16, 4, C_NOPE), ALU.mult))
                    settle(layer)
                    gq = grow[:, GR_CQ:GR_CQ + C_QK].unsqueeze(1).unsqueeze(1).broadcast_to([P, TT, 4, C_QK])
                    nc.vector.tensor_tensor(qo, qo, gq, ALU.mult)
                    gk = grow[:, GR_CK:GR_CK + C_NOPE].unsqueeze(1).unsqueeze(1).broadcast_to([P, TT, 4, C_NOPE])
                    nc.vector.tensor_tensor(ko[:, :, :, 0:C_NOPE], ko[:, :, :, 0:C_NOPE], gk, ALU.mult)
                    gp = grow[:, GR_CK + C_NOPE:GR_CK + C_QK].unsqueeze(1).broadcast_to([P, TT, C_ROPE])
                    done(nc.vector.tensor_tensor(proj[:, :, CKR:DQ], proj[:, :, CKR:DQ], gp, ALU.mult))

                def rope_c():
                    settle(layer)
                    for t in range(TT):
                        s = cat[:, t, 0:4, C_NOPE:C_QK].unsqueeze(2)
                        done(rope(layer, s, s, 4, (0,), t))
                        s = proj[:, t, CKR:DQ].unsqueeze(1).unsqueeze(1)
                        done(rope(layer, s, s, 1, (0,), t, 128))
                        settle(layer)
                    for t in range(TT):
                        ins = nc.vector.tensor_copy(cat[:, t, 4:8, C_NOPE:C_QK],
                                                    proj[:, t, CKR:DQ].unsqueeze(1).broadcast_to([P, 4, C_ROPE]))
                    ins.then_inc(normed, 1)

                for u in range(N_UNIT + 1):
                    if u:
                        unit_norm(layer, u - 1)
                    if u < N_UNIT:
                        unit_scores(layer, u)
                    if u == 0:
                        prepare_d()
                    if u == 2:
                        mean_c()
                    if u == STEP_NORM_C:
                        norm_c()
                    if u == STEP_ROPE_C:
                        rope_c()

                for j in range(16):
                    n, pair = j // 4, j % 4
                    vec.wait_ge(job_ready, layer * N_JOB + (J_MERGE + j + 1))
                    if j == 0:
                        vec.wait_ge(mixed, layer * N_UNIT + N_UNIT)
                    vec.wait_ge(gate_ready, layer * N_GATE + (j + 1))
                    dst = merged[:, 2 * pair:2 * pair + 2, :]
                    gate = gate_chunks(8 * n + 2 * pair, 2)
                    src = psum[(J_MERGE + j) % 2][:].rearrange("p (c t) -> p c t", c=2)
                    if n == 0:
                        nc.vector.tensor_tensor(dst, src, gate, ALU.mult).then_inc(job_sum, 1)
                        continue
                    part = prod[:, j % 2].rearrange("p (c t) -> p c t", c=2)
                    nc.vector.tensor_tensor(part, src, gate, ALU.mult).then_inc(job_sum, 1)
                    vec.wait_ge(job_sum, layer * N_JOB_VEC + (j + 1))
                    ins = nc.vector.tensor_tensor(dst, dst, part, ALU.add)
                    done(ins)
                    if pair == 3:
                        settle(layer)
                vec.sem_inc(merged_ready, 1)

                for j in range(4):
                    vec.wait_ge(job_ready, layer * N_JOB + (J_OUT + j + 1))
                    dst = h[:, :, j * 256:(j + 1) * 256]
                    nc.vector.tensor_tensor(dst, psum[(J_OUT + j) % 2][:].rearrange("p (t c) -> p t c", t=TT),
                                            dst, ALU.add).then_inc(job_sum, 1)
                vec.wait_ge(job_sum, layer * N_JOB_VEC + N_JOB_VEC)
                vec.sem_inc(h2_ready, 1)

                squares(10)
                mean(ST_H2, 2, DM).then_inc(mean_ready, 1)
                vec.wait_ge(block_ready, layer * N_BLOCK + N_BLOCK)
                done(nc.vector.tensor_copy(x_hi[:], x_t[:]))
                settle(layer)
                nc.vector.tensor_tensor(x_lo[:], x_t[:], x_hi[:], ALU.subtract).then_inc(x_split, 1)

                vec.wait_ge(peer_scored, layer + 1)
                vec.sem_inc(vec_passed, 1)
                choose(layer, 0, 1)
                vec.wait_ge(score_out, layer * 4 + 4)
                vec.sem_inc(vec_passed, 1)
                choose(layer, 1, 0)
                assert count[0] == VEC_ORDER, count[0]

                vec.wait_ge(chosen_out, layer + 1)
                vec.sem_inc(vec_passed, 1)

                def match_rows(lap, k):
                    vec.wait_ge(gates_filled, layer * N_GROUP + lap * (2 * DEEP) + (k + 1))
                    shape = [P, 2, GROUP, P]
                    at = i12_t[:, :, bass.ds(lap * (2 * DEEP * GROUP) + k * GROUP, GROUP)]
                    nc.vector.tensor_tensor(hots[:, k % 2], iota[:].unsqueeze(1).unsqueeze(1).broadcast_to(shape),
                                            at.unsqueeze(3).broadcast_to(shape), ALU.is_equal)\
                        .then_inc(hot_ready, 1)

                def gate_ahead(lap, k):
                    vec.wait_ge(gates_filled, layer * N_GROUP + lap * (2 * DEEP) + (k + 3))
                    at = gate_all[:, 0:AHEAD, bass.ds(lap * (2 * DEEP * GROUP) + k * GROUP, GROUP)]
                    src = psum[k % 4][:].rearrange("p (t e) -> p e t", t=GROUP)[:, 0:AHEAD]
                    return nc.vector.tensor_tensor(at, src, at, ALU.mult).then_inc(gates_mult, 1)

                def gate_act(first, s):
                    vec.wait_ge(act_ready, layer * N_EXP + first + (s + 1 + RING))
                    at = gate_all[:, bass.ds(first + s, 1), :]
                    nc.vector.tensor_tensor(at, act_out[s % 2][:].unsqueeze(1), at, ALU.mult).then_inc(act_gated, 1)

                def pair_step(lap, s, more=True, first=False):
                    if not first:
                        vec.wait_ge(gates_mult, layer * N_GROUP + lap * (2 * DEEP) + 2 * s)
                        gate_act(lap * DEEP + N_FREE, s - 2)
                    for b in range(2):
                        if more:
                            match_rows(lap + (s + 1) // DEEP, (2 * s + 2 + b) % (2 * DEEP))
                        if b == 0:
                            vec.wait_ge(act_gated, layer * (N_EXP - N_FREE) + lap * DEEP + (s + 1))
                        gate_ahead(lap, 2 * s + b)

                vec.wait_ge(ones_ready, layer + 1)
                for k in range(2):
                    match_rows(0, k)
                for s in range(DEEP):
                    pair_step(0, s, first=s < 2)
                with vec.Fori(1, N_PAIR // DEEP - 1) as lap:
                    for s in range(DEEP):
                        pair_step(lap, s)
                for s in range(DEEP):
                    pair_step(N_PAIR // DEEP - 1, s, s < DEEP - 1)
                vec.wait_ge(gates_mult, layer * N_GROUP + N_GROUP)
                gate_act(AHEAD, -2)
                gate_act(AHEAD, -1)

                def split_gated(lap, s):
                    vec.wait_ge(v_used, layer * N_EXP + lap * RING + (s - 1 + RING))
                    at = gate_all[:, bass.ds(lap * RING + s, 1), :] if not isinstance(lap, int) \
                        else gate_all[:, lap * RING + s:lap * RING + s + 1, :]
                    nc.vector.tensor_copy(g_hi[:, s % 2].unsqueeze(1), at).then_inc(gated_ready, 1)
                    vec.wait_ge(gated_ready, layer * (2 * N_EXP) + lap * (2 * RING) + (2 * s + 1))
                    nc.vector.tensor_tensor(g_lo[:, s % 2].unsqueeze(1), at, g_hi[:, s % 2].unsqueeze(1),
                                            ALU.subtract).then_inc(gated_ready, 1)

                def next_v(lap, s):
                    lap, s = lap + (s + 1) // RING, (s + 1) % RING
                    split_gated(lap, s)
                    lo_v(lap, s)

                def lo_v(lap, s):
                    vec.wait_ge(v_hi_ready, layer * N_EXP + lap * RING + (s + 1))
                    nc.vector.tensor_tensor(stream_lo[:, s, 1024:2048], tile[:, s, 1024:2048], v_hi[:, s % 2],
                                            ALU.subtract).then_inc(v_lo_ready, 1)

                vec.wait_ge(act_gated, layer * (N_EXP - N_FREE) + (N_PAIR + 2))
                vec.wait_ge(residual_in, layer + 1)
                split_gated(0, 0)
                lo_v(0, 0)
                with vec.Fori(0, N_BOTH // RING) as lap:
                    for s in range(RING):
                        gate_act(lap * RING + AHEAD, s)
                        next_v(lap, s)
                vec.wait_ge(act_gated, (layer + 1) * (N_EXP - N_FREE) + 2)
                vec.sem_inc(vec_passed, 1)
                with vec.Fori(N_BOTH // RING, N_EXP // RING - 1) as lap:
                    for s in range(RING):
                        next_v(lap, s)
                for s in range(RING - 1):
                    next_v(N_EXP // RING - 1, s)

                vec.wait_ge(experts_done, layer + 1)
                for b in range(4):
                    ins = nc.vector.tensor_copy(h[:, b // 2, b % 2 * 512:(b % 2 + 1) * 512], psum[b][:])
                ins.then_inc(h_ready, 1)

        @block.tensor
        def _(pe):
            pe.sem_inc(tile_used, RING)
            pe.sem_inc(v_used, RING)
            pe.sem_inc(gates_filled, 2)
            pe.wait_ge(rel_loaded, 48)
            nc.tensor.matmul(psum[0][0:16, :], relb_sb[0:32, :], one_hot_b[0:32, :], start=True,
                             stop=True).then_inc(rel_product, 1)
            pe.wait_ge(consts_loaded, 48)

            def turn(layer, k, srcs, rows=P):
                if k not in (BL_H1, BL_H1 + 1):
                    pe.wait_ge(block_ready, layer * N_BLOCK + (k - 1))
                for t, src in enumerate(srcs):
                    ins = nc.tensor.transpose(psum[5 + k % 2][0:rows, t * P:(t + 1) * P], src, ident[:])
                ins.then_inc(turned, 1)

            def tile_there(layer, j):
                pe.wait_ge(loaded[j % RING], layer * (16 * U_LOADS) + 16 * (j // RING + 1))

            def bank_free(layer, j):
                if j < 2:
                    return
                k = j - 2
                if k < J_MERGE:
                    pe.wait_ge(job_out, layer * N_JOB_ACT + (k + 1))
                elif k < J_WQ:
                    pe.wait_ge(job_sum, layer * N_JOB_VEC + (k - J_MERGE + 1))
                else:
                    pe.wait_ge(job_out, layer * N_JOB_ACT + (J_MERGE + k - J_WQ + 1))

            def rows_job(layer, j, stile, width, x_rows, w, chunks):
                tile_there(layer, stile)
                bank_free(layer, j)
                for t in range(TT):
                    for c in range(chunks):
                        ins = nc.tensor.matmul(psum[j % 2][:, t * width:(t + 1) * width], x_rows(c, t), w(c),
                                               start=(c == 0), stop=(c == chunks - 1))
                return ins

            def cols_job(layer, j, stile, w, x_cols, chunks):
                tile_there(layer, stile)
                bank_free(layer, j)
                for i in range(2):
                    for c in range(chunks):
                        ins = nc.tensor.matmul(psum[j % 2][:, i * SEQ:(i + 1) * SEQ], w(c, i), x_cols(c),
                                               start=(c == 0), stop=(c == chunks - 1))
                return ins

            def split_product(dst, hi_hi, hi_lo, lo_hi, start, stop):
                nc.tensor.matmul(dst, *hi_hi, start=start, stop=False, skip_group_check=True)
                nc.tensor.matmul(dst, *hi_lo, start=False, stop=False, skip_group_check=True)
                return nc.tensor.matmul(dst, *lo_hi, start=False, stop=stop, skip_group_check=True)

            def split_rows_job(layer, j):
                pe.wait_ge(w_lo_ready, layer * N_PROJ + (j + 1))
                bank_free(layer, j)
                for t in range(TT):
                    rows = slice(t * P, (t + 1) * P)
                    for c in range(DC):
                        cols = slice(c * PROJ_W, (c + 1) * PROJ_W)
                        wh, wl = w_hi[j % 3][:, cols], stream_lo[:, j % RING, cols]
                        ins = split_product(psum[j % 2][:, t * PROJ_W:(t + 1) * PROJ_W],
                                            (x_hi[:, c, rows], wh), (x_hi[:, c, rows], wl),
                                            (x_lo[:, c, rows], wh), c == 0, c == DC - 1)
                return ins

            def wide(stile, width=256):
                return lambda c: tile[:, stile % RING, c * width:(c + 1) * width]

            def gate_job(layer, j, n):
                pe.wait_ge(gw_lo_ready, layer * N_GATE + (n + 1))
                bank_free(layer, j)
                wh, wl = (a.rearrange("p (c i m) -> p c i m", c=DC, i=2)
                          for a in (gw_hi[n % 2][:], stream_lo[:, gate_tile(n) % RING, :]))
                for i in range(2):
                    for c in range(DC):
                        ins = split_product(psum[j % 2][:, i * SEQ:(i + 1) * SEQ], (wh[:, c, i], x_hi[:, c]),
                                            (wh[:, c, i], x_lo[:, c]), (wl[:, c, i], x_hi[:, c]),
                                            c == 0, c == DC - 1)
                ins.then_inc(job_ready, 1)

            def scores(layer, u):
                mixer, head = UNITS[u]
                if mixer == "a" and u >= 3:
                    pe.wait_ge(score_read, layer * N_UNIT + (u - 2))
                elif mixer == "b" or u in (8, 9, 10):
                    pe.wait_ge(score_read, layer * N_UNIT + min(u, 8))
                elif u > 10:
                    pe.wait_ge(score_read, layer * N_UNIT + (u - 2))
                for g in range(3 if mixer == "b" else 1):
                    if mixer in "ad":
                        first = QK_A if mixer == "a" else QK_D
                        q, k, rows = first + head % 2, first + 2, slice(64 * (head // 2), 64 * (head // 2) + 64)
                    elif mixer == "b":
                        q, k, rows = QK_B + 2 * g + head // 2, QK_B + 6 + 2 * g + head // 2, \
                            slice(64 * (head % 2), 64 * (head % 2) + 64)
                    else:
                        q, k, rows = QK_C + head, QK_C + 4 + head, slice(0, C_QK)
                    bank = 2 + g if mixer == "b" else 2 + u % 3
                    for t in range(TT):
                        ins = nc.tensor.matmul(psum[bank][:, t * SEQ:(t + 1) * SEQ],
                                               qk_t[rows, q, t * P:(t + 1) * P], qk_t[rows, k, :],
                                               start=True, stop=True)
                ins.then_inc(scored, 1)

            def values(u, chunk):
                mixer, head = UNITS[u]
                g, t = chunk // 2, chunk % 2
                if mixer == "a":
                    return proj[:, t, AV + head // 2 * DH:AV + (head // 2 + 1) * DH]
                if mixer == "b":
                    at = BV + (g * 4 + head) * DH
                    return proj[:, t, at:at + DH]
                if mixer == "d":
                    return proj[:, t, DV + head // 2 * DH:DV + (head // 2 + 1) * DH]
                at = 384 + head * 128 + C_NOPE
                return c_out[:, t, at:at + DH]

            def turn_probs(layer, u):
                pe.wait_ge(prob_ready, layer * N_UNIT + (u + 1))
                for i in range(PT_JOBS[u]):
                    k = PT_BEFORE[u] + i
                    if k >= 2:
                        pe.wait_ge(pt_out, layer * N_PT + (k - 1))
                    for c in range(2):
                        for t in range(TT):
                            at = (2 * i + c) * P
                            ins = nc.tensor.transpose(psum[5 + k % 2][:, c * SEQ + t * P:c * SEQ + (t + 1) * P],
                                                      prob[:, u % 2, t, at:at + P], ident[:])
                    ins.then_inc(pt_ready, 1)

            def mix_values(layer, u):
                if u % 2 == 0 and u:
                    pe.wait_ge(mixed_out, layer * (N_UNIT // 2) + u // 2)
                pe.wait_ge(pt_out, layer * N_PT + PT_BEFORE[u + 1])
                n = 2 * PT_JOBS[u]
                rows = slice(64 * (u % 2), 64 * (u % 2) + 64)
                for c in range(n):
                    ins = nc.tensor.matmul(psum[7][rows, 0:SEQ], values(u, c), prob_t[:, u % 2, c, :],
                                           start=(c == 0), stop=(c == n - 1))
                ins.then_inc(mixed, 1)

            def expert_up(layer, first, s, hi, lo):
                pe.wait_ge(u_lo_ready, layer * N_EXP + first + (s + 1))
                pe.wait_ge(act_ready, layer * N_EXP + first + (s + 1))
                lo = lo.rearrange("p (c e) -> p c e", c=DC)
                for c in range(DC):
                    ins = split_product(psum[4 + s % RING][:, 0:SEQ], (hi[:, c], x_hi[:, c]),
                                        (hi[:, c], x_lo[:, c]), (lo[:, c], x_hi[:, c]), c == 0, c == DC - 1)
                ins.then_inc(tile_used, 1)

            def expert_down(layer, lap, s, stop=False):
                pe.wait_ge(v_lo_ready, layer * N_EXP + lap * RING + (s + 1))
                pe.wait_ge(gated_ready, layer * (2 * N_EXP) + lap * (2 * RING) + (2 * s + 2))
                for t in range(TT):
                    a_hi, a_lo = (a[:, s % 2, t * P:(t + 1) * P] for a in (g_hi, g_lo))
                    for half in range(2):
                        v = slice(1024 + half * 512, 1024 + (half + 1) * 512)
                        vh, vl = v_hi[:, s % 2, half * 512:(half + 1) * 512], stream_lo[:, s, v]
                        ins = split_product(psum[2 * t + half][:], (a_hi, vh), (a_hi, vl), (a_lo, vh),
                                            False, stop)
                ins.then_inc(v_used, 1)

            with pe.Fori(0, LAYERS) as layer:
                pe.wait_ge(hn_ready, layer * 4 + 2)
                for c in range(DC):
                    turn(layer, BL_H1 + c, [hn[:, t, c * P:(c + 1) * P] for t in range(TT)])
                pe.wait_ge(chunk_split, layer * DC + DC)
                for j in range(N_PROJ):
                    ins = split_rows_job(layer, j)
                    ins.then_inc(job_ready, 1)

                def proj_blocks(first, cols, n, ready):
                    pe.wait_ge(normed, layer * N_NORMED + ready)
                    for i in range(n):
                        turn(layer, first + i,
                             [proj[:, t, cols + i * P:cols + (i + 1) * P] for t in range(TT)])

                proj_blocks(BL_A, AQ, 3, 1)
                proj_blocks(BL_B, BQ, 12, 2)
                proj_blocks(BL_LAT, CQ, 3, 3)

                def second_c():
                    for i in range(4):
                        j, stile = J_C + i, T_CW + i // 2
                        t = i % 2
                        tile_there(layer, stile)
                        bank_free(layer, j)
                        if i < 2:
                            for c in range(2):
                                ins = nc.tensor.matmul(psum[j % 2][:, 0:384], lat_t[:, c, t * P:(t + 1) * P],
                                                       tile[:, stile % RING, c * 384:(c + 1) * 384],
                                                       start=(c == 0), stop=(c == 1))
                        else:
                            ins = nc.tensor.matmul(psum[j % 2][:], lat_t[:, 2, t * P:(t + 1) * P],
                                                   tile[:, stile % RING, 0:512], start=True, stop=True)
                        ins.then_inc(job_ready, 1)

                pe.wait_ge(block_ready, layer * N_BLOCK + BL_D)
                for u in range(N_UNIT + 1):
                    if u == STEP_TURN_D:
                        proj_blocks(BL_D, DQ, 3, 4)
                        pe.wait_ge(block_ready, layer * N_BLOCK + BL_C)
                    if u == STEP_TURN_C:
                        pe.wait_ge(normed, layer * N_NORMED + 5)
                        for i in range(8):
                            turn(layer, BL_C + i, [cat[:, t, i, :] for t in range(TT)], rows=C_QK)
                        pe.wait_ge(block_ready, layer * N_BLOCK + BL_H2)
                    if u < N_UNIT:
                        scores(layer, u)
                    if u:
                        turn_probs(layer, u - 1)
                    if u < N_UNIT:
                        gate_job(layer, J_GATE_A + u if u < 2 else J_GATE_B + u - 2, u)
                    if u == STEP_C:
                        second_c()
                    if u:
                        mix_values(layer, u - 1)

                pe.wait_ge(mixed_out, layer * (N_UNIT // 2) + N_UNIT // 2)
                for n in range(4):
                    stile = T_BRANCH + n
                    w = tile[:, stile % RING, :].rearrange("p (c m) -> p c m", c=2)
                    for pair in range(4):
                        j = J_MERGE + 4 * n + pair
                        ins = cols_job(layer, j, stile, lambda c, i: w[:, c, (2 * pair + i) * P:(2 * pair + i + 1) * P],
                                       lambda c: y_t[:, 2 * n + c, :], 2)
                        ins.then_inc(job_ready, 1)
                pe.wait_ge(merged_ready, layer + 1)
                for j in range(4):
                    ins = rows_job(layer, J_OUT + j, T_OUT + j, 256, lambda c, t: merged[:, c, t * P:(t + 1) * P],
                                   wide(T_OUT + j), DC)
                    ins.then_inc(job_ready, 1)

                pe.wait_ge(hn_ready, layer * 4 + 4)
                for c in range(DC):
                    turn(layer, BL_H2 + c, [hn[:, t, c * P:(c + 1) * P] for t in range(TT)])
                pe.wait_ge(block_ready, layer * N_BLOCK + N_BLOCK)
                for n in range(4):
                    j = J_WQ + n
                    w = tile[:, (T_WQ + n) % RING, :].rearrange("p (c i m) -> p c i m", c=DC, i=2)
                    ins = cols_job(layer, j, T_WQ + n, lambda c, i: w[:, c, i], lambda c: x_t[:, c, :], DC)
                    ins.then_inc(job_ready, 1)
                pe.wait_ge(job_out, layer * N_JOB_ACT + N_JOB_ACT)
                for n in range(2):
                    stile = T_KEYS + n
                    tile_there(layer, stile)
                    w = tile[:, stile % RING, 0:512].rearrange("p (h k) -> p h k", h=4)
                    for t in range(TT):
                        for i in range(4):
                            head = 4 * n + i
                            for half in range(2):
                                rows = slice(64 * half, 64 * half + 64)
                                bank = (4, 0)[t] + 2 * half + head // 4
                                ins = nc.tensor.matmul(psum[bank][:, i * KEYS:(i + 1) * KEYS],
                                                       q_t[rows, head, t * P:(t + 1) * P], w[rows, i, :],
                                                       start=True, stop=True)
                    ins.then_inc(tile_used, 1)
                pe.wait_ge(tile_used, layer * N_USED + (N_KEYS + RING))
                pe.sem_inc(peer_scored, 1)

                pe.wait_ge(x_split, layer + 1)
                pe.sem_inc(pe_passed, 1)
                with pe.Fori(0, N_FREE // DEEP) as lap:
                    for s in range(DEEP):
                        if s < RING:
                            pe.wait_ge(score_out, layer * 4 + (s + 1))
                        expert_up(layer, lap * DEEP, s, u_hi[:, s % RING], half_tile(stream_lo, s))

                pe.wait_ge(chosen, layer * TT + TT)
                for i in range(3):
                    for t in range(TT):
                        ins = nc.tensor.transpose(psum[i][:, t * P:(t + 1) * P], sel[:, i, t], ident[:])
                ins.then_inc(chosen_turned, 1)

                pe.wait_ge(chosen_out, layer + 1)
                pe.sem_inc(pe_passed, 1)
                with pe.Fori(0, N_PAIR // DEEP) as lap:
                    for s in range(DEEP):
                        for b in range(2):
                            k = 2 * s + b
                            pe.wait_ge(hot_gated, layer * N_GROUP + lap * (2 * DEEP) + (k + 1))
                            pe.wait_ge(gates_out, layer * N_GROUP + lap * (2 * DEEP) + (k + 1))
                            for i in range(GROUP):
                                ins = nc.tensor.matmul(psum[k % 4][:, i * P:(i + 1) * P], hots[:, b, 1, i],
                                                       hots[:, b, 0, i], start=True, stop=True)
                            ins.then_inc(gates_filled, 1)
                        expert_up(layer, lap * DEEP + N_FREE, s, u_hi[:, s % 2], half_tile(stream_lo, s))

                pe.wait_ge(gates_out, (layer + 1) * N_GROUP + 4)
                for t in range(TT):
                    for half in range(2):
                        ins = nc.tensor.matmul(psum[2 * t + half][:], ident[:], h[:, t, half * 512:(half + 1) * 512],
                                               start=True, stop=False, skip_group_check=True)
                ins.then_inc(residual_in, 1)
                with pe.Fori(0, N_BOTH // RING) as lap:
                    for s in range(RING):
                        expert_up(layer, lap * RING + AHEAD, s, u_hi[:, s % 2], half_tile(stream_lo, s))
                        expert_down(layer, lap, s)
                with pe.Fori(N_BOTH // RING, N_EXP // RING - 1) as lap:
                    for s in range(RING):
                        expert_down(layer, lap, s)
                for s in range(RING):
                    expert_down(layer, N_EXP // RING - 1, s, s == RING - 1)
                pe.wait_ge(v_used, layer * N_EXP + (N_EXP + RING))
                pe.sem_inc(experts_done, 1)


def distance_buckets():
    rel = np.arange(-255, 257)
    n = np.abs(rel)
    nf = np.maximum(n, 1).astype(np.float32)
    large = 8 + (np.log(nf / np.float32(8)) / np.float32(math.log(1024 / 8)) * np.float32(8)).astype(np.int32)
    return np.where(rel > 0, 16, 0) + np.where(n < 8, n, np.minimum(large, 15)), rel


def shape_constants():
    bucket, rel = distance_buckets()
    onehot = np.zeros((33, 512), np.float32)
    onehot[bucket, np.arange(512)] = 1.0
    mask = np.zeros((16, 512), np.float32)
    mask[0:4, np.abs(rel) > 128] = NEG
    for g, dil in enumerate((1, 4, 16)):
        mask[4 + 4 * g:8 + 4 * g, (rel % dil != 0) | (np.abs(rel) > 64 * dil)] = NEG
    pos = np.arange(SEQ)
    freqs = (np.float32(10000.0) ** (-np.arange(16, dtype=np.float32) / np.float32(16))).astype(np.float32)
    rope = np.zeros((P, TT, 3, 2, 16), np.float32)
    for i, at in enumerate((pos, pos // 64, pos % 64)):
        ang = at.astype(np.float32)[:, None] * freqs[None, :]
        rope[:, :, i, 0] = np.cos(ang).reshape(TT, P, 16).transpose(1, 0, 2)
        rope[:, :, i, 1] = np.sin(ang).reshape(TT, P, 16).transpose(1, 0, 2)
    iota = np.broadcast_to(np.arange(P, dtype=np.float32), (P, P))
    return {"ident": np.eye(P, dtype=np.float32), "iota": np.ascontiguousarray(iota), "rope": rope,
            "onehot": onehot, "mask": mask}


def tiles_of(w, n):
    layers, rows, cols = w.shape
    t = w.reshape(layers, rows // P, P, n, cols // n).transpose(0, 3, 2, 1, 4)
    return np.ascontiguousarray(t).reshape(layers, n, P, -1)


def laid_out(i):
    w_in = i["w_in"]
    order = [h * DH + c for h in HEAD_ORDER for c in range(DH)]
    cols = np.arange(MIX)
    cols[AQ:AQ + 256] = AQ + np.array(order)
    cols[DQ:DQ + 256] = DQ + np.array(order)
    per = lambda a: a.reshape(LAYERS, -1, P).transpose(0, 2, 1)
    twice = lambda a: np.concatenate([a, a], axis=1)[:, :, None]
    gcols = np.concatenate(
        [per(i["norm1_gain"]), per(i["norm2_gain"]), per(i["gate_bias"]), twice(i["a_q_gain"]),
         twice(i["a_k_gain"])] + [twice(i["b_q_gain"][:, g]) for g in range(3)]
        + [twice(i["b_k_gain"][:, g]) for g in range(3)] + [per(i["c_q_lat_gain"]), per(i["c_kv_lat_gain"])],
        axis=2)
    grows = np.concatenate([i["c_q_gain"], i["c_k_gain"], i["d_q_gain"], i["d_k_gain"], i["a_sink"]], axis=1)
    relb = np.zeros((33, 16), np.float32)
    relb[0:32] = i["rel_bias"]
    keys = i["peer_sub_keys"].transpose(0, 2, 4, 1, 3).reshape(LAYERS, P, 2, 4 * KEYS).transpose(0, 2, 1, 3)
    w_u = i["peer_w_u"].reshape(LAYERS, N_EXP, P, DC, P).transpose(0, 1, 4, 3, 2)
    branch = i["w_branch"].reshape(LAYERS, 4, 2, P, DM).transpose(0, 1, 3, 2, 4)
    return {
        "x": i["x"].reshape(SEQ, DM), "relb": relb,
        "w_proj": tiles_of(w_in[:, :, cols], N_PROJ), "w_gate": tiles_of(w_in[:, :, MIX:], N_GATE),
        "w_cq": tiles_of(i["c_w_uq"], 1), "w_ckv": tiles_of(i["c_w_ukv"], 1),
        "w_branch": branch.reshape(LAYERS, 4, P, 2048), "w_out": tiles_of(i["w_out"], 4),
        "w_q": tiles_of(i["peer_w_q"], 4), "keys": keys,
        "w_u": w_u.reshape(LAYERS, N_EXP, P, 1024), "w_v": i["peer_w_v"].reshape(LAYERS, N_EXP, P, DM),
        "gcols": gcols, "grows": grows[:, None, :],
    } | shape_constants()


ORDER = ["x", "relb", "w_proj", "w_gate", "w_cq", "w_ckv", "w_branch", "w_out", "w_q", "keys", "w_u", "w_v",
         "gcols", "grows", "ident", "iota", "rope", "onehot", "mask"]


def kernel(**inputs):
    import concourse.bacc as bacc
    from concourse.bass_utils import run_bass_kernel_spmd

    placed = laid_out({k: np.asarray(v) for k, v in inputs.items()})
    arrays = {f"in_{n}": np.ascontiguousarray(placed[n]) for n in ORDER}
    nc = bacc.Bacc("TRN2", target_bir_lowering=False, num_devices=1)
    args = [nc.dram_tensor(f"in_{n}", arrays[f"in_{n}"].shape, F32, kind="ExternalInput").ap() for n in ORDER]
    out = nc.dram_tensor("out_0", (SEQ, DM), F32, kind="ExternalOutput").ap()
    trunk(nc, *args, out)
    r = run_bass_kernel_spmd(nc, [arrays], core_ids=[0])
    return r.results[0]["out_0"].reshape(1, SEQ, DM)
```

```python
import math
from contextlib import ExitStack

import numpy as np

import concourse.bass as bass
from concourse import mybir

F32 = mybir.dt.float32
F32R = mybir.dt.float32r
U32 = mybir.dt.uint32
I32 = mybir.dt.int32
ALU = mybir.AluOpType
ACT = mybir.ActivationFunctionType
AX_X = mybir.AxisListType.X

P = 128
LAYERS = 2
SEQ = 256
TT = SEQ // P
DM = 1024
DC = DM // P
EPS = 1e-6
NEG = -1e30
DH = 64

AQ, AK, AV = 0, 256, 384
BQ, BK, BV = 512, 1280, 2048
CQ, CKV, CKR = 2816, 3072, 3200
DQ, DK, DV = 3232, 3488, 3616
MIX = 3744
C_NOPE, C_ROPE, C_QK = 64, 32, 96
HEAD_ORDER = (0, 2, 1, 3)

RING = 4
N_PROJ = 16
PROJ_W = MIX // N_PROJ
N_GATE = 16
T_PROJ = 0
T_GATE_A = T_PROJ + N_PROJ
T_CW = T_GATE_A + 2
T_GATE_B = T_CW + 2
T_BRANCH = T_GATE_B + N_GATE - 2
T_OUT = T_BRANCH + 4
T_WQ = T_OUT + 4
T_KEYS = T_WQ + 4
N_PRE = T_KEYS + 2
N_EXP = 128
N_MW = 12
N_KEYS = 2
N_USED = N_KEYS + N_EXP
assert N_PRE % RING == 0 and N_EXP % RING == 0

BL_H1, BL_A, BL_B, BL_LAT, BL_D, BL_C, BL_H2 = 0, 8, 11, 23, 26, 29, 37
N_BLOCK = 45
QK_A, QK_B, QK_D, QK_C = 0, 3, 15, 18

UNITS = [("a", h) for h in range(4)] + [("b", h) for h in range(4)] \
    + [("d", h) for h in range(4)] + [("c", h) for h in range(4)]
N_UNIT = 16
PT_JOBS = [3 if m == "b" else 1 for m, _ in UNITS]
PT_BEFORE = [sum(PT_JOBS[:u]) for u in range(N_UNIT + 1)]
N_PT = PT_BEFORE[N_UNIT]
BRANCH_OF = {"a": 0, "b": 1, "c": 2, "d": 3}
TURNS_AT_START = {14: (BL_B, BL_B + 1), 15: (BL_B + 4, BL_B + 5)}
TURNS_IN_MIDDLE = {12: (BL_A, BL_A + 1), 13: (BL_A + 2,), 14: (BL_B + 2, BL_B + 3), 15: (BL_B + 6, BL_B + 7)}
BL_BEHIND = BL_B + 8
LO_VEC = 12
STEP_C = 1
STEP_NORM_D = 1
STEP_ROPE_D = 2
STEP_TURN_D = 5
STEP_MEAN_C = 3
STEP_NORM_C = 8
STEP_ROPE_C = 9
STEP_TURN_C = 11

J_PROJ, J_GATE_A, J_C, J_GATE_B, J_MERGE, J_OUT, J_WQ = 0, 16, 18, 22, 36, 52, 56
N_JOB = 60
LAST_JOB = [J_PROJ + j for j in range(N_PROJ)] + [J_GATE_A, J_GATE_A + 1, J_C + 1, J_C + 3] \
    + [J_GATE_B + j for j in range(N_GATE - 2)] + [J_MERGE + 4 * n + 3 for n in range(4)] \
    + [J_OUT + j for j in range(4)] + [J_WQ + n for n in range(4)]
N_JOB_ACT = 40
N_JOB_VEC = 20

ST_H1, ST_A, ST_B, ST_LAT, ST_D, ST_C, ST_H2 = 0, 2, 14, 62, 68, 80, 104
N_STAT = 106
N_RMS = 7
N_SQ = 10

GC_N1, GC_N2, GC_GB, GC_AQ, GC_AK, GC_BQ, GC_BK, GC_CQL, GC_CKL = 0, 8, 16, 48, 49, 50, 53, 56, 58
N_GC = 59
GR_CQ, GR_CK, GR_DQ, GR_DK, GR_SINK = 0, 96, 192, 256, 320
N_GR = 324

HEADS, TOPK, KEYS = 8, 16, 128
CAND_ROWS = [(0, 1, 16), (1, 1, 8), (2, 1, 5), (3, 1, 4), (4, 1, 3), (5, 3, 2), (8, 8, 1)]
N_CAND = sum(n * w for _, n, w in CAND_ROWS)
DEAD = -3.0e38
GROUP = 4
N_GROUP = SEQ // GROUP
N_FREE = 48
N_PAIR = N_GROUP // 2
EXP_LAP = 2
AHEAD = N_FREE + N_PAIR
N_BOTH = N_EXP - AHEAD
DEEP = 2 * RING
ONES_PARTS, ONES_LAPS = 2, 2
assert ONES_PARTS * ONES_LAPS < N_FREE // DEEP - 1
assert N_FREE % DEEP == 0 and N_PAIR % DEEP == 0 and N_BOTH % RING == 0
U_LOADS = N_PRE // RING + AHEAD // DEEP + N_BOTH // RING
V_LOADS = AHEAD // DEEP + N_EXP // RING

VEC_ORDER = 131
N_NORMED = 5


def trunk(nc, x, relb, w_proj, w_gate, w_cq, w_ckv, w_branch, w_out, w_q, keys, w_u, w_v,
          gcols, grows, ident_d, iota_d, rope_d, onehot_d, mask_d, out):
    ctx = ExitStack()
    with ctx:
        base = (nc.sbuf_base + 31) // 32 * 32
        top = nc.sbuf_usable_end // 32 * 32
        taken = {}

        def place(name, shape, dt, at):
            size = 4 * int(np.prod(shape[1:]))
            assert at + size <= top, (name, at, size, top)
            taken[name] = (at, size)
            return nc.alloc_sbuf_tensor_at(name, shape, dt, offset=at)

        class Region:
            def __init__(self, at):
                self.at = at

            def put(self, name, shape, dt=F32):
                t = place(name, shape, dt, self.at)
                self.at += (4 * int(np.prod(shape[1:])) + 31) // 32 * 32
                return t

        lasting = Region(base)
        ident = lasting.put("ident", [P, P])
        iota = lasting.put("iota", [P, P])
        rope_t = lasting.put("rope_t", [P, TT, 3, 2, 16])
        gcol = lasting.put("gcol", [P, N_GC])
        grow_at = lasting.at
        grow = lasting.put("grow", [P, N_GR])
        act_out = [lasting.put("act_out0", [P, SEQ]), place("act_out1", [P, SEQ], F32, grow_at)]
        half_neg = lasting.put("half_neg", [P, 64])
        gate_t = lasting.put("gate_t", [P, SEQ])
        i12_t = lasting.put("i12_t", [P, 2, SEQ])
        stream_at = lasting.at
        tile = lasting.put("stream_tile", [P, RING, 2048])
        stream_lo = place("stream_lo", [P, RING, 2048], F32R, stream_at)
        hi_at = lasting.at
        u_hi = lasting.put("u_hi", [P, RING, DC, P], F32R)
        v_hi = place("v_hi", [P, 2, DM], F32R, hi_at + 8192)
        x_hi = lasting.put("x_hi", [P, DC, SEQ], F32R)
        x_lo = lasting.put("x_lo", [P, DC, SEQ], F32R)
        gates_low = place("gates_low", [P, 16, SEQ], F32, hi_at)
        hots = place("hots", [P, 2, 2, GROUP, P], F32, hi_at + 8192)
        h_at = lasting.at
        h = lasting.put("h", [P, TT, DM])
        g_hi = place("g_hi", [P, 2, SEQ], F32R, h_at)
        g_lo = place("g_lo", [P, 2, SEQ], F32R, h_at + 2048)
        union = lasting.at

        mix = Region(union)
        proj_at = mix.at
        proj = mix.put("proj", [P, TT, MIX])
        gates_high = [place(f"gates_high{t}", [P, 8, SEQ], F32, proj_at + 4 * (t * MIX + BQ)) for t in range(TT)]
        bias_at = mix.at
        bias_t = mix.put("bias_t", [P, 2, 3, 384])
        qk_at = mix.at
        qk_t = mix.put("qk_t", [P, 26, SEQ])
        s_at = mix.at
        prob = mix.put("prob", [P, 2, TT, 772])
        pt_at = mix.at
        prob_t = mix.put("prob_t", [P, 2, 6, SEQ])
        y_at = mix.at
        y_t = mix.put("y_t", [P, 8, SEQ])
        x_at = mix.at
        x_t = mix.put("x_t", [P, DC, SEQ])
        m_at = mix.at
        merged = mix.put("merged", [P, DC, SEQ])
        c_out = mix.put("c_out", [P, TT, 896])
        cat_at = mix.at
        cat = mix.put("cat", [P, TT, 8, C_QK])
        stat_at = mix.at
        stat = mix.put("stat", [P, N_STAT])
        rstd = mix.put("rstd", [P, N_STAT])
        unit_m = mix.put("unit_m", [P, 2, TT])
        unit_n = mix.put("unit_n", [P, 2, TT])
        unit_d = mix.put("unit_d", [P, 2, TT])
        unit_r = mix.put("unit_r", [P, 2, TT])
        w_hi = [place(f"w_hi{i}", [P, DC * PROJ_W], F32R, at)
                for i, at in enumerate((hi_at, hi_at + 8192, m_at))]
        gw_hi = [place(f"gw_hi{i}", [P, 2048], F32R, at) for i, at in enumerate((x_at, m_at))]
        mw_hi3 = [place(f"mw_hi{i}", [P, 2048], F32R, at)
                  for i, at in enumerate((x_at, hi_at + 16384, hi_at + 24576))]
        qw_hi3 = [place(f"qw_hi{i}", [P, 2048], F32R, at) for i, at in enumerate((hi_at, hi_at + 8192, m_at))]
        mw_hi = [mw_hi3[k % 3] for k in range(8)] + [qw_hi3[k % 3] for k in range(4)]
        y_hi = place("y_hi", [P, 8, SEQ], F32R, bias_at)
        y_lo = place("y_lo", [P, 8, SEQ], F32R, y_at)
        m_hi = place("m_hi", [P, DC, SEQ], F32R, pt_at)
        m_lo = place("m_lo", [P, DC, SEQ], F32R, m_at)
        hn = place("hn", [P, TT, DM], F32, qk_at)
        junk = place("junk", [P, TT, DM], F32, s_at)
        sq_b = place("sq_b", [P, TT, 1536], F32, s_at)
        sq_c = place("sq_c", [P, TT, 640], F32, proj_at + 4 * BQ)
        rot = place("rot", [P, 4, 192], F32, proj_at + 4 * (MIX + BQ))
        sq_a = place("sq_a", [P, TT, 384], F32, pt_at + 8192)
        sq_d = place("sq_d", [P, TT, 384], F32, pt_at + 2048)
        lat_t = place("lat_t", [P, 3, SEQ], F32, pt_at + 8192)
        sq_l = place("sq_l", [P, TT, 416], F32, cat_at)
        prod = place("prod", [P, 2, 512], F32, s_at)
        one_hot_b = place("one_hot_b", [33, 512], F32, y_at)
        relb_sb = place("relb_sb", [33, 16], F32, y_at + 2048)
        mask_sb = place("mask_sb", [16, 512], F32, y_at + 4096)
        rel_sb = place("rel_sb", [16, 512], F32, y_at + 6144)

        q_t = place("q_t", [P, HEADS, SEQ], F32, y_at)
        peer = Region(union + AHEAD * SEQ * 4)
        score_sb = peer.put("score_sb", [P, 4, 512])
        left = peer.put("left", [P, 2 * HEADS, KEYS])
        top_v = peer.put("top_v", [P, 2 * HEADS, TOPK])
        top_i = peer.put("top_i", [P, 2 * HEADS, TOPK], U32)
        top_f = peer.put("top_f", [P, 2 * HEADS, TOPK])
        cand = peer.put("cand", [P, HEADS, N_CAND])
        cand_i = peer.put("cand_i", [P, HEADS, N_CAND])
        cand_left = peer.put("cand_left", [P, HEADS, N_CAND])
        best = peer.put("best", [P, HEADS, TOPK])
        best_p = peer.put("best_p", [P, HEADS, TOPK], U32)
        best_f = peer.put("best_f", [P, HEADS, TOPK])
        shifted = peer.put("shifted", [P, HEADS, TOPK])
        expd = peer.put("expd", [P, HEADS, TOPK])
        esum = peer.put("esum", [P, HEADS])
        erec = peer.put("erec", [P, HEADS])
        idx_f = peer.put("idx_f", [P, HEADS, TOPK])
        idx_i = peer.put("idx_i", [P, HEADS, TOPK], I32)
        idx_1 = peer.put("idx_1", [P, HEADS, TOPK], I32)
        idx_2 = peer.put("idx_2", [P, HEADS, TOPK], I32)
        sel = peer.put("sel", [P, 3, TT, P])
        match = peer.put("match", [P, HEADS // 2, TOPK, N_CAND])
        assert peer.at <= stat_at

        gate_all = place("gate_all", [P, N_EXP, SEQ], F32, union)

        psum = [ctx.enter_context(nc.psum_tensor(f"bank{b}", [P, 512], F32)) for b in range(8)]
        rel_dram = nc.dram_tensor("rel_by_distance", (16, P, 512), F32).ap()

        def half_tile(buf, s):
            return buf[:, s % RING, s // RING * 1024:(s // RING + 1) * 1024]

        def half_there(eng, layer, lap, s):
            if s < RING:
                eng.wait_ge(loaded[s], layer * (16 * U_LOADS) + lap * 16 + 16 * (N_PRE // RING + 1))
            else:
                eng.wait_ge(v_loaded[s - RING], layer * (16 * V_LOADS) + lap * 16 + 16)

        def gate_chunks(c, n):
            if c < 16:
                return gates_low[:, c:c + n, :]
            return gates_high[(c - 16) // 8][:, c % 8:c % 8 + n, :]

        def gate_tile(n):
            return T_GATE_A + n if n < 2 else T_GATE_B + n - 2

        def sem(name):
            return ctx.enter_context(nc.semaphore(name))

        consts_loaded = sem("consts_loaded")
        x_loaded = sem("x_loaded")
        rel_loaded = sem("rel_loaded")
        half_set = sem("half_set")
        vec_passed = sem("vec_passed")
        pool_passed = sem("pool_passed")
        pe_passed = sem("pe_passed")
        rel_product = sem("rel_product")
        rel_ready = sem("rel_ready")
        rel_stored = sem("rel_stored")
        h_ready = sem("h_ready")
        gains_loaded = sem("gains_loaded")
        bias_loaded = [sem(f"bias_loaded{i}") for i in range(2)]
        loaded = [sem(f"loaded{i}") for i in range(RING)]
        v_loaded = [sem(f"v_loaded{i}") for i in range(RING)]
        half_loaded = loaded + v_loaded
        tile_used = sem("tile_used")
        v_used = sem("v_used")
        squared = sem("squared")
        mean_ready = sem("mean_ready")
        rstd_ready = sem("rstd_ready")
        hn_ready = sem("hn_ready")
        turned = sem("turned")
        block_ready = sem("block_ready")
        job_ready = sem("job_ready")
        job_out = sem("job_out")
        job_sum = sem("job_sum")
        normed = sem("normed")
        scored = sem("scored")
        score_read = sem("score_read")
        max_ready = sem("max_ready")
        exped = sem("exped")
        prob_ready = sem("prob_ready")
        pt_ready = sem("pt_ready")
        pt_out = sem("pt_out")
        mixed = sem("mixed")
        mixed_out = sem("mixed_out")
        gate_ready = sem("gate_ready")
        merged_ready = sem("merged_ready")
        h2_ready = sem("h2_ready")
        w_hi_ready = sem("w_hi_ready")
        w_lo_ready = sem("w_lo_ready")
        w_lo_vec = sem("w_lo_vec")
        gw_hi_ready = sem("gw_hi_ready")
        gw_lo_ready = sem("gw_lo_ready")
        chunk_split = sem("chunk_split")
        mw_hi_ready = sem("mw_hi_ready")
        mw_lo_ready = sem("mw_lo_ready")
        y_split = sem("y_split")
        peer_scored = sem("peer_scored")
        gate_exp = sem("gate_exp")
        gate_shift = sem("gate_shift")
        chosen = sem("chosen")
        chosen_turned = sem("chosen_turned")
        chosen_out = sem("chosen_out")
        hot_ready = sem("hot_ready")
        hot_gated = sem("hot_gated")
        score_out = sem("score_out")
        ones_ready = sem("ones_ready")
        gates_filled = sem("gates_filled")
        gates_mult = sem("gates_mult")
        gates_out = sem("gates_out")
        u_hi_ready = sem("u_hi_ready")
        v_hi_ready = sem("v_hi_ready")
        u_lo_ready = sem("u_lo_ready")
        v_lo_ready = sem("v_lo_ready")
        act_ready = sem("act_ready")
        act_gated = sem("act_gated")
        residual_in = sem("residual_in")
        gated_ready = sem("gated_ready")
        experts_done = sem("experts_done")
        vec_order = sem("vec_order")
        stored = sem("stored")

        block = ctx.enter_context(nc.Block())

        @block.sync
        def _(sp):
            sp.dma_start(h[:], x.rearrange("(t p) d -> p t d", p=P)).then_inc(x_loaded, 16)
            pre = [(w_proj, j, DC * PROJ_W) for j in range(N_PROJ)]
            pre += [(w_gate, j, 2048) for j in range(2)]
            pre += [(w_cq, 0, 768), (w_ckv, 0, 512)]
            pre += [(w_gate, j, 2048) for j in range(2, N_GATE)]
            pre += [(w_branch, j, 2048) for j in range(4)]
            pre += [(w_out, j, 2048) for j in range(4)]
            pre += [(w_q, j, 2048) for j in range(4)]
            pre += [(keys, j, 512) for j in range(2)]
            assert len(pre) == N_PRE
            with sp.Fori(0, LAYERS) as layer:
                def pre_used(j):
                    if j < T_KEYS:
                        sp.wait_ge(job_ready, layer * N_JOB + (LAST_JOB[j] + 1))
                    else:
                        sp.wait_ge(tile_used, layer * N_USED + (RING + j - T_KEYS + 1))

                sp.wait_ge(act_gated, layer * (N_EXP - N_FREE) + 2)
                sp.dma_start(gcol[:], gcols[layer]).then_inc(gains_loaded, 16)
                sp.dma_start(grow[:], grows[layer].partition_broadcast(P)).then_inc(gains_loaded, 16)
                sp.wait_ge(x_loaded, 16)
                for j, (src, n, width) in enumerate(pre):
                    if j == 0:
                        sp.wait_ge(tile_used, layer * N_USED + RING)
                        sp.wait_ge(v_used, layer * N_EXP + RING)
                    if j >= RING:
                        pre_used(j - RING)
                    sp.dma_start(tile[:, j % RING, 0:width], src[layer, n]).then_inc(loaded[j % RING], 16)

                def load_ahead(lap, s):
                    sp.dma_start(half_tile(tile, s), w_u[layer, lap * DEEP + s]).then_inc(half_loaded[s], 16)

                def load_u(lap, s, used):
                    sp.wait_ge(tile_used, used)
                    sp.dma_start(tile[:, s, 0:1024], w_u[layer, lap * RING + s]).then_inc(loaded[s], 16)

                def load_v(lap, s):
                    sp.dma_start(tile[:, s, 1024:2048], w_v[layer, lap * RING + s]).then_inc(v_loaded[s], 16)

                experts_used = layer * N_USED + (N_KEYS + RING)
                for s in range(DEEP):
                    if s < RING:
                        pre_used(N_PRE - RING + s)
                    load_ahead(0, s)
                with sp.Fori(1, AHEAD // DEEP) as lap:
                    for s in range(DEEP):
                        sp.wait_ge(tile_used, experts_used + (lap - 1) * DEEP + (s + 1))
                        load_ahead(lap, s)
                for s in range(RING):
                    load_u(AHEAD // RING, s, experts_used + (AHEAD - DEEP + s + 1))
                for s in range(RING):
                    sp.wait_ge(tile_used, experts_used + (AHEAD - RING + s + 1))
                    load_v(0, s)
                with sp.Fori(1, N_BOTH // RING) as lap:
                    for s in range(RING):
                        load_u(lap + AHEAD // RING, s, experts_used + AHEAD + (lap - 1) * RING + (s + 1))
                        sp.wait_ge(v_used, layer * N_EXP + lap * RING + (s + 1))
                        load_v(lap, s)
                with sp.Fori(N_BOTH // RING, N_EXP // RING) as lap:
                    for s in range(RING):
                        sp.wait_ge(v_used, layer * N_EXP + lap * RING + (s + 1))
                        load_v(lap, s)
            sp.wait_ge(h_ready, 2 * LAYERS + 2)
            sp.dma_start(out.rearrange("(t p) d -> p t d", p=P), h[:]).then_inc(stored, 16)
            sp.wait_ge(stored, 16)

        @block.gpsimd
        def _(pool):
            nc.gpsimd.memset(half_neg[:], -0.5).then_inc(half_set, 1)
            pool.wait_ge(rel_ready, 1)
            pool.dma_start(rel_dram, rel_sb[:].unsqueeze(1).broadcast_to([16, P, 512])).then_inc(rel_stored, 16)
            pool.wait_ge(half_set, 1)

            def bias_load(layer, u):
                mixer, head = UNITS[u]
                if u >= 2:
                    pool.wait_ge(score_read, layer * N_UNIT + (u - 1))
                    pool.sem_inc(pool_passed, 1)
                if mixer == "a":
                    src = bass.AP(tensor=rel_dram.tensor, offset=head * P * 512 + 127, ap=[[511, P], [1, 384]])
                    dst = bias_t[:, u % 2, 0, :]
                else:
                    src = bass.AP(tensor=rel_dram.tensor, offset=(4 + head) * P * 512 + 127,
                                  ap=[[511, P], [4 * P * 512, 3], [1, 384]])
                    dst = bias_t[:, u % 2]
                pool.dma_start(dst, src).then_inc(bias_loaded[u % 2], 16)

            def rsqrt(layer, k, at, n):
                pool.wait_ge(mean_ready, layer * N_RMS + (k + 1))
                nc.gpsimd.tensor_tensor(rstd[:, at:at + n], stat[:, at:at + n], half_neg[:, 0:n],
                                        ALU.pow).then_inc(rstd_ready, 1)

            with pool.Fori(0, LAYERS) as layer:
                rsqrt(layer, 0, ST_H1, 2)
                for j in range(N_PROJ):
                    if j == 8:
                        pool.wait_ge(rel_stored, 16)
                        bias_load(layer, 0)
                        bias_load(layer, 1)
                    if j != LO_VEC:
                        pool.wait_ge(w_hi_ready, layer * N_PROJ + (j + 1))
                        nc.gpsimd.tensor_tensor(stream_lo[:, j % RING, 0:DC * PROJ_W],
                                                tile[:, j % RING, 0:DC * PROJ_W],
                                                w_hi[j % 3][:], ALU.subtract).then_inc(w_lo_ready, 1)
                    if j == 5:
                        rsqrt(layer, 1, ST_A, 12)
                    if j == 11:
                        rsqrt(layer, 2, ST_B, 48)
                rsqrt(layer, 3, ST_LAT, 6)
                for u in range(N_UNIT):
                    if 2 <= u < 8:
                        bias_load(layer, u)
                    pool.wait_ge(gw_hi_ready, layer * N_GATE + (u + 1))
                    slot = gate_tile(u) % RING
                    nc.gpsimd.tensor_tensor(stream_lo[:, slot, :], tile[:, slot, :], gw_hi[u % 2][:],
                                            ALU.subtract).then_inc(gw_lo_ready, 1)
                    if u == 0:
                        rsqrt(layer, 4, ST_D, 12)
                    if u == 4:
                        rsqrt(layer, 5, ST_C, 24)
                for k in range(N_MW):
                    pool.wait_ge(mw_hi_ready, layer * N_MW + (k + 1))
                    slot = (T_BRANCH + k) % RING
                    nc.gpsimd.tensor_tensor(stream_lo[:, slot, :], tile[:, slot, :], mw_hi[k][:],
                                            ALU.subtract).then_inc(mw_lo_ready, 1)
                    if k == N_MW - 3:
                        rsqrt(layer, 6, ST_H2, 2)

                def lo_u(first, s, hi):
                    pool.wait_ge(u_hi_ready, layer * N_EXP + first + (s + 1))
                    nc.gpsimd.tensor_tensor(half_tile(stream_lo, s), half_tile(tile, s),
                                            hi.rearrange("p c e -> p (c e)"),
                                            ALU.subtract).then_inc(u_lo_ready, 1)

                part = N_PAIR // ONES_PARTS
                for i in range(ONES_PARTS):
                    with pool.Fori(i * ONES_LAPS, (i + 1) * ONES_LAPS) as lap:
                        for s in range(DEEP):
                            lo_u(lap * DEEP, s, u_hi[:, s % RING])
                    first = N_FREE + i * part
                    nc.gpsimd.memset(gate_all[:, first:first + part, :], 1.0).then_inc(ones_ready, 1)
                with pool.Fori(ONES_PARTS * ONES_LAPS, N_FREE // DEEP - 1) as lap:
                    for s in range(DEEP):
                        lo_u(lap * DEEP, s, u_hi[:, s % RING])
                for s in range(DEEP):
                    lo_u(N_FREE - DEEP, s, u_hi[:, s if s < RING else s % 2])
                with pool.Fori(N_FREE // DEEP, AHEAD // DEEP) as lap:
                    for s in range(DEEP):
                        lo_u(lap * DEEP, s, u_hi[:, s % 2])
                with pool.Fori(AHEAD // RING, N_EXP // RING) as lap:
                    for s in range(RING):
                        lo_u(lap * RING, s, u_hi[:, s % 2])

        @block.scalar
        def _(act):
            act.sem_inc(gates_out, 4)
            act.sem_inc(act_ready, RING)
            act.dma_start(relb_sb[:], relb).then_inc(rel_loaded, 16)
            act.dma_start(one_hot_b[:], onehot_d).then_inc(rel_loaded, 16)
            act.dma_start(mask_sb[:], mask_d).then_inc(rel_loaded, 16)
            act.dma_start(ident[:], ident_d).then_inc(consts_loaded, 16)
            act.dma_start(iota[:], iota_d).then_inc(consts_loaded, 16)
            act.dma_start(rope_t[:], rope_d).then_inc(consts_loaded, 16)
            act.wait_ge(x_loaded, 16)

            def rms_rows(layer, at, block0, gain0, src_ready, meanwhile=None):
                src_ready()
                for t in reversed(range(TT)):
                    nc.scalar.activation(junk[:, t], h[:, t], ACT.Square,
                                         accum_out=stat[:, at + t:at + t + 1]).then_inc(squared, 1)
                if meanwhile:
                    meanwhile()
                act.wait_ge(gains_loaded, layer * 32 + 32)
                for c in range(DC):
                    turn_out(layer, block0 + c, x_t[:, c, :], gcol[:, gain0 + c:gain0 + c + 1])

            def turn_out(layer, k, dst, gain=None, rows=P):
                act.wait_ge(turned, layer * N_BLOCK + (k + 1))
                scale = 1.0 if gain is None else gain
                nc.scalar.activation(dst, psum[5 + k % 2][0:rows, 0:SEQ], ACT.Copy,
                                     scale=scale).then_inc(block_ready, 1)

            def job_wait(layer, j):
                act.wait_ge(job_ready, layer * N_JOB + (j + 1))

            def gate_out(layer, j, tile_no):
                job_wait(layer, j)
                for i in range(2):
                    c = 2 * tile_no + i
                    ins = nc.scalar.activation(gate_chunks(c, 1).rearrange("p a t -> p (a t)"),
                                               psum[j % 2][:, i * SEQ:(i + 1) * SEQ],
                                               ACT.Identity, bias=gcol[:, GC_GB + c:GC_GB + c + 1])
                ins.then_inc(job_out, 1)

            def exp_rows(layer, u):
                mixer, _ = UNITS[u]
                act.wait_ge(max_ready, layer * N_UNIT + (u + 1))
                if mixer in "cd":
                    act.wait_ge(pt_ready, layer * N_PT + PT_BEFORE[u - 1])
                for t in range(TT):
                    if mixer == "a":
                        dst, src, scale = prob[:, u % 2, t, 0:257], prob[:, u % 2, t, 0:257], 1.0
                    elif mixer == "b":
                        dst, src, scale = prob[:, u % 2, t, 0:768], prob[:, u % 2, t, 0:768], 1.0
                    else:
                        scale = DH ** -0.5 if mixer == "d" else C_QK ** -0.5
                        dst = prob[:, u % 2, t, 0:SEQ]
                        src = psum[2 + u % 3][:, t * SEQ:(t + 1) * SEQ]
                    nc.scalar.activation(dst, src, ACT.Exp, bias=unit_m[:, u % 2, t:t + 1], scale=scale,
                                         accum_out=unit_d[:, u % 2, t:t + 1]).then_inc(exped, 1)
                if mixer in "cd":
                    act.wait_ge(exped, layer * (2 * N_UNIT) + (2 * u + 2))
                    act.sem_inc(score_read, 1)

            def turned_probs_out(layer, u):
                if u >= 2:
                    act.wait_ge(mixed, layer * N_UNIT + (u - 1))
                for i in range(PT_JOBS[u]):
                    k = PT_BEFORE[u] + i
                    act.wait_ge(pt_ready, layer * N_PT + (k + 1))
                    nc.scalar.activation(prob_t[:, u % 2, 2 * i:2 * i + 2, :],
                                         psum[5 + k % 2][:].rearrange("p (c q) -> p c q", c=2),
                                         ACT.Copy).then_inc(pt_out, 1)

            def mixed_pair_out(layer, u):
                if u % 2:
                    mixer, head = UNITS[u]
                    act.wait_ge(mixed, layer * N_UNIT + (u + 1))
                    nc.scalar.activation(y_t[:, 2 * BRANCH_OF[mixer] + head // 2, :], psum[7][:, 0:SEQ],
                                         ACT.Copy).then_inc(mixed_out, 1)

            with act.Fori(0, LAYERS) as layer:
                def layer_start():
                    act.wait_ge(h_ready, layer * 2 + 2)

                def w_hi_part(j):
                    act.wait_ge(loaded[j % RING], layer * (16 * U_LOADS) + 16 * (j // RING + 1))
                    nc.scalar.activation(w_hi[j % 3][:], tile[:, j % RING, 0:DC * PROJ_W],
                                         ACT.Copy).then_inc(w_hi_ready, 1)

                def gw_hi_part(n):
                    j = gate_tile(n)
                    act.wait_ge(loaded[j % RING], layer * (16 * U_LOADS) + 16 * (j // RING + 1))
                    nc.scalar.activation(gw_hi[n % 2][:], tile[:, j % RING, :], ACT.Copy).then_inc(gw_hi_ready, 1)

                rms_rows(layer, ST_H1, BL_H1, GC_N1, layer_start, lambda: w_hi_part(0))
                w_hi_part(1)
                w_hi_part(2)
                def qk_out(k):
                    i = k - BL_B
                    if i < 0:
                        gain, at = (GC_AK if k == BL_A + 2 else GC_AQ), QK_A + k - BL_A
                    else:
                        gain, at = (GC_BQ if i < 6 else GC_BK) + i % 6 // 2, QK_B + i
                    turn_out(layer, k, qk_t[:, at, :], gcol[:, gain:gain + 1])

                for j in range(N_PROJ):
                    for k in TURNS_AT_START.get(j, ()) + TURNS_IN_MIDDLE.get(j, ()):
                        qk_out(k)
                    job_wait(layer, j)
                    nc.scalar.activation(proj[:, :, j * PROJ_W:(j + 1) * PROJ_W],
                                         psum[j % 2][:, 0:2 * PROJ_W].rearrange("p (t c) -> p t c", t=TT),
                                         ACT.Copy).then_inc(job_out, 1)
                    if j + 3 < N_PROJ:
                        w_hi_part(j + 3)
                    elif j < N_PROJ - 1:
                        gw_hi_part(j + 3 - N_PROJ)
                    if j == 1:
                        act.wait_ge(job_out, layer * N_JOB_ACT + 2)
                        nc.scalar.activation(sq_a[:], proj[:, :, AQ:AV], ACT.Square).then_inc(squared, 1)
                    if j == 8:
                        act.wait_ge(job_out, layer * N_JOB_ACT + 9)
                        nc.scalar.activation(sq_b[:], proj[:, :, BQ:BV], ACT.Square).then_inc(squared, 1)
                    if j == 13:
                        act.wait_ge(job_out, layer * N_JOB_ACT + 14)
                        nc.scalar.activation(sq_l[:], proj[:, :, CQ:DQ], ACT.Square).then_inc(squared, 1)
                act.wait_ge(job_out, layer * N_JOB_ACT + N_PROJ)
                nc.scalar.activation(sq_d[:], proj[:, :, DQ:DV], ACT.Square).then_inc(squared, 1)

                for k in range(BL_BEHIND, BL_LAT):
                    qk_out(k)
                for i in range(3):
                    turn_out(layer, BL_LAT + i, lat_t[:, i, :], gcol[:, GC_CQL + i:GC_CQL + i + 1])

                def second_c_out():
                    for i in range(4):
                        j = J_C + i
                        job_wait(layer, j)
                        dst = c_out[:, i % 2, 0:384] if i < 2 else c_out[:, i % 2, 384:896]
                        nc.scalar.activation(dst, psum[j % 2][:, 0:384 if i < 2 else 512],
                                             ACT.Copy).then_inc(job_out, 1)
                    act.wait_ge(job_out, layer * N_JOB_ACT + (J_C + 4))
                    nc.scalar.activation(sq_c[:, :, 0:384], c_out[:, :, 0:384], ACT.Square).then_inc(squared, 1)
                    for t in range(TT):
                        ins = nc.scalar.activation(
                            sq_c[:, t, 384:640].rearrange("p (h c) -> p h c", h=4),
                            c_out[:, t, 384:896].rearrange("p (h c) -> p h c", h=4)[:, :, 0:C_NOPE], ACT.Square)
                    ins.then_inc(squared, 1)

                def mw_hi_part(k):
                    j = T_BRANCH + k
                    act.wait_ge(loaded[j % RING], layer * (16 * U_LOADS) + 16 * (j // RING + 1))
                    if 3 <= k < 8 or k == 11:
                        act.wait_ge(job_ready, layer * N_JOB + (LAST_JOB[j - 3] + 1))
                    nc.scalar.activation(mw_hi[k][:], tile[:, j % RING, :], ACT.Copy).then_inc(mw_hi_ready, 1)

                for u in range(N_UNIT + 1):
                    if u == STEP_TURN_D:
                        for i in range(3):
                            turn_out(layer, BL_D + i, qk_t[:, QK_D + i, :])
                    if u == STEP_TURN_C:
                        for i in range(8):
                            turn_out(layer, BL_C + i, qk_t[0:C_QK, QK_C + i, :], rows=C_QK)
                    if 1 <= u < N_UNIT - 1:
                        gw_hi_part(u + 1)
                    elif u:
                        mw_hi_part(u + 1 - N_UNIT)
                    if u:
                        turned_probs_out(layer, u - 1)
                    if u < N_UNIT:
                        exp_rows(layer, u)
                        gate_out(layer, J_GATE_A + u if u < 2 else J_GATE_B + u - 2, u)
                    if u == STEP_C:
                        second_c_out()
                    if u:
                        mixed_pair_out(layer, u - 1)

                act.wait_ge(job_out, layer * N_JOB_ACT + J_MERGE)
                for i in range(N_GATE):
                    pair = gate_chunks(2 * i, 2)
                    nc.scalar.activation(pair, pair, ACT.Sigmoid).then_inc(gate_ready, 1)
                    if i == 1:
                        mw_hi_part(2)
                    if i in (7, 11, 15):
                        mw_hi_part(i // 4 + 2)
                mw_hi_part(6)
                act.wait_ge(merged_ready, layer * 4 + 4)
                mw_hi_part(7)
                mw_hi_part(8)
                mw_hi_part(9)

                def h2_there():
                    act.wait_ge(h2_ready, layer + 1)

                rms_rows(layer, ST_H2, BL_H2, GC_N2, h2_there)
                mw_hi_part(10)
                for i in range(4):
                    j = J_WQ + i
                    job_wait(layer, j)
                    nc.scalar.activation(q_t[:, 2 * i:2 * i + 2, :],
                                         psum[j % 2][:].rearrange("p (h t) -> p h t", h=2),
                                         ACT.Copy).then_inc(job_out, 1)
                    if i == 0:
                        mw_hi_part(11)

                def hi_part(dst, src, ready):
                    nc.scalar.activation(dst, src.rearrange("p (c e) -> p c e", c=DC), ACT.Copy).then_inc(ready, 1)

                def hi_ahead(lap, s, dst):
                    half_there(act, layer, lap, s)
                    hi_part(dst, half_tile(tile, s), u_hi_ready)

                def hi_u(lap, s, dst):
                    act.wait_ge(loaded[s], layer * (16 * U_LOADS) + (lap - AHEAD // RING) * 16
                                + 16 * (N_PRE // RING + AHEAD // DEEP + 1))
                    hi_part(dst, tile[:, s, 0:1024], u_hi_ready)

                def hi_v(lap, s):
                    act.wait_ge(v_loaded[s], layer * (16 * V_LOADS) + lap * 16 + 16 * (AHEAD // DEEP + 1))
                    act.wait_ge(v_used, layer * N_EXP + lap * RING + (s - 1 + RING))
                    nc.scalar.activation(v_hi[:, s % 2], tile[:, s, 1024:2048], ACT.Copy).then_inc(v_hi_ready, 1)

                def product_done(first, s):
                    act.wait_ge(tile_used, layer * N_USED + first + (N_KEYS + RING + s + 1))

                def gelu(s, dst):
                    nc.scalar.activation(dst, psum[4 + s % RING][:, 0:SEQ], ACT.Gelu).then_inc(act_ready, 1)

                def next_v(lap, s):
                    hi_v(lap + (s + 1) // RING, (s + 1) % RING)

                for s in range(2):
                    hi_ahead(0, s, u_hi[:, s])
                act.wait_ge(peer_scored, layer + 1)
                for b in range(4):
                    nc.scalar.activation(score_sb[:, b], psum[4 + b][:], ACT.Copy).then_inc(score_out, 1)
                for s in range(2, RING):
                    hi_ahead(0, s, u_hi[:, s])

                def gelu_out(first, s):
                    act.wait_ge(act_gated, layer * (N_EXP - N_FREE) + first - N_FREE + (s + 1))
                    gelu(s, act_out[s % 2][:])

                def free_laps(first, last):
                    with act.Fori(first, last) as lap:
                        for s in range(DEEP):
                            product_done(lap * DEEP, s)
                            hi_ahead(lap + (s + RING) // DEEP, (s + RING) % DEEP, u_hi[:, s % RING])
                            gelu(s, gate_all[:, bass.ds(lap * DEEP + s, 1), :].rearrange("p a t -> p (a t)"))

                def choice_exp(t):
                    act.wait_ge(gate_shift, layer * TT + (t + 1))
                    nc.scalar.activation(expd[:], shifted[:], ACT.Exp).then_inc(gate_exp, 1)

                free_laps(0, EXP_LAP)
                choice_exp(0)
                last = N_FREE // DEEP - 1
                free_laps(EXP_LAP, last)
                choice_exp(1)

                def last_free(s):
                    product_done(last * DEEP, s)
                    if s < 2:
                        hi_ahead(last, s + RING, u_hi[:, s])
                    elif s >= RING:
                        hi_ahead(last + (s + 2) // DEEP, (s + 2) % DEEP, u_hi[:, s % 2])
                    gelu(s, gate_all[:, last * DEEP + s])

                for s in range(RING):
                    last_free(s)
                act.wait_ge(chosen_turned, layer + 1)
                for i, dst in enumerate((gate_t[:], i12_t[:, 0], i12_t[:, 1])):
                    ins = nc.scalar.activation(dst, psum[i][:, 0:SEQ], ACT.Copy)
                ins.then_inc(chosen_out, 1)

                def gate_hots(lap, k):
                    act.wait_ge(hot_ready, layer * N_GROUP + lap * (2 * DEEP) + (k + 1))
                    for i in range(GROUP):
                        t = lap * (2 * DEEP * GROUP) + (k * GROUP + i)
                        row = hots[:, k % 2, 0, i]
                        ins = nc.scalar.activation(row, row, ACT.Copy, scale=gate_t[:, bass.ds(t, 1)])
                    ins.then_inc(hot_gated, 1)

                def gates_rest(lap, k):
                    act.wait_ge(gates_mult, layer * N_GROUP + lap * (2 * DEEP) + (k + 1))
                    nc.scalar.activation(
                        gate_all[:, AHEAD:N_EXP, bass.ds(lap * (2 * DEEP * GROUP) + k * GROUP, GROUP)],
                        psum[k % 4][:].rearrange("p (t e) -> p e t", t=GROUP)[:, AHEAD:N_EXP],
                        ACT.Copy).then_inc(gates_out, 1)

                for s in range(RING, DEEP):
                    last_free(s)
                    if s == DEEP - 2:
                        for k in range(2):
                            gate_hots(0, k)

                def pair_step(lap, s, last=False):
                    for b in range(2):
                        if not (last and s == DEEP - 1):
                            gate_hots(lap + (s + 1) // DEEP, (2 * s + 2 + b) % (2 * DEEP))
                        gates_rest(lap, 2 * s + b)
                    tiles = lap + N_FREE // DEEP
                    product_done(tiles * DEEP, s)
                    if last and s >= DEEP - 2:
                        hi_u(AHEAD // RING, s + 2 - DEEP, u_hi[:, s % 2])
                    else:
                        hi_ahead(tiles + (s + 2) // DEEP, (s + 2) % DEEP, u_hi[:, s % 2])
                    gelu_out(tiles * DEEP, s)

                with act.Fori(0, N_PAIR // DEEP - 1) as lap:
                    for s in range(DEEP):
                        pair_step(lap, s)
                for s in range(DEEP):
                    pair_step(N_PAIR // DEEP - 1, s, True)
                act.wait_ge(gates_filled, layer * N_GROUP + (N_GROUP + 2))
                hi_v(0, 0)

                def both_step(lap, s, last=False):
                    tiles = lap + AHEAD // RING
                    product_done(tiles * RING, s)
                    if not (last and s >= 2):
                        hi_u(tiles + (s + 2) // RING, (s + 2) % RING, u_hi[:, s % 2])
                    gelu_out(tiles * RING, s)
                    next_v(lap, s)

                with act.Fori(0, N_BOTH // RING - 1) as lap:
                    for s in range(RING):
                        both_step(lap, s)
                for s in range(RING):
                    both_step(N_BOTH // RING - 1, s, True)
                with act.Fori(N_BOTH // RING, N_EXP // RING - 1) as lap:
                    for s in range(RING):
                        next_v(lap, s)
                for s in range(RING - 1):
                    next_v(N_EXP // RING - 1, s)

                act.wait_ge(experts_done, layer + 1)
                for b in range(2):
                    ins = nc.scalar.activation(h[:, 1, b * 512:(b + 1) * 512], psum[2 + b][:], ACT.Copy)
                ins.then_inc(h_ready, 1)

        @block.vector
        def _(vec):
            count = [0]

            def done(ins):
                count[0] += 1
                ins.then_inc(vec_order, 1)

            def settle(layer):
                vec.wait_ge(vec_order, layer * VEC_ORDER + count[0])

            def settle_apart(layer):
                settle(layer)
                vec.sem_inc(vec_passed, 1)

            vec.wait_ge(rel_product, 1)
            vec.wait_ge(rel_loaded, 48)
            nc.vector.tensor_tensor(rel_sb[:], psum[0][0:16, :], mask_sb[:], ALU.add).then_inc(rel_ready, 1)
            vec.wait_ge(consts_loaded, 48)
            vec.wait_ge(x_loaded, 16)
            vec.sem_inc(h_ready, 2)
            vec.sem_inc(act_gated, 2)

            def mean(at, n, width):
                return nc.vector.tensor_scalar(stat[:, at:at + n], stat[:, at:at + n], 1.0 / width, EPS,
                                               ALU.mult, ALU.add)

            def stats(at, heads):
                return stat[:, at:at + TT * heads].rearrange("p (t h) -> p t h", t=TT)

            def scales(at, heads, width):
                r = rstd[:, at:at + TT * heads].rearrange("p (t h) -> p t h", t=TT)
                return r.unsqueeze(3).broadcast_to([P, TT, heads, width])

            def rope(layer, src, dst, heads, axes, t, at=0):
                n = heads * len(axes) * 16
                parts = [rot[:, i, at:at + n].rearrange("p (h a c) -> p h a c", h=heads, a=len(axes))
                         for i in range(4)]
                tab = rope_t[:, t, axes[0]:axes[-1] + 1]
                cos, sin = (tab[:, :, i, :].unsqueeze(1).broadcast_to([P, heads, len(axes), 16])
                            for i in range(2))
                lo, hi = src[:, :, :, 0:16], src[:, :, :, 16:32]
                nc.vector.tensor_tensor(parts[0], lo, cos, ALU.mult)
                nc.vector.tensor_tensor(parts[1], hi, sin, ALU.mult)
                nc.vector.tensor_tensor(parts[2], lo, sin, ALU.mult)
                done(nc.vector.tensor_tensor(parts[3], hi, cos, ALU.mult))
                settle(layer)
                nc.vector.tensor_tensor(dst[:, :, :, 0:16], parts[0], parts[1], ALU.subtract)
                return nc.vector.tensor_tensor(dst[:, :, :, 16:32], parts[2], parts[3], ALU.add)

            def unit_scores(layer, u):
                mixer, head = UNITS[u]
                vec.wait_ge(scored, layer * N_UNIT + (u + 1))
                if mixer in "cd":
                    src = psum[2 + u % 3][:].rearrange("p (t k) -> p t k", t=TT)
                    done(nc.vector.tensor_reduce(unit_n[:, u % 2], src, AX_X, ALU.max))
                    settle(layer)
                    scale = DH ** -0.5 if mixer == "d" else C_QK ** -0.5
                    nc.vector.tensor_scalar(unit_m[:, u % 2], unit_n[:, u % 2], -scale, None,
                                            ALU.mult).then_inc(max_ready, 1)
                    return
                vec.wait_ge(bias_loaded[u % 2], layer * 64 + 16 * (u // 2 + 1))
                if u >= 2:
                    vec.wait_ge(pt_ready, layer * N_PT + PT_BEFORE[u - 1])
                groups = 1 if mixer == "a" else 3
                for g in range(groups):
                    bank = 2 + u % 3 if mixer == "a" else 2 + g
                    for t in range(TT):
                        ins = nc.vector.scalar_tensor_tensor(
                            out=prob[:, u % 2, t, g * SEQ:(g + 1) * SEQ], in0=psum[bank][:, t * SEQ:(t + 1) * SEQ],
                            scalar=DH ** -0.5, in1=bias_t[:, u % 2, g, P - P * t:P - P * t + SEQ],
                            op0=ALU.mult, op1=ALU.add)
                width = groups * SEQ
                ins.then_inc(score_read, 1)
                if mixer == "a":
                    done(nc.vector.tensor_copy(
                        prob[:, u % 2, :, SEQ:SEQ + 1],
                        grow[:, GR_SINK + head:GR_SINK + head + 1].unsqueeze(1).broadcast_to([P, TT, 1])))
                    width += 1
                    settle(layer)
                vec.wait_ge(score_read, layer * N_UNIT + (u + 1))
                nc.vector.tensor_reduce(unit_m[:, u % 2], prob[:, u % 2, :, 0:width], AX_X, ALU.max,
                                        negate=True).then_inc(max_ready, 1)

            def unit_norm(layer, u):
                width = 768 if UNITS[u][0] == "b" else SEQ
                vec.wait_ge(exped, layer * (2 * N_UNIT) + (2 * u + 2))
                done(nc.vector.reciprocal(unit_r[:, u % 2], unit_d[:, u % 2]))
                settle(layer)
                for t in range(TT):
                    ins = nc.vector.tensor_scalar(prob[:, u % 2, t, 0:width], prob[:, u % 2, t, 0:width],
                                                  unit_r[:, u % 2, t:t + 1], None, ALU.mult)
                ins.then_inc(prob_ready, 1)

            def top16(layer, n, src, work, values, places):
                for i in range(n):
                    ins = nc.vector.max(values[:, i, 0:8], src(i))
                done(ins)
                settle_apart(layer)
                for i in range(n):
                    nc.vector.max_index(places[:, i, 0:8], values[:, i, 0:8], src(i))
                for i in range(n):
                    ins = nc.vector.match_replace(work[:, i, :], values[:, i, 0:8], src(i), DEAD)
                done(ins)
                settle_apart(layer)
                for i in range(n):
                    ins = nc.vector.max(values[:, i, 8:16], work[:, i, :])
                done(ins)
                settle_apart(layer)
                for i in range(n):
                    ins = nc.vector.max_index(places[:, i, 8:16], values[:, i, 8:16], work[:, i, :])
                return ins

            def spread(dst, first, second, op):
                at = 0
                for a, rows, width in CAND_ROWS:
                    o = dst[:, :, at:at + rows * width].rearrange("p h (a b) -> p h a b", a=rows)
                    shape = [P, HEADS, rows, width]
                    ins = nc.vector.tensor_tensor(o, first[:, :, a:a + rows].unsqueeze(3).broadcast_to(shape),
                                                  second[:, :, 0:width].unsqueeze(2).broadcast_to(shape), op)
                    at += rows * width
                return ins

            def choose(layer, n, t):
                def scores(i):
                    head, half = i // 2, i % 2
                    b = score_sb[:, 2 * half + head // 4] if t == 0 else psum[2 * half + head // 4]
                    at = head % 4 * KEYS
                    return b[:, at:at + KEYS]

                done(top16(layer, 2 * HEADS, scores, left, top_v, top_i))
                settle(layer)
                done(nc.vector.tensor_copy(top_f[:], top_i[:]))
                halves_v = top_v[:].rearrange("p (h c) k -> p h c k", c=2)
                halves_f = top_f[:].rearrange("p (h c) k -> p h c k", c=2)
                done(spread(cand, halves_v[:, :, 0], halves_v[:, :, 1], ALU.add))
                settle(layer)
                done(nc.vector.tensor_scalar(halves_f[:, :, 0], halves_f[:, :, 0], float(KEYS), None, ALU.mult))
                settle(layer)
                done(spread(cand_i, halves_f[:, :, 0], halves_f[:, :, 1], ALU.add))
                settle_apart(layer)
                done(top16(layer, HEADS, lambda i: cand[:, i, :], cand_left, best, best_p))
                settle(layer)
                nc.vector.tensor_tensor(shifted[:], best[:], best[:, :, 0:1].broadcast_to([P, HEADS, TOPK]),
                                        ALU.subtract).then_inc(gate_shift, 1)
                done(nc.vector.tensor_copy(best_f[:], best_p[:]))
                settle(layer)
                few = HEADS // 2
                for first in (0, few):
                    for i in range(few):
                        shape = [P, TOPK, N_CAND]
                        ins = nc.vector.tensor_tensor(match[:, i],
                                                      iota[:, 0:N_CAND].unsqueeze(1).broadcast_to(shape),
                                                      best_f[:, first + i].unsqueeze(2).broadcast_to(shape),
                                                      ALU.is_equal)
                    done(ins)
                    settle(layer)
                    of = cand_i[:, first:first + few].unsqueeze(2).broadcast_to([P, few, TOPK, N_CAND])
                    done(nc.vector.tensor_tensor(match[:], match[:], of, ALU.mult))
                    settle(layer)
                    done(nc.vector.tensor_reduce(idx_f[:, first:first + few], match[:], AX_X, ALU.add))
                    settle(layer)
                done(nc.vector.tensor_copy(idx_i[:], idx_f[:]))
                settle(layer)
                nc.vector.tensor_scalar(idx_1[:], idx_i[:], 7, None, ALU.arith_shift_right)
                done(nc.vector.tensor_scalar(idx_2[:], idx_i[:], KEYS - 1, None, ALU.bitwise_and))
                settle(layer)

                def flat(a):
                    return a[:].rearrange("p h k -> p (h k)")

                nc.vector.tensor_copy(sel[:, 1, t], flat(idx_1))
                nc.vector.tensor_copy(sel[:, 2, t], flat(idx_2))
                vec.wait_ge(gate_exp, layer * TT + (n + 1))
                done(nc.vector.tensor_reduce(esum[:], expd[:], AX_X, ALU.add))
                settle(layer)
                done(nc.vector.reciprocal(erec[:], esum[:]))
                settle(layer)
                nc.vector.tensor_tensor(sel[:, 0, t].rearrange("p (h k) -> p h k", h=HEADS), expd[:],
                                        erec[:].unsqueeze(2).broadcast_to([P, HEADS, TOPK]),
                                        ALU.mult).then_inc(chosen, 1)

            with vec.Fori(0, LAYERS) as layer:
                count[0] = 0

                def squares(k):
                    vec.wait_ge(squared, layer * N_SQ + k)

                def rsqrts(k):
                    vec.wait_ge(rstd_ready, layer * N_RMS + k)

                squares(2)
                mean(ST_H1, 2, DM).then_inc(mean_ready, 1)

                def scale_rows(at, k):
                    rsqrts(k)
                    for t in range(TT):
                        nc.vector.tensor_scalar(hn[:, t], h[:, t], rstd[:, at + t:at + t + 1], None,
                                                ALU.mult).then_inc(hn_ready, 1)

                def split_chunks(block0):
                    for c in range(DC):
                        vec.wait_ge(block_ready, layer * N_BLOCK + (block0 + c + 1))
                        done(nc.vector.tensor_copy(x_hi[:, c, :], x_t[:, c, :]))
                        settle(layer)
                        nc.vector.tensor_tensor(x_lo[:, c, :], x_t[:, c, :], x_hi[:, c, :],
                                                ALU.subtract).then_inc(chunk_split, 1)

                scale_rows(ST_H1, 1)
                split_chunks(BL_H1)

                squares(3)
                done(nc.vector.tensor_reduce(stats(ST_A, 6), sq_a[:].rearrange("p t (h c) -> p t h c", h=6),
                                             AX_X, ALU.add))
                settle(layer)
                mean(ST_A, 12, DH).then_inc(mean_ready, 1)
                rsqrts(2)
                v = proj[:, :, AQ:AV].rearrange("p t (h c) -> p t h c", h=6)
                nc.vector.tensor_tensor(v, v, scales(ST_A, 6, DH), ALU.mult).then_inc(normed, 1)

                squares(4)
                done(nc.vector.tensor_reduce(stats(ST_B, 24), sq_b[:].rearrange("p t (h c) -> p t h c", h=24),
                                             AX_X, ALU.add))
                settle(layer)
                mean(ST_B, 48, DH).then_inc(mean_ready, 1)
                vec.wait_ge(w_hi_ready, layer * N_PROJ + (LO_VEC + 1))
                nc.vector.tensor_tensor(stream_lo[:, LO_VEC % RING, 0:DC * PROJ_W],
                                        tile[:, LO_VEC % RING, 0:DC * PROJ_W],
                                        w_hi[LO_VEC % 3][:], ALU.subtract).then_inc(w_lo_vec, 1)
                rsqrts(3)
                v = proj[:, :, BQ:BV].rearrange("p t (h c) -> p t h c", h=24)
                nc.vector.tensor_tensor(v, v, scales(ST_B, 24, DH), ALU.mult).then_inc(normed, 1)

                squares(5)
                for i, (lo, hi) in enumerate(((0, 256), (256, 384), (384, 416))):
                    ins = nc.vector.tensor_reduce(stat[:, ST_LAT + 2 * i:ST_LAT + 2 * i + 2].unsqueeze(2),
                                                  sq_l[:, :, lo:hi], AX_X, ALU.add)
                done(ins)
                settle(layer)
                mean(ST_LAT, 2, 256)
                mean(ST_LAT + 2, 2, 128)
                mean(ST_LAT + 4, 2, C_ROPE).then_inc(mean_ready, 1)
                rsqrts(4)
                for i, (lo, hi) in enumerate(((CQ, CKV), (CKV, CKR), (CKR, DQ))):
                    r = rstd[:, ST_LAT + 2 * i:ST_LAT + 2 * i + 2].unsqueeze(2).broadcast_to([P, TT, hi - lo])
                    ins = nc.vector.tensor_tensor(proj[:, :, lo:hi], proj[:, :, lo:hi], r, ALU.mult)
                ins.then_inc(normed, 1)

                def mean_d():
                    squares(6)
                    done(nc.vector.tensor_reduce(stats(ST_D, 6), sq_d[:].rearrange("p t (h c) -> p t h c", h=6),
                                                 AX_X, ALU.add))
                    settle(layer)
                    mean(ST_D, 12, DH).then_inc(mean_ready, 1)

                def norm_d():
                    rsqrts(5)
                    v = proj[:, :, DQ:DV].rearrange("p t (h c) -> p t h c", h=6)
                    done(nc.vector.tensor_tensor(v, v, scales(ST_D, 6, DH), ALU.mult))
                    settle(layer)
                    vec.wait_ge(gains_loaded, layer * 32 + 32)
                    for lo, hi, g in ((0, 4, GR_DQ), (4, 6, GR_DK)):
                        shape = [P, TT, hi - lo, DH]
                        gain = grow[:, g:g + DH].unsqueeze(1).unsqueeze(1).broadcast_to(shape)
                        ins = nc.vector.tensor_tensor(v[:, :, lo:hi], v[:, :, lo:hi], gain, ALU.mult)
                    done(ins)

                def rope_d():
                    settle(layer)
                    for t in range(TT):
                        s = proj[:, t, DQ:DV].rearrange("p (h a c) -> p h a c", h=6, a=2)
                        done(rope(layer, s, s, 6, (1, 2), t))
                        settle(layer)
                    vec.sem_inc(normed, 1)

                def mean_c():
                    squares(8)
                    q4 = sq_c[:, :, 0:384].rearrange("p t (h c) -> p t h c", h=4)
                    nc.vector.tensor_reduce(stats(ST_C, 4), q4[:, :, :, 0:C_NOPE], AX_X, ALU.add)
                    nc.vector.tensor_reduce(stats(ST_C + 8, 4), q4[:, :, :, C_NOPE:C_QK], AX_X, ALU.add)
                    done(nc.vector.tensor_reduce(stats(ST_C + 16, 4), sq_c[:, :, 384:640]
                                                 .rearrange("p t (h c) -> p t h c", h=4), AX_X, ALU.add))
                    settle(layer)
                    mean(ST_C, 8, C_NOPE)
                    mean(ST_C + 8, 8, C_ROPE)
                    mean(ST_C + 16, 8, C_NOPE).then_inc(mean_ready, 1)

                def norm_c():
                    rsqrts(6)
                    qv = c_out[:, :, 0:384].rearrange("p t (h c) -> p t h c", h=4)
                    kv = c_out[:, :, 384:896].rearrange("p t (h c) -> p t h c", h=4)
                    qo, ko = cat[:, :, 0:4], cat[:, :, 4:8]
                    nc.vector.tensor_tensor(qo[:, :, :, 0:C_NOPE], qv[:, :, :, 0:C_NOPE], scales(ST_C, 4, C_NOPE),
                                            ALU.mult)
                    nc.vector.tensor_tensor(qo[:, :, :, C_NOPE:C_QK], qv[:, :, :, C_NOPE:C_QK],
                                            scales(ST_C + 8, 4, C_ROPE), ALU.mult)
                    done(nc.vector.tensor_tensor(ko[:, :, :, 0:C_NOPE], kv[:, :, :, 0:C_NOPE],
                                                 scales(ST_C + 16, 4, C_NOPE), ALU.mult))
                    settle(layer)
                    gq = grow[:, GR_CQ:GR_CQ + C_QK].unsqueeze(1).unsqueeze(1).broadcast_to([P, TT, 4, C_QK])
                    nc.vector.tensor_tensor(qo, qo, gq, ALU.mult)
                    gk = grow[:, GR_CK:GR_CK + C_NOPE].unsqueeze(1).unsqueeze(1).broadcast_to([P, TT, 4, C_NOPE])
                    nc.vector.tensor_tensor(ko[:, :, :, 0:C_NOPE], ko[:, :, :, 0:C_NOPE], gk, ALU.mult)
                    gp = grow[:, GR_CK + C_NOPE:GR_CK + C_QK].unsqueeze(1).broadcast_to([P, TT, C_ROPE])
                    done(nc.vector.tensor_tensor(proj[:, :, CKR:DQ], proj[:, :, CKR:DQ], gp, ALU.mult))

                def rope_c():
                    settle(layer)
                    for t in range(TT):
                        s = cat[:, t, 0:4, C_NOPE:C_QK].unsqueeze(2)
                        done(rope(layer, s, s, 4, (0,), t))
                        s = proj[:, t, CKR:DQ].unsqueeze(1).unsqueeze(1)
                        done(rope(layer, s, s, 1, (0,), t, 128))
                        settle(layer)
                    for t in range(TT):
                        ins = nc.vector.tensor_copy(cat[:, t, 4:8, C_NOPE:C_QK],
                                                    proj[:, t, CKR:DQ].unsqueeze(1).broadcast_to([P, 4, C_ROPE]))
                    ins.then_inc(normed, 1)

                def split_mixed(pairs, first):
                    vec.wait_ge(mixed_out, layer * (N_UNIT // 2) + pairs)
                    at = slice(first, first + 2)
                    done(nc.vector.tensor_copy(y_hi[:, at], y_t[:, at]))
                    settle(layer)
                    nc.vector.tensor_tensor(y_lo[:, at], y_t[:, at], y_hi[:, at], ALU.subtract).then_inc(y_split, 1)

                mean_d()
                for u in range(N_UNIT + 1):
                    if u:
                        unit_norm(layer, u - 1)
                    if u < N_UNIT:
                        unit_scores(layer, u)
                    if u == STEP_NORM_D:
                        norm_d()
                    if u == STEP_ROPE_D:
                        rope_d()
                    if u == STEP_MEAN_C:
                        mean_c()
                    if u == STEP_NORM_C:
                        norm_c()
                    if u == 10:
                        split_mixed(4, 2 * BRANCH_OF["a"])
                        split_mixed(4, 2 * BRANCH_OF["b"])
                    if u == 13:
                        split_mixed(6, 2 * BRANCH_OF["d"])
                    if u == STEP_ROPE_C:
                        rope_c()

                for j in range(16):
                    if j == 2:
                        split_mixed(8, 2 * BRANCH_OF["c"])
                    n, pair = j // 4, j % 4
                    vec.wait_ge(job_ready, layer * N_JOB + (J_MERGE + j + 1))
                    if j == 0:
                        vec.wait_ge(mixed, layer * N_UNIT + N_UNIT)
                    vec.wait_ge(gate_ready, layer * N_GATE + (j + 1))
                    dst = merged[:, 2 * pair:2 * pair + 2, :]
                    gate = gate_chunks(8 * n + 2 * pair, 2)
                    src = psum[(J_MERGE + j) % 2][:].rearrange("p (c t) -> p c t", c=2)
                    if n == 0:
                        nc.vector.tensor_tensor(dst, src, gate, ALU.mult).then_inc(job_sum, 1)
                        continue
                    part = prod[:, j % 2].rearrange("p (c t) -> p c t", c=2)
                    nc.vector.tensor_tensor(part, src, gate, ALU.mult).then_inc(job_sum, 1)
                    vec.wait_ge(job_sum, layer * N_JOB_VEC + (j + 1))
                    ins = nc.vector.tensor_tensor(dst, dst, part, ALU.add)
                    done(ins)
                    if n < 3:
                        if pair == 3:
                            settle(layer)
                        continue
                    settle(layer)
                    at = slice(2 * pair, 2 * pair + 2)
                    done(nc.vector.tensor_copy(m_hi[:, at], dst))
                    settle(layer)
                    nc.vector.tensor_tensor(m_lo[:, at], dst, m_hi[:, at], ALU.subtract).then_inc(merged_ready, 1)

                for j in range(4):
                    vec.wait_ge(job_ready, layer * N_JOB + (J_OUT + j + 1))
                    dst = h[:, :, j * 256:(j + 1) * 256]
                    nc.vector.tensor_tensor(dst, psum[(J_OUT + j) % 2][:].rearrange("p (t c) -> p t c", t=TT),
                                            dst, ALU.add).then_inc(job_sum, 1)
                vec.wait_ge(job_sum, layer * N_JOB_VEC + N_JOB_VEC)
                vec.sem_inc(h2_ready, 1)

                squares(10)
                mean(ST_H2, 2, DM).then_inc(mean_ready, 1)
                scale_rows(ST_H2, 7)
                split_chunks(BL_H2)

                vec.wait_ge(peer_scored, layer + 1)
                vec.sem_inc(vec_passed, 1)
                choose(layer, 0, 1)
                vec.wait_ge(score_out, layer * 4 + 4)
                vec.sem_inc(vec_passed, 1)
                choose(layer, 1, 0)
                assert count[0] == VEC_ORDER, count[0]

                vec.wait_ge(chosen_out, layer + 1)
                vec.sem_inc(vec_passed, 1)

                def match_rows(lap, k):
                    vec.wait_ge(gates_filled, layer * N_GROUP + lap * (2 * DEEP) + (k + 1))
                    shape = [P, 2, GROUP, P]
                    at = i12_t[:, :, bass.ds(lap * (2 * DEEP * GROUP) + k * GROUP, GROUP)]
                    nc.vector.tensor_tensor(hots[:, k % 2], iota[:].unsqueeze(1).unsqueeze(1).broadcast_to(shape),
                                            at.unsqueeze(3).broadcast_to(shape), ALU.is_equal)\
                        .then_inc(hot_ready, 1)

                def gate_ahead(lap, k):
                    vec.wait_ge(gates_filled, layer * N_GROUP + lap * (2 * DEEP) + (k + 3))
                    at = gate_all[:, 0:AHEAD, bass.ds(lap * (2 * DEEP * GROUP) + k * GROUP, GROUP)]
                    src = psum[k % 4][:].rearrange("p (t e) -> p e t", t=GROUP)[:, 0:AHEAD]
                    return nc.vector.tensor_tensor(at, src, at, ALU.mult).then_inc(gates_mult, 1)

                def gate_act(first, s):
                    vec.wait_ge(act_ready, layer * N_EXP + first + (s + 1 + RING))
                    at = gate_all[:, bass.ds(first + s, 1), :]
                    nc.vector.tensor_tensor(at, act_out[s % 2][:].unsqueeze(1), at, ALU.mult).then_inc(act_gated, 1)

                def pair_step(lap, s, more=True, first=False):
                    if not first:
                        vec.wait_ge(gates_mult, layer * N_GROUP + lap * (2 * DEEP) + 2 * s)
                        gate_act(lap * DEEP + N_FREE, s - 2)
                    for b in range(2):
                        if more:
                            match_rows(lap + (s + 1) // DEEP, (2 * s + 2 + b) % (2 * DEEP))
                        if b == 0:
                            vec.wait_ge(act_gated, layer * (N_EXP - N_FREE) + lap * DEEP + (s + 1))
                        gate_ahead(lap, 2 * s + b)

                vec.wait_ge(ones_ready, layer * ONES_PARTS + ONES_PARTS)
                for k in range(2):
                    match_rows(0, k)
                vec.wait_ge(act_ready, layer * N_EXP + (N_FREE + RING))
                for s in range(DEEP):
                    pair_step(0, s, first=s < 2)
                with vec.Fori(1, N_PAIR // DEEP - 1) as lap:
                    for s in range(DEEP):
                        pair_step(lap, s)
                for s in range(DEEP):
                    pair_step(N_PAIR // DEEP - 1, s, s < DEEP - 1)
                vec.wait_ge(gates_mult, layer * N_GROUP + N_GROUP)
                gate_act(AHEAD, -2)
                gate_act(AHEAD, -1)

                def split_gated(lap, s):
                    vec.wait_ge(v_used, layer * N_EXP + lap * RING + (s - 1 + RING))
                    at = gate_all[:, bass.ds(lap * RING + s, 1), :] if not isinstance(lap, int) \
                        else gate_all[:, lap * RING + s:lap * RING + s + 1, :]
                    nc.vector.tensor_copy(g_hi[:, s % 2].unsqueeze(1), at).then_inc(gated_ready, 1)
                    vec.wait_ge(gated_ready, layer * (2 * N_EXP) + lap * (2 * RING) + (2 * s + 1))
                    nc.vector.tensor_tensor(g_lo[:, s % 2].unsqueeze(1), at, g_hi[:, s % 2].unsqueeze(1),
                                            ALU.subtract).then_inc(gated_ready, 1)

                def next_v(lap, s):
                    lap, s = lap + (s + 1) // RING, (s + 1) % RING
                    split_gated(lap, s)
                    lo_v(lap, s)

                def lo_v(lap, s):
                    vec.wait_ge(v_hi_ready, layer * N_EXP + lap * RING + (s + 1))
                    nc.vector.tensor_tensor(stream_lo[:, s, 1024:2048], tile[:, s, 1024:2048], v_hi[:, s % 2],
                                            ALU.subtract).then_inc(v_lo_ready, 1)

                vec.wait_ge(act_gated, layer * (N_EXP - N_FREE) + (N_PAIR + 2))
                vec.wait_ge(residual_in, layer + 1)
                split_gated(0, 0)
                lo_v(0, 0)
                with vec.Fori(0, N_BOTH // RING) as lap:
                    for s in range(RING):
                        gate_act(lap * RING + AHEAD, s)
                        next_v(lap, s)
                vec.wait_ge(act_gated, (layer + 1) * (N_EXP - N_FREE) + 2)
                vec.sem_inc(vec_passed, 1)
                with vec.Fori(N_BOTH // RING, N_EXP // RING - 1) as lap:
                    for s in range(RING):
                        next_v(lap, s)
                for s in range(RING - 1):
                    next_v(N_EXP // RING - 1, s)

                vec.wait_ge(experts_done, layer + 1)
                for b in range(2):
                    ins = nc.vector.tensor_copy(h[:, 0, b * 512:(b + 1) * 512], psum[b][:])
                ins.then_inc(h_ready, 1)

        @block.tensor
        def _(pe):
            pe.sem_inc(tile_used, RING)
            pe.sem_inc(v_used, RING)
            pe.sem_inc(gates_filled, 2)
            pe.wait_ge(rel_loaded, 48)
            nc.tensor.matmul(psum[0][0:16, :], relb_sb[0:32, :], one_hot_b[0:32, :], start=True,
                             stop=True).then_inc(rel_product, 1)
            pe.wait_ge(consts_loaded, 48)

            def turn(layer, k, srcs, rows=P):
                if k not in (BL_H1, BL_H1 + 1):
                    pe.wait_ge(block_ready, layer * N_BLOCK + (k - 1))
                for t, src in enumerate(srcs):
                    ins = nc.tensor.transpose(psum[5 + k % 2][0:rows, t * P:(t + 1) * P], src, ident[:])
                ins.then_inc(turned, 1)

            def tile_there(layer, j):
                pe.wait_ge(loaded[j % RING], layer * (16 * U_LOADS) + 16 * (j // RING + 1))

            def bank_free(layer, j):
                if j < 2:
                    return
                k = j - 2
                if k < J_MERGE:
                    pe.wait_ge(job_out, layer * N_JOB_ACT + (k + 1))
                elif k < J_WQ:
                    pe.wait_ge(job_sum, layer * N_JOB_VEC + (k - J_MERGE + 1))
                else:
                    pe.wait_ge(job_out, layer * N_JOB_ACT + (J_MERGE + k - J_WQ + 1))

            def split_product(dst, hi_hi, hi_lo, lo_hi, start, stop):
                nc.tensor.matmul(dst, *hi_hi, start=start, stop=False, skip_group_check=True)
                nc.tensor.matmul(dst, *hi_lo, start=False, stop=False, skip_group_check=True)
                return nc.tensor.matmul(dst, *lo_hi, start=False, stop=stop, skip_group_check=True)

            def chunk_there(layer, c):
                pe.wait_ge(chunk_split, layer * (2 * DC) + (c + 1))

            def qk_turn(layer, k):
                if k in (BL_A, BL_B):
                    pe.wait_ge(normed, layer * N_NORMED + (1 if k == BL_A else 2))
                at = AQ + (k - BL_A) * P if k < BL_B else BQ + (k - BL_B) * P
                turn(layer, k, [proj[:, t, at:at + P] for t in range(TT)])

            def split_rows_job(layer, j):
                if j == LO_VEC:
                    pe.wait_ge(w_lo_vec, layer + 1)
                else:
                    pe.wait_ge(w_lo_ready, layer * (N_PROJ - 1) + (j + 1 if j < LO_VEC else j))
                bank_free(layer, j)
                for k in TURNS_AT_START.get(j, ()):
                    qk_turn(layer, k)
                for t in range(TT):
                    if t:
                        for k in TURNS_IN_MIDDLE.get(j, ()):
                            qk_turn(layer, k)
                    rows = slice(t * P, (t + 1) * P)
                    for c in range(DC):
                        if j == t == 0:
                            chunk_there(layer, c)
                        cols = slice(c * PROJ_W, (c + 1) * PROJ_W)
                        wh, wl = w_hi[j % 3][:, cols], stream_lo[:, j % RING, cols]
                        ins = split_product(psum[j % 2][:, t * PROJ_W:(t + 1) * PROJ_W],
                                            (x_hi[:, c, rows], wh), (x_hi[:, c, rows], wl),
                                            (x_lo[:, c, rows], wh), c == 0, c == DC - 1)
                return ins

            def split_cols_job(layer, j, wh, wl, xh, xl, chunks):
                bank_free(layer, j)
                for i in range(2):
                    for c in range(chunks):
                        if j == J_WQ and i == 0:
                            chunk_there(layer, DC + c)
                        ins = split_product(psum[j % 2][:, i * SEQ:(i + 1) * SEQ], (wh(c, i), xh(c)),
                                            (wh(c, i), xl(c)), (wl(c, i), xh(c)), c == 0, c == chunks - 1)
                ins.then_inc(job_ready, 1)

            def x_job(layer, j, hi, stile):
                wh, wl = (a.rearrange("p (c i m) -> p c i m", c=DC, i=2)
                          for a in (hi[:], stream_lo[:, stile % RING, :]))
                split_cols_job(layer, j, lambda c, i: wh[:, c, i], lambda c, i: wl[:, c, i],
                               lambda c: x_hi[:, c], lambda c: x_lo[:, c], DC)

            def gate_job(layer, j, n):
                pe.wait_ge(gw_lo_ready, layer * N_GATE + (n + 1))
                x_job(layer, j, gw_hi[n % 2], gate_tile(n))

            def scores(layer, u):
                mixer, head = UNITS[u]
                if mixer == "a" and u >= 3:
                    pe.wait_ge(score_read, layer * N_UNIT + (u - 2))
                elif mixer == "b" or u in (8, 9, 10):
                    pe.wait_ge(score_read, layer * N_UNIT + min(u, 8))
                elif u > 10:
                    pe.wait_ge(score_read, layer * N_UNIT + (u - 2))
                for g in range(3 if mixer == "b" else 1):
                    if mixer in "ad":
                        first = QK_A if mixer == "a" else QK_D
                        q, k, rows = first + head % 2, first + 2, slice(64 * (head // 2), 64 * (head // 2) + 64)
                    elif mixer == "b":
                        q, k, rows = QK_B + 2 * g + head // 2, QK_B + 6 + 2 * g + head // 2, \
                            slice(64 * (head % 2), 64 * (head % 2) + 64)
                    else:
                        q, k, rows = QK_C + head, QK_C + 4 + head, slice(0, C_QK)
                    bank = 2 + g if mixer == "b" else 2 + u % 3
                    for t in range(TT):
                        ins = nc.tensor.matmul(psum[bank][:, t * SEQ:(t + 1) * SEQ],
                                               qk_t[rows, q, t * P:(t + 1) * P], qk_t[rows, k, :],
                                               start=True, stop=True)
                ins.then_inc(scored, 1)

            def values(u, chunk):
                mixer, head = UNITS[u]
                g, t = chunk // 2, chunk % 2
                if mixer == "a":
                    return proj[:, t, AV + head // 2 * DH:AV + (head // 2 + 1) * DH]
                if mixer == "b":
                    at = BV + (g * 4 + head) * DH
                    return proj[:, t, at:at + DH]
                if mixer == "d":
                    return proj[:, t, DV + head // 2 * DH:DV + (head // 2 + 1) * DH]
                at = 384 + head * 128 + C_NOPE
                return c_out[:, t, at:at + DH]

            def turn_probs(layer, u):
                pe.wait_ge(prob_ready, layer * N_UNIT + (u + 1))
                for i in range(PT_JOBS[u]):
                    k = PT_BEFORE[u] + i
                    if k >= 2:
                        pe.wait_ge(pt_out, layer * N_PT + (k - 1))
                    for c in range(2):
                        for t in range(TT):
                            at = (2 * i + c) * P
                            ins = nc.tensor.transpose(psum[5 + k % 2][:, c * SEQ + t * P:c * SEQ + (t + 1) * P],
                                                      prob[:, u % 2, t, at:at + P], ident[:])
                    ins.then_inc(pt_ready, 1)

            def mix_values(layer, u):
                if u % 2 == 0 and u:
                    pe.wait_ge(mixed_out, layer * (N_UNIT // 2) + u // 2)
                pe.wait_ge(pt_out, layer * N_PT + PT_BEFORE[u + 1])
                n = 2 * PT_JOBS[u]
                rows = slice(64 * (u % 2), 64 * (u % 2) + 64)
                for c in range(n):
                    ins = nc.tensor.matmul(psum[7][rows, 0:SEQ], values(u, c), prob_t[:, u % 2, c, :],
                                           start=(c == 0), stop=(c == n - 1))
                ins.then_inc(mixed, 1)

            def expert_up(layer, first, s, hi, lo):
                pe.wait_ge(u_lo_ready, layer * N_EXP + first + (s + 1))
                pe.wait_ge(act_ready, layer * N_EXP + first + (s + 1))
                lo = lo.rearrange("p (c e) -> p c e", c=DC)
                for c in range(DC):
                    ins = split_product(psum[4 + s % RING][:, 0:SEQ], (hi[:, c], x_hi[:, c]),
                                        (hi[:, c], x_lo[:, c]), (lo[:, c], x_hi[:, c]), c == 0, c == DC - 1)
                ins.then_inc(tile_used, 1)

            def expert_down(layer, lap, s, stop=False):
                pe.wait_ge(v_lo_ready, layer * N_EXP + lap * RING + (s + 1))
                pe.wait_ge(gated_ready, layer * (2 * N_EXP) + lap * (2 * RING) + (2 * s + 2))
                for t in range(TT):
                    a_hi, a_lo = (a[:, s % 2, t * P:(t + 1) * P] for a in (g_hi, g_lo))
                    for half in range(2):
                        v = slice(1024 + half * 512, 1024 + (half + 1) * 512)
                        vh, vl = v_hi[:, s % 2, half * 512:(half + 1) * 512], stream_lo[:, s, v]
                        ins = split_product(psum[2 * t + half][:], (a_hi, vh), (a_hi, vl), (a_lo, vh),
                                            False, stop)
                ins.then_inc(v_used, 1)

            with pe.Fori(0, LAYERS) as layer:
                pe.wait_ge(hn_ready, layer * 4 + 2)
                for c in range(DC):
                    turn(layer, BL_H1 + c, [hn[:, t, c * P:(c + 1) * P] for t in range(TT)])
                for j in range(N_PROJ):
                    ins = split_rows_job(layer, j)
                    ins.then_inc(job_ready, 1)

                def proj_blocks(first, cols, n, ready):
                    pe.wait_ge(normed, layer * N_NORMED + ready)
                    for i in range(n):
                        turn(layer, first + i,
                             [proj[:, t, cols + i * P:cols + (i + 1) * P] for t in range(TT)])

                for k in range(BL_BEHIND, BL_LAT):
                    qk_turn(layer, k)
                proj_blocks(BL_LAT, CQ, 3, 3)

                def second_c():
                    for i in range(4):
                        j, stile = J_C + i, T_CW + i // 2
                        t = i % 2
                        tile_there(layer, stile)
                        bank_free(layer, j)
                        if i < 2:
                            for c in range(2):
                                ins = nc.tensor.matmul(psum[j % 2][:, 0:384], lat_t[:, c, t * P:(t + 1) * P],
                                                       tile[:, stile % RING, c * 384:(c + 1) * 384],
                                                       start=(c == 0), stop=(c == 1))
                        else:
                            ins = nc.tensor.matmul(psum[j % 2][:], lat_t[:, 2, t * P:(t + 1) * P],
                                                   tile[:, stile % RING, 0:512], start=True, stop=True)
                        ins.then_inc(job_ready, 1)

                def parts_there(k):
                    pe.wait_ge(mw_lo_ready, layer * N_MW + (k + 1))

                def branch_job(n, pair):
                    if pair == 0:
                        parts_there(n)
                        pe.wait_ge(y_split, layer * 4 + (1, 2, 4, 4)[n])
                    wh, wl = (a.rearrange("p (c q m) -> p c q m", c=2, q=8)
                              for a in (mw_hi[n][:], stream_lo[:, (T_BRANCH + n) % RING, :]))
                    split_cols_job(layer, J_MERGE + 4 * n + pair, lambda c, i: wh[:, c, 2 * pair + i],
                                   lambda c, i: wl[:, c, 2 * pair + i], lambda c: y_hi[:, 2 * n + c, :],
                                   lambda c: y_lo[:, 2 * n + c, :], 2)

                pe.wait_ge(block_ready, layer * N_BLOCK + BL_D)
                for u in range(N_UNIT + 1):
                    if u == STEP_TURN_D:
                        proj_blocks(BL_D, DQ, 3, 4)
                        pe.wait_ge(block_ready, layer * N_BLOCK + BL_C)
                    if u == STEP_TURN_C:
                        pe.wait_ge(normed, layer * N_NORMED + 5)
                        for i in range(8):
                            turn(layer, BL_C + i, [cat[:, t, i, :] for t in range(TT)], rows=C_QK)
                        pe.wait_ge(block_ready, layer * N_BLOCK + BL_H2)
                    if u < N_UNIT:
                        scores(layer, u)
                    if u:
                        turn_probs(layer, u - 1)
                    if u < N_UNIT:
                        gate_job(layer, J_GATE_A + u if u < 2 else J_GATE_B + u - 2, u)
                    if u == STEP_C:
                        second_c()
                    if u == N_UNIT:
                        for pair in range(2):
                            branch_job(0, pair)
                    if u:
                        mix_values(layer, u - 1)

                for n in range(4):
                    for pair in range(2 if n == 0 else 0, 4):
                        branch_job(n, pair)
                for i in range(4):
                    j = J_OUT + i
                    parts_there(4 + i)
                    bank_free(layer, j)
                    for t in range(TT):
                        rows = slice(t * P, (t + 1) * P)
                        for c in range(DC):
                            if i == t == 0 and c % 2 == 0:
                                pe.wait_ge(merged_ready, layer * 4 + (c // 2 + 1))
                            cols = slice(c * 256, (c + 1) * 256)
                            wh, wl = mw_hi[4 + i][:, cols], stream_lo[:, (T_OUT + i) % RING, cols]
                            ins = split_product(psum[j % 2][:, t * 256:(t + 1) * 256], (m_hi[:, c, rows], wh),
                                                (m_hi[:, c, rows], wl), (m_lo[:, c, rows], wh),
                                                c == 0, c == DC - 1)
                    ins.then_inc(job_ready, 1)

                pe.wait_ge(hn_ready, layer * 4 + 4)
                for c in range(DC):
                    turn(layer, BL_H2 + c, [hn[:, t, c * P:(c + 1) * P] for t in range(TT)])
                for n in range(4):
                    parts_there(8 + n)
                    x_job(layer, J_WQ + n, mw_hi[8 + n], T_WQ + n)
                for n in range(2):
                    pe.wait_ge(job_out, layer * N_JOB_ACT + (N_JOB_ACT - 1 + n))
                    stile = T_KEYS + n
                    tile_there(layer, stile)
                    w = tile[:, stile % RING, 0:512].rearrange("p (h k) -> p h k", h=4)
                    for t in range(TT):
                        for i in range(4):
                            head = 4 * n + i
                            for half in range(2):
                                rows = slice(64 * half, 64 * half + 64)
                                bank = (4, 0)[t] + 2 * half + head // 4
                                ins = nc.tensor.matmul(psum[bank][:, i * KEYS:(i + 1) * KEYS],
                                                       q_t[rows, head, t * P:(t + 1) * P], w[rows, i, :],
                                                       start=True, stop=True)
                    ins.then_inc(tile_used, 1)
                pe.wait_ge(tile_used, layer * N_USED + (N_KEYS + RING))
                pe.sem_inc(peer_scored, 1)

                with pe.Fori(0, N_FREE // DEEP - 1) as lap:
                    for s in range(DEEP):
                        if s < RING:
                            pe.wait_ge(score_out, layer * 4 + (s + 1))
                        expert_up(layer, lap * DEEP, s, u_hi[:, s % RING], half_tile(stream_lo, s))

                for s in range(RING):
                    expert_up(layer, N_FREE - DEEP, s, u_hi[:, s], half_tile(stream_lo, s))

                pe.wait_ge(chosen, layer * TT + TT)
                for i in range(3):
                    for t in range(TT):
                        ins = nc.tensor.transpose(psum[i][:, t * P:(t + 1) * P], sel[:, i, t], ident[:])
                ins.then_inc(chosen_turned, 1)
                for s in range(RING, DEEP):
                    expert_up(layer, N_FREE - DEEP, s, u_hi[:, s % 2], half_tile(stream_lo, s))

                pe.wait_ge(chosen_out, layer + 1)
                pe.sem_inc(pe_passed, 1)
                with pe.Fori(0, N_PAIR // DEEP) as lap:
                    for s in range(DEEP):
                        for b in range(2):
                            k = 2 * s + b
                            pe.wait_ge(hot_gated, layer * N_GROUP + lap * (2 * DEEP) + (k + 1))
                            pe.wait_ge(gates_out, layer * N_GROUP + lap * (2 * DEEP) + (k + 1))
                            for i in range(GROUP):
                                ins = nc.tensor.matmul(psum[k % 4][:, i * P:(i + 1) * P], hots[:, b, 1, i],
                                                       hots[:, b, 0, i], start=True, stop=True)
                            ins.then_inc(gates_filled, 1)
                        expert_up(layer, lap * DEEP + N_FREE, s, u_hi[:, s % 2], half_tile(stream_lo, s))

                pe.wait_ge(gates_out, (layer + 1) * N_GROUP + 4)
                for t in range(TT):
                    for half in range(2):
                        ins = nc.tensor.matmul(psum[2 * t + half][:], ident[:], h[:, t, half * 512:(half + 1) * 512],
                                               start=True, stop=False, skip_group_check=True)
                ins.then_inc(residual_in, 1)
                with pe.Fori(0, N_BOTH // RING) as lap:
                    for s in range(RING):
                        expert_up(layer, lap * RING + AHEAD, s, u_hi[:, s % 2], half_tile(stream_lo, s))
                        expert_down(layer, lap, s)
                with pe.Fori(N_BOTH // RING, N_EXP // RING - 1) as lap:
                    for s in range(RING):
                        expert_down(layer, lap, s)
                for s in range(RING):
                    expert_down(layer, N_EXP // RING - 1, s, s == RING - 1)
                pe.wait_ge(v_used, layer * N_EXP + (N_EXP + RING))
                pe.sem_inc(experts_done, 1)


def distance_buckets():
    rel = np.arange(-255, 257)
    n = np.abs(rel)
    nf = np.maximum(n, 1).astype(np.float32)
    large = 8 + (np.log(nf / np.float32(8)) / np.float32(math.log(1024 / 8)) * np.float32(8)).astype(np.int32)
    return np.where(rel > 0, 16, 0) + np.where(n < 8, n, np.minimum(large, 15)), rel


def shape_constants():
    bucket, rel = distance_buckets()
    onehot = np.zeros((33, 512), np.float32)
    onehot[bucket, np.arange(512)] = 1.0
    mask = np.zeros((16, 512), np.float32)
    mask[0:4, np.abs(rel) > 128] = NEG
    for g, dil in enumerate((1, 4, 16)):
        mask[4 + 4 * g:8 + 4 * g, (rel % dil != 0) | (np.abs(rel) > 64 * dil)] = NEG
    pos = np.arange(SEQ)
    freqs = (np.float32(10000.0) ** (-np.arange(16, dtype=np.float32) / np.float32(16))).astype(np.float32)
    rope = np.zeros((P, TT, 3, 2, 16), np.float32)
    for i, at in enumerate((pos, pos // 64, pos % 64)):
        ang = at.astype(np.float32)[:, None] * freqs[None, :]
        rope[:, :, i, 0] = np.cos(ang).reshape(TT, P, 16).transpose(1, 0, 2)
        rope[:, :, i, 1] = np.sin(ang).reshape(TT, P, 16).transpose(1, 0, 2)
    iota = np.broadcast_to(np.arange(P, dtype=np.float32), (P, P))
    return {"ident": np.eye(P, dtype=np.float32), "iota": np.ascontiguousarray(iota), "rope": rope,
            "onehot": onehot, "mask": mask}


def tiles_of(w, n):
    layers, rows, cols = w.shape
    t = w.reshape(layers, rows // P, P, n, cols // n).transpose(0, 3, 2, 1, 4)
    return np.ascontiguousarray(t).reshape(layers, n, P, -1)


def laid_out(i):
    w_in = i["w_in"]
    order = [h * DH + c for h in HEAD_ORDER for c in range(DH)]
    cols = np.arange(MIX)
    cols[AQ:AQ + 256] = AQ + np.array(order)
    cols[DQ:DQ + 256] = DQ + np.array(order)
    per = lambda a: a.reshape(LAYERS, -1, P).transpose(0, 2, 1)
    twice = lambda a: np.concatenate([a, a], axis=1)[:, :, None]
    gcols = np.concatenate(
        [per(i["norm1_gain"]), per(i["norm2_gain"]), per(i["gate_bias"]), twice(i["a_q_gain"]),
         twice(i["a_k_gain"])] + [twice(i["b_q_gain"][:, g]) for g in range(3)]
        + [twice(i["b_k_gain"][:, g]) for g in range(3)] + [per(i["c_q_lat_gain"]), per(i["c_kv_lat_gain"])],
        axis=2)
    grows = np.concatenate([i["c_q_gain"], i["c_k_gain"], i["d_q_gain"], i["d_k_gain"], i["a_sink"]], axis=1)
    relb = np.zeros((33, 16), np.float32)
    relb[0:32] = i["rel_bias"]
    keys = i["peer_sub_keys"].transpose(0, 2, 4, 1, 3).reshape(LAYERS, P, 2, 4 * KEYS).transpose(0, 2, 1, 3)
    w_u = i["peer_w_u"].reshape(LAYERS, N_EXP, P, DC, P).transpose(0, 1, 4, 3, 2)
    branch = i["w_branch"].reshape(LAYERS, 4, 2, P, DM).transpose(0, 1, 3, 2, 4)
    return {
        "x": i["x"].reshape(SEQ, DM), "relb": relb,
        "w_proj": tiles_of(w_in[:, :, cols], N_PROJ), "w_gate": tiles_of(w_in[:, :, MIX:], N_GATE),
        "w_cq": tiles_of(i["c_w_uq"], 1), "w_ckv": tiles_of(i["c_w_ukv"], 1),
        "w_branch": branch.reshape(LAYERS, 4, P, 2048), "w_out": tiles_of(i["w_out"], 4),
        "w_q": tiles_of(i["peer_w_q"], 4), "keys": keys,
        "w_u": w_u.reshape(LAYERS, N_EXP, P, 1024), "w_v": i["peer_w_v"].reshape(LAYERS, N_EXP, P, DM),
        "gcols": gcols, "grows": grows[:, None, :],
    } | shape_constants()


ORDER = ["x", "relb", "w_proj", "w_gate", "w_cq", "w_ckv", "w_branch", "w_out", "w_q", "keys", "w_u", "w_v",
         "gcols", "grows", "ident", "iota", "rope", "onehot", "mask"]


def kernel(**inputs):
    import concourse.bacc as bacc
    from concourse.bass_utils import run_bass_kernel_spmd

    placed = laid_out({k: np.asarray(v) for k, v in inputs.items()})
    arrays = {f"in_{n}": np.ascontiguousarray(placed[n]) for n in ORDER}
    nc = bacc.Bacc("TRN2", target_bir_lowering=False, num_devices=1)
    args = [nc.dram_tensor(f"in_{n}", arrays[f"in_{n}"].shape, F32, kind="ExternalInput").ap() for n in ORDER]
    out = nc.dram_tensor("out_0", (SEQ, DM), F32, kind="ExternalOutput").ap()
    trunk(nc, *args, out)
    r = run_bass_kernel_spmd(nc, [arrays], core_ids=[0])
    return r.results[0]["out_0"].reshape(1, SEQ, DM)
```
